# Optimizing a Trainium2 kernel written in Bass

```python
import math
import jax, jax.numpy as jnp
from jax import lax
import numpy as np

D_MODEL = 1024
BATCH = 1
SEQ = 1024
DEPTH = 1

N_ATT_HEADS = 8
ATT_HEAD_DIM = 128
ATT_WIDTH = N_ATT_HEADS * ATT_HEAD_DIM
KV_RANK = 256
IDX_HEADS = 8
IDX_DIM = 64
TOPK_MAX = 256
Q_BLOCK = 128
SSM_EXPAND = 2
D_INNER = SSM_EXPAND * D_MODEL
SSM_HEAD_DIM = 64
N_SSM_HEADS = D_INNER // SSM_HEAD_DIM
N_SSM_GROUPS = 4
HEADS_PER_GROUP = N_SSM_HEADS // N_SSM_GROUPS
D_STATE = 128
CONV_WIDTH = 4
CONV_DIM = D_INNER + 2 * N_SSM_GROUPS * D_STATE
CHUNK = 128
D_FF = 4 * D_MODEL
N_MOD = 6
EPS = 1e-6

IN_SPLITS = (ATT_WIDTH, KV_RANK, IDX_HEADS * IDX_DIM, IDX_DIM, IDX_HEADS,
             D_INNER, CONV_DIM, N_SSM_HEADS, D_MODEL, D_MODEL)
D_IN_PROJ = ATT_WIDTH + KV_RANK + IDX_HEADS * IDX_DIM + IDX_DIM + IDX_HEADS + D_INNER + CONV_DIM + N_SSM_HEADS + 2 * D_MODEL

kernel_name = "hybrid_dsa_ssd_adaln_block"

def _normalize(x):
    xf = x.astype(jnp.float32)
    return xf * lax.rsqrt(jnp.mean(xf * xf, axis=-1, keepdims=True) + EPS)

def rms_norm(x, g):
    return (_normalize(x) * g.astype(jnp.float32)).astype(x.dtype)

def _split_last(t, sizes):
    offs = np.cumsum(np.array(sizes))[:-1].tolist()
    return jnp.split(t, offs, axis=-1)

def dsa_attention(q, c_kv, q_idx, k_idx, w_idx, w_uk, w_uv):
    b, s = q.shape[0], q.shape[1]
    topk = min(TOPK_MAX, s // 4)
    n_blocks = s // Q_BLOCK
    scale = ATT_HEAD_DIM ** -0.5
    q_abs = jnp.einsum('bshd,rhd->bshr', q, w_uk)
    key_pos = jnp.arange(s)
    gather_rows = jax.vmap(lambda table, idx: table[idx])

    def one_block(start):
        qa = lax.dynamic_slice_in_dim(q_abs, start, Q_BLOCK, axis=1)
        qi = lax.dynamic_slice_in_dim(q_idx, start, Q_BLOCK, axis=1)
        wi = lax.dynamic_slice_in_dim(w_idx, start, Q_BLOCK, axis=1)
        q_pos = start + jnp.arange(Q_BLOCK)
        causal = key_pos[None, :] <= q_pos[:, None]
        logits = jnp.einsum('bqhd,bsd->bqhs', qi, k_idx)
        index_score = jnp.einsum('bqh,bqhs->bqs', wi.astype(jnp.float32),
                                 jax.nn.relu(logits).astype(jnp.float32))
        index_score = jnp.where(causal[None], index_score, -jnp.inf)
        _, sel = lax.top_k(index_score, topk)
        valid = sel <= q_pos[None, :, None]
        c_sel = gather_rows(c_kv, sel)
        scores = jnp.einsum('bqhr,bqkr->bqhk', qa, c_sel).astype(jnp.float32) * scale
        scores = jnp.where(valid[:, :, None, :], scores, -jnp.inf)
        p = jax.nn.softmax(scores, axis=-1).astype(c_sel.dtype)
        return jnp.einsum('bqhk,bqkr->bqhr', p, c_sel)

    o_lat = lax.map(one_block, jnp.arange(n_blocks) * Q_BLOCK)
    o_lat = jnp.moveaxis(o_lat, 0, 1).reshape(b, s, N_ATT_HEADS, KV_RANK)
    o = jnp.einsum('bshr,rhd->bshd', o_lat, w_uv)
    return o.reshape(b, s, ATT_WIDTH)

def causal_depthwise_conv(x, w, bias):
    y = lax.conv_general_dilated(x, w[:, None, :].astype(x.dtype), window_strides=(1,),
                                 padding=[(CONV_WIDTH - 1, 0)],
                                 dimension_numbers=('NWC', 'WIO', 'NWC'),
                                 feature_group_count=x.shape[-1])
    return y + bias

def ssd_chunked(xs, dt, a, bm, cm):
    b, s, g, hg, p = xs.shape
    n = bm.shape[-1]
    nc = s // CHUNK
    f32 = jnp.float32
    xs = xs.astype(f32).reshape(b, nc, CHUNK, g, hg, p)
    dt = dt.astype(f32).reshape(b, nc, CHUNK, g, hg)
    bm = bm.astype(f32).reshape(b, nc, CHUNK, g, n)
    cm = cm.astype(f32).reshape(b, nc, CHUNK, g, n)
    a_cum = jnp.cumsum(dt * a.astype(f32), axis=2)
    xdt = xs * dt[..., None]
    a_t = jnp.moveaxis(a_cum, 2, -1)
    seg = a_t[..., :, None] - a_t[..., None, :]
    tril = jnp.tril(jnp.ones((CHUNK, CHUNK), dtype=bool))
    decay = jnp.exp(jnp.where(tril, seg, -jnp.inf))
    cb = jnp.einsum('bclgn,bcsgn->bcgls', cm, bm)
    y_diag = jnp.einsum('bcgls,bcghls,bcsghp->bclghp', cb, decay, xdt)
    decay_to_end = jnp.exp(a_cum[:, :, -1:] - a_cum)
    chunk_states = jnp.einsum('bclgn,bclgh,bclghp->bcghpn', bm, decay_to_end, xdt)
    chunk_decay = jnp.exp(a_cum[:, :, -1])

    def carry_step(state, inp):
        st, dec = inp
        return state * dec[..., None, None] + st, state

    init = jnp.zeros((b, g, hg, p, n), f32)
    _, prev = lax.scan(carry_step, init,
                       (jnp.moveaxis(chunk_states, 1, 0), jnp.moveaxis(chunk_decay, 1, 0)))
    prev = jnp.moveaxis(prev, 0, 1)
    y_off = jnp.einsum('bclgn,bcghpn,bclgh->bclghp', cm, prev, jnp.exp(a_cum))
    return (y_diag + y_off).reshape(b, s, g, hg, p)

def hybrid_mixer(h, w_in, kv_norm_g, kidx_norm_g, w_uk, w_uv, conv_w, conv_b, dt_bias, a_log,
                 d_skip, ssm_norm_g, w_o_att, w_o_ssd, w_out):
    b, s, _ = h.shape
    proj = h @ w_in
    q, kv_lat, q_idx, k_idx, w_idx, z, xbc, dt_raw, g_att, g_ssd = _split_last(proj, IN_SPLITS)
    q = q.reshape(b, s, N_ATT_HEADS, ATT_HEAD_DIM)
    c_kv = rms_norm(kv_lat, kv_norm_g)
    q_idx = q_idx.reshape(b, s, IDX_HEADS, IDX_DIM)
    k_idx = rms_norm(k_idx, kidx_norm_g)
    w_idx = w_idx * (IDX_HEADS ** -0.5)
    att = dsa_attention(q, c_kv, q_idx, k_idx, w_idx, w_uk, w_uv)
    xbc = jax.nn.silu(causal_depthwise_conv(xbc, conv_w, conv_b))
    xs, bm, cm = _split_last(xbc, (D_INNER, N_SSM_GROUPS * D_STATE, N_SSM_GROUPS * D_STATE))
    xs = xs.reshape(b, s, N_SSM_GROUPS, HEADS_PER_GROUP, SSM_HEAD_DIM)
    bm = bm.reshape(b, s, N_SSM_GROUPS, D_STATE)
    cm = cm.reshape(b, s, N_SSM_GROUPS, D_STATE)
    dt = jax.nn.softplus((dt_raw + dt_bias).astype(jnp.float32)).reshape(b, s, N_SSM_GROUPS, HEADS_PER_GROUP)
    a = -jnp.exp(a_log.astype(jnp.float32)).reshape(N_SSM_GROUPS, HEADS_PER_GROUP)
    y = ssd_chunked(xs, dt, a, bm, cm).astype(h.dtype)
    y = y + xs * d_skip.reshape(N_SSM_GROUPS, HEADS_PER_GROUP, 1)
    y = y.reshape(b, s, D_INNER) * jax.nn.silu(z)
    y = _normalize(y.reshape(b, s, N_SSM_GROUPS, D_INNER // N_SSM_GROUPS)).reshape(b, s, D_INNER)
    y = (y * ssm_norm_g.astype(jnp.float32)).astype(h.dtype)
    branch_att = att @ w_o_att
    branch_ssd = y @ w_o_ssd
    merged = jax.nn.sigmoid(g_att) * branch_att + jax.nn.sigmoid(g_ssd) * branch_ssd
    return merged @ w_out

def squared_relu_mlp(h, w_up, w_down):
    return jnp.square(jax.nn.relu(h @ w_up)) @ w_down

def setup_inputs(seed: int = 0) -> dict:
    key = jax.random.key(seed)
    ks = jax.random.split(key, 24)
    L = DEPTH

    def nrm(k, shape, scale):
        return jax.random.normal(k, shape, jnp.float32) * scale

    dt_init = jnp.exp(jax.random.uniform(ks[12], (L, N_SSM_HEADS), jnp.float32,
                                         minval=math.log(1e-3), maxval=math.log(1e-1)))
    dt_bias = dt_init + jnp.log(-jnp.expm1(-dt_init))
    a_log = jnp.log(jax.random.uniform(ks[13], (L, N_SSM_HEADS), jnp.float32, minval=1.0, maxval=16.0))
    return {
        "x": nrm(ks[0], (BATCH, SEQ, D_MODEL), 1.0),
        "c": nrm(ks[1], (BATCH, D_MODEL), 1.0),
        "ada_w": nrm(ks[2], (L, D_MODEL, N_MOD * D_MODEL), D_MODEL ** -0.5),
        "ada_b": nrm(ks[3], (L, N_MOD * D_MODEL), 0.02),
        "norm_g": 1.0 + nrm(ks[4], (L, 4, D_MODEL), 0.05),
        "w_in": nrm(ks[5], (L, D_MODEL, D_IN_PROJ), D_MODEL ** -0.5),
        "kv_norm_g": 1.0 + nrm(ks[6], (L, KV_RANK), 0.05),
        "kidx_norm_g": 1.0 + nrm(ks[7], (L, IDX_DIM), 0.05),
        "w_uk": nrm(ks[8], (L, KV_RANK, N_ATT_HEADS, ATT_HEAD_DIM), KV_RANK ** -0.5),
        "w_uv": nrm(ks[9], (L, KV_RANK, N_ATT_HEADS, ATT_HEAD_DIM), KV_RANK ** -0.5),
        "conv_w": nrm(ks[10], (L, CONV_WIDTH, CONV_DIM), CONV_WIDTH ** -0.5),
        "conv_b": nrm(ks[11], (L, CONV_DIM), 0.02),
        "dt_bias": dt_bias,
        "a_log": a_log,
        "d_skip": 1.0 + nrm(ks[14], (L, N_SSM_HEADS), 0.1),
        "ssm_norm_g": 1.0 + nrm(ks[15], (L, D_INNER), 0.05),
        "w_o_att": nrm(ks[16], (L, ATT_WIDTH, D_MODEL), ATT_WIDTH ** -0.5),
        "w_o_ssd": nrm(ks[17], (L, D_INNER, D_MODEL), D_INNER ** -0.5),
        "w_out": nrm(ks[18], (L, D_MODEL, D_MODEL), D_MODEL ** -0.5),
        "w_up": nrm(ks[19], (L, D_MODEL, D_FF), D_MODEL ** -0.5),
        "w_down": nrm(ks[20], (L, D_FF, D_MODEL), D_FF ** -0.5),
    }

def reference(x, c, ada_w, ada_b, norm_g, w_in, kv_norm_g, kidx_norm_g, w_uk, w_uv, conv_w, conv_b,
              dt_bias, a_log, d_skip, ssm_norm_g, w_o_att, w_o_ssd, w_out, w_up, w_down):
    c_act = jax.nn.silu(c)
    for layer in range(DEPTH):
        mod = (c_act @ ada_w[layer] + ada_b[layer])[:, None, :]
        sh_m, sc_m, gt_m, sh_f, sc_f, gt_f = jnp.split(mod, N_MOD, axis=-1)
        h = rms_norm(x, norm_g[layer, 0]) * (1 + sc_m) + sh_m
        y = hybrid_mixer(h, w_in[layer], kv_norm_g[layer], kidx_norm_g[layer], w_uk[layer], w_uv[layer],
                         conv_w[layer], conv_b[layer], dt_bias[layer], a_log[layer], d_skip[layer],
                         ssm_norm_g[layer], w_o_att[layer], w_o_ssd[layer], w_out[layer])
        x = x + gt_m * rms_norm(y, norm_g[layer, 1])
        h = rms_norm(x, norm_g[layer, 2]) * (1 + sc_f) + sh_f
        y = squared_relu_mlp(h, w_up[layer], w_down[layer])
        x = x + gt_f * rms_norm(y, norm_g[layer, 3])
    return x


_drawn_inputs = setup_inputs


def setup_inputs(seed=0):
    import zlib

    import numpy as np

    out = dict(_drawn_inputs(seed))
    spreads = {}
    factors = {'kv_norm_g': 4.764,
     'kidx_norm_g': 6.945,
     'conv_b': 23.885,
     'd_skip': 24.314,
     'ssm_norm_g': 7.73}
    for name, (base, spread) in spreads.items():
        noise = np.random.default_rng([zlib.crc32(name.encode()), seed]).standard_normal(out[name].shape)
        drawn = base * np.exp(spread * noise) if base else spread * noise
        out[name] = __import__('jax').numpy.asarray(drawn.astype(out[name].dtype))
    for name, factor in factors.items():
        out[name] = (out[name] * factor).astype(out[name].dtype)
    return out
```

```python
from contextlib import ExitStack

import concourse.bass as bass
from concourse import mybir

P = 128
F32 = mybir.dt.float32
F32R = mybir.dt.float32r
BF16 = mybir.dt.bfloat16
ALU = mybir.AluOpType
ACT = mybir.ActivationFunctionType
AX_X = mybir.AxisListType.X


class Count:

    def __init__(self, engine, sem):
        self.engine, self.sem, self.n, self.turn, self.per = engine, sem, 0, None, 0

    def add(self, ins):
        ins.then_inc(self.sem, 1)
        self.n += 1
        return ins

    def value(self):
        return self.n if self.turn is None else self.n + self.turn * self.per

    def wait(self):
        self.engine.wait_ge(self.sem, self.value())

    def link(self, ins):
        self.add(ins)
        self.wait()

    def step(self):
        self.engine.sem_inc(self.sem, 1)
        self.n += 1

    def enter(self, turn, per):
        self.turn, self.per, self.base = turn, per, self.n

    def leave(self, turns):
        assert self.n - self.base == self.per, (self.n - self.base, self.per)
        self.turn = None
        self.n = self.base + turns * self.per


def hybrid_block(nc, x, c, ada_w, ada_b, norm_g, w_in, kv_norm_g, kidx_norm_g, w_uk, w_uv, conv_w, conv_b,
                 dt_bias, a_log, d_skip, ssm_norm_g, w_o_att, w_o_ssd, w_out, w_up, w_down, out):
    SEQ, D = x.shape[1], x.shape[2]
    R = kv_norm_g.shape[1]
    DI = kidx_norm_g.shape[1]
    NH, HD = w_uk.shape[2], w_uk.shape[3]
    NS = dt_bias.shape[1]
    CD = conv_w.shape[2]
    DIN = ssm_norm_g.shape[1]
    DFF = w_up.shape[2]
    HI = 8
    NG = 4
    HG = NS // NG
    PD = DIN // NS
    DG = DIN // NG
    TAPS = conv_w.shape[1]
    TOPK = 256
    EPS = 1e-6
    SCALE = float(HD) ** -0.5
    KT = D // P
    NT = SEQ // P
    HALF = SEQ // 2
    WC = 256
    NEG = -1e30
    TAKEN = -3e38
    C_Q = 0
    C_KV = C_Q + NH * HD
    C_QI = C_KV + R
    C_KI = C_QI + HI * DI
    C_Z = C_KI + DI + HI
    C_X = C_Z + DIN
    C_B = C_X + DIN
    C_C = C_B + NG * P
    C_DT = C_X + CD
    C_GA = C_DT + NS
    C_GS = C_GA + D
    NSM = DI + HI + NS
    assert SEQ == D == 1024 and C_GS + D == w_in.shape[2] and HD == P and R == WC and 2 * DI == P
    assert DG == 4 * P and HG * PD == DG

    N_Q, N_UK, N_GS, N_SSM = 4, 8, 10, 14
    N_O = N_SSM + 6 * NG
    N_OUT = N_O + 12
    N_MLP = N_OUT + 4
    NC = DFF // WC
    N_ALL = N_MLP + 2 * NC

    at = [16512]

    def place(name, shape, dt, offset=None):
        size = 1
        for s in shape[1:]:
            size *= s
        size = (size * (2 if dt == BF16 else 4) + 31) // 32 * 32
        if offset is None:
            offset = at[0]
            at[0] += size
        assert offset + size <= 229344, (name, offset + size)
        return nc.alloc_sbuf_tensor_at(name, shape, dt, offset=offset)

    raw = [place(f"raw{s}", [P, KT * WC], F32) for s in range(2)]
    w_hi = [place(f"w_hi{s}", [P, KT * WC], F32R) for s in range(2)]
    w_lo = [place(f"w_lo{s}", [P, KT * WC], F32R) for s in range(2)]
    ACT_AT = at[0]
    a_hi = place("a_hi", [P, KT, SEQ], F32R)
    a_lo = place("a_lo", [P, KT, SEQ], F32R)
    R1 = at[0]
    x_tm = place("x_tm", [P, NT, D], F32)
    ident = place("ident", [P, P], F32)
    ident_bf = place("ident_bf", [P, P], BF16)
    ones = place("ones", [P, P], F32)
    tri = place("tri", [P, P], F32)
    future = place("future", [P, P], F32)
    past_bf = place("past_bf", [P, P], BF16)
    vec_a = place("vec_a", [P, 112], F32)
    vec_b = place("vec_b", [P, 112], F32)
    mod = place("mod", [P, 48], F32)
    gain = place("gain", [P, 2 * KT], F32)
    gate_cols = place("gate_cols", [P, 2 * KT], F32)
    c_act = place("c_act", [P, KT], F32)
    stat = place("stat", [P, 16 * KT], F32)
    kv_row = place("kv_row", [P, R], F32)
    ki_row = place("ki_row", [P, DI], F32)
    dtb_row = place("dtb_row", [P, NS], F32)
    alog_row = place("alog_row", [P, NS], F32)
    skip_row = place("skip_row", [P, NS], F32)
    w_idx = place("w_idx", [P, NT, HI], F32)
    att_stat = place("att_stat", [P, 16 * 4], F32)
    top8 = place("top8", [P, 8], F32)
    R2 = at[0]
    K = 1024
    rows_a = place("rows_a", [112, P], F32, R2)
    rows_b = place("rows_b", [112, P], F32, R2 + 512)
    h_tmp = [place(f"h_tmp{i}", [P, 512], F32, R2 + (16 + 2 * i) * K) for i in range(4)]
    sq0 = place("sq0", [P, D], F32, R2 + 44 * K)
    ada0 = place("ada0", [P, KT, 2 * D], F32, ACT_AT)
    q_idx = place("q_idx", [P, 4, SEQ], F32, R2)
    ckv_hi = place("ckv_hi", [P, 2, SEQ], F32R, R2 + 16 * K)
    ckv_lo = place("ckv_lo", [P, 2, SEQ], F32R, R2 + 24 * K)
    ckv_tm = place("ckv_tm", [P, NT, R], F32, R2 + 32 * K)
    kidx_tm = place("kidx_tm", [P, NT, P], F32, R2 + 40 * K)
    relu_buf = place("relu_buf", [P, 4, 512], F32, R2 + 40 * K)
    k_idx = place("k_idx", [P, SEQ], F32, R2 + 48 * K)
    score = place("score", [P, NT, SEQ], F32, R1)
    bias_bf = place("bias_bf", [P, NT, SEQ], BF16, R2)
    spill = [place(f"spill{i}", [P, SEQ], F32, R2 + (32 + 4 * i) * K) for i in range(4)]
    ada_raw = [place(f"ada_raw{i}", [P, KT, WC], F32, R2 + (16 + 8 * i) * K) for i in range(2)]
    DT0 = R2 + 51 * K
    dta = place("dta", [P, NT, NS], F32, DT0)
    acum = place("acum", [P, NT, NS], F32, DT0 + K)
    ea = place("ea", [P, NT, NS], F32, DT0 + 2 * K)
    dte = place("dte", [P, NT, NS], F32, DT0 + 3 * K)
    dec = place("dec", [P, NT, NS], F32, DT0 + 4 * K)
    dt = place("dt", [P, NT, NS], F32, DT0 + 5 * K)
    dta_g = place("dta_g", [P, NT, HG], F32, DT0 + 6 * K)
    hq = [place(f"hq{i}", [P, SEQ], F32, R2 + (16 + 12 * i) * K) for i in range(2)]
    hk = [place(f"hk{i}", [P, SEQ], F32, R2 + (20 + 12 * i) * K) for i in range(2)]
    hv = [place(f"hv{i}", [P, NT, P], F32, R2 + (24 + 12 * i) * K) for i in range(2)]
    prob = [place(f"prob{i}", [P, SEQ], F32, R2 + (40 + 4 * i) * K) for i in range(2)]
    att_o = [place(f"att_o{i}", [P, 512], F32, R2 + (48 + 2 * i) * K) for i in range(2)]
    probT = [place(f"probT{i}", [P, NT, 512], F32, R1 + 16 * i * K) for i in range(2)]
    xs_tm = place("xs_tm", [P, NT, DG], F32, R1)
    zy = place("zy", [P, NT, DG], F32, R1 + 16 * K)
    PADW = SEQ + 8
    c_in = [place(f"c_in{i}", [P, PADW], F32, R2 + 4128 * i) for i in range(2)]
    o = R2 + 2 * 4128
    c_out = [place(f"c_out{i}", [P, SEQ], F32, o + 4 * K * i) for i in range(2)]
    o += 8 * K
    b_fm = place("b_fm", [P, SEQ], F32, o)
    c_fm = place("c_fm", [P, SEQ], F32, o + 4 * K)
    b_tm = place("b_tm", [P, NT, P], F32, o + 8 * K)
    o += 12 * K
    decay = [place(f"decay{i}", [P, HG, P], F32, o + 4 * K * i) for i in range(2)]
    o += 8 * K
    xdt = [place(f"xdt{i}", [P, HG, PD], F32, o + 2 * K * i) for i in range(2)]
    xde = [place(f"xde{i}", [P, HG, PD], F32, o + 4 * K + 2 * K * i) for i in range(2)]
    o += 8 * K
    state = place("state", [P, HG, PD], F32, o)
    y_t = [place(f"y_t{i}", [P, HG, PD], F32, o + 2 * K + 2 * K * i) for i in range(2)]
    assert o + 6 * K + 512 <= DT0, (o + 6 * K, DT0)
    cb_sb = place("cb_sb", [P, P], F32, o + 6 * K)
    acc = place("acc", [P, KT, SEQ], F32, R1)
    act_raw = [place(f"act_raw{i}", [P, SEQ], F32, R2 + 4 * i * K) for i in range(2)]
    gates = [place(f"gates{i}", [P, 2, SEQ], F32, R2 + (8 + 8 * i) * K) for i in range(2)]
    gated = [place(f"gated{i}", [P, 512], F32, R2 + (24 + 2 * i) * K) for i in range(2)]
    row = [place(f"row{i}", [P, D], F32, R2 + (32 + 4 * i) * K) for i in range(2)]
    diag = [place(f"diag{i}", [P, P], F32, R2 + 40 * K + 512 * i) for i in range(2)]
    x_in = [place(f"x_in{i}", [P, D], F32, R2 + 4 * i * K) for i in range(4)]
    sq = place("sq", [P, D], F32, R2 + 50 * K)
    u_hi = [place(f"u_hi{i}", [P, 2, SEQ], F32R, R2 + 16 * i * K) for i in range(2)]
    u_lo = [place(f"u_lo{i}", [P, 2, SEQ], F32R, R2 + (8 + 16 * i) * K) for i in range(2)]
    u_tmp = [place(f"u_tmp{i}", [P, 512], F32, R2 + (40 + 2 * i) * K) for i in range(4)]

    q_d = nc.dram_tensor("q_d", (NH, P, SEQ), F32, kind="Internal").ap()
    k_d = nc.dram_tensor("k_d", (NH, P, SEQ), F32, kind="Internal").ap()
    v_d = nc.dram_tensor("v_d", (SEQ, NH * HD), F32, kind="Internal").ap()
    gate_d = nc.dram_tensor("gate_d", (2 * KT, P, SEQ), F32, kind="Internal").ap()
    acts_d = nc.dram_tensor("acts_d", (3 * KT, P, SEQ), F32, kind="Internal").ap()
    x1_d = nc.dram_tensor("x1_d", (SEQ, D), F32, kind="Internal").ap()

    ctx = ExitStack()
    with ctx:
        ps = ctx.enter_context(nc.psum_tensor("ps", [P, 8, 512], F32))

        def sem(name):
            return ctx.enter_context(nc.semaphore(name))

        raw_in = [sem(f"raw_in{s}") for s in range(2)]
        w_split = [sem(f"w_split{s}") for s in range(2)]
        w_used = [sem(f"w_used{s}") for s in range(2)]
        c_cols_in = sem("c_cols_in")
        hi_made = sem("hi_made")
        act_own, dve_own, pool_own = sem("act_own"), sem("dve_own"), sem("pool_own")
        met = sem("met")
        const_made = sem("const_made")
        small_in = sem("small_in")
        x_landed = [sem(f"x_landed{t}") for t in range(NT)]
        ada_in = sem("ada_in")
        vec_turned = sem("vec_turned")
        c_ready = sem("c_ready")
        mod0_done = sem("mod0_done")
        gain_ready = sem("gain_ready")
        squares = sem("squares")
        vars_ready = sem("vars_ready")
        roots = sem("roots")
        normed = sem("normed")
        turned = sem("turned")
        h_ready = sem("h_ready")
        h_split = sem("h_split")
        kv_sq, kv_var, kv_root, kv_turned, kv_out, kv_out_split = (
            sem(n) for n in ("kv_sq", "kv_var", "kv_root", "kv_turned", "kv_out", "kv_out_split"))
        qi_out = sem("qi_out")
        logit_done, relu_done, relu_used = sem("logit_done"), sem("relu_done"), sem("relu_used")

        unit_done, unit_out = sem("unit_done"), sem("unit_out")
        spilled = [sem(f"spilled{i}") for i in range(4)]
        ada2_in = [sem(f"ada2_in{i}") for i in range(2)]
        ada2_used, mod_ready = sem("ada2_used"), sem("mod_ready")
        head_in = [sem(f"head_in{i}") for i in range(2)]
        qk_done, masked, exp_done, p_ready = (sem(n) for n in ("qk_done", "masked", "exp_done", "p_ready"))
        pt_done, pt_out, pv_done, pv_out = (sem(n) for n in ("pt_done", "pt_out", "pv_done", "pv_out"))
        att_stored = [sem(f"att_stored{i}") for i in range(2)]
        dta_ready, acum_done, aend_out, dte_ready = (sem(n) for n in ("dta_ready", "acum_done", "aend_out", "dte_ready"))
        dt_abs, dt_exp, dt_plus, dt_ln = (sem(n) for n in ("dt_abs", "dt_exp", "dt_plus", "dt_ln"))
        conv_in, conv_done, silu_done, tile_turned, tile_out = (sem(n) for n in ("conv_in", "conv_done", "silu_done", "tile_turned", "tile_out"))
        z_done, z_out, ga_out = sem("z_done"), sem("z_out"), sem("ga_out")
        ga_stored = [sem(f"ga_stored{i}") for i in range(2)]
        dtag_ready, seg_done, seg_out, decay_done, cb_out = (sem(n) for n in ("dtag_ready", "seg_done", "seg_out", "decay_done", "cb_out"))
        mix_ready, mix_done, state_ready, y_ready = (sem(n) for n in ("mix_ready", "mix_done", "state_ready", "y_ready"))
        gn_squares, gn_var, gn_root, gn_ready, yt_done, yt_out = (
            sem(n) for n in ("gn_squares", "gn_var", "gn_root", "gn_ready", "yt_done", "yt_out"))
        y_stored = [sem(f"y_stored{i}") for i in range(2)]
        group_end = sem("group_end")
        act_in = [sem(f"act_in{i}") for i in range(2)]
        gates_in = [sem(f"gates_in{i}") for i in range(2)]
        hi_copied, act_split, act_used, gate_used = (sem(n) for n in ("hi_copied", "act_split", "act_used", "gate_used"))
        diag_made, diag_used, merge_done, merge_out = (sem(n) for n in ("diag_made", "diag_used", "merge_done", "merge_out"))
        res_in = [sem(f"res_in{i}") for i in range(4)]
        x1_made, x1_stored, out_made, out_stored = (sem(n) for n in ("x1_made", "x1_stored", "out_made", "out_stored"))
        up_out, u_squared, u_split, down_done, down_out = (sem(n) for n in ("up_out", "u_squared", "u_split", "down_done", "down_out"))

        block = ctx.enter_context(nc.Block())

        def key_chunks(b):
            return [(k0, min(512, (b + 1) * P - k0)) for k0 in range(0, (b + 1) * P, 512)]

        def spread(ap, n):
            return ap.rearrange("p (h o) -> p h o", o=1).broadcast_to([P, HG, n])

        def meet(e, i):
            e.drain().then_inc(met, 1)
            e.wait_ge(met, 3 * (i + 1))

        def cols(w, c0, n=WC):
            return w[:, bass.ds(c0, n)].rearrange("(k p) c -> p k c", p=P)

        W3 = "p (k c) -> p k c"

        @block.sync
        def _(sp):
            def load(n, src, dst=None, turn=None, per=0):
                s = n % 2
                if n >= 2 or turn is not None:
                    sp.wait_ge(w_split[s], n // 2 + (0 if turn is None else turn * (per // 2)))
                dst = raw[s][:, :].rearrange(W3, c=WC) if dst is None else dst
                sp.dma_start(dst, src).then_inc(raw_in[s], 16)

            for t in range(NT):
                sp.dma_start(x_tm[:, t, :], x[0, t * P:(t + 1) * P, :]).then_inc(x_landed[t], 16)
            for k in range(KT):
                sp.dma_start(ada0[:, k, :], ada_w[0, k * P:(k + 1) * P, 0:2 * D]).then_inc(ada_in, 16)
            w = w_in[0]
            load(0, cols(w, C_KV))
            small_w = raw[1][:, 0:KT * NSM].rearrange(W3, c=NSM)
            sp.dma_start(small_w[:, :, 0:DI + HI], cols(w, C_KI, DI + HI)).then_inc(raw_in[1], 16)
            sp.dma_start(small_w[:, :, DI + HI:NSM], cols(w, C_DT, NS)).then_inc(raw_in[1], 16)
            load(2, cols(w, C_QI))
            load(3, cols(w, C_QI + WC))
            with sp.Fori(0, 2) as i:
                load(4, cols(w, C_Q + i * 2 * WC), turn=i, per=2)
                load(5, cols(w, C_Q + i * 2 * WC + WC), turn=i, per=2)
            for n, w_u in ((N_UK, w_uk), (N_UK + 1, w_uv)):
                load(n, w_u[0].rearrange("(k p) h d -> p k (h d)", p=P),
                     raw[n % 2][:, :].rearrange(W3, c=NH * HD))
            with sp.Fori(0, 2) as i:
                load(N_GS, cols(w, C_GS + i * 2 * WC), turn=i, per=2)
                load(N_GS + 1, cols(w, C_GS + i * 2 * WC + WC), turn=i, per=2)
            sp.wait_ge(unit_done, 2 * NH)
            for s in range(2):
                sp.dma_start(ada_raw[s][:, :, :], cols(ada_w[0], 2 * D + s * WC)).then_inc(ada2_in[s], 16)
            with sp.Fori(0, 7) as i:
                for s in range(2):
                    sp.wait_ge(ada2_used, 2 * i + s + 1)
                    sp.dma_start(ada_raw[s][:, :, :], cols(ada_w[0], (i * 2 + 2 + s) * WC + 2 * D)).then_inc(ada2_in[s], 16)
            for b in range(4):
                sp.wait_ge(spilled[b], 16 * 8)

            def load_head(h, p):
                def one(t):
                    return t[bass.ds(h, 1)].rearrange("a p s -> p (a s)")
                sp.dma_start(hq[p][:, :], one(q_d)).then_inc(head_in[p], 16)
                sp.dma_start(hk[p][:, :], one(k_d)).then_inc(head_in[p], 16)
                sp.dma_start(hv[p][:, :, :], v_d[:, bass.ds(h * P, P)].rearrange("(t p) d -> p t d", p=P)).then_inc(head_in[p], 16)

            sp.wait_ge(met, 3 * 6)
            for p in range(2):
                load_head(p, p)
            with sp.Fori(1, NH // 2) as i:
                for p in range(2):
                    sp.wait_ge(pv_done, 4 * i + (2 * p - 2))
                    load_head(i * 2 + p, p)
            with sp.Fori(0, NG) as g:
                def load_g(j, src):
                    n = N_SSM + j
                    sp.wait_ge(w_split[n % 2], g * 3 + n // 2)
                    return sp.dma_start(raw[n % 2][:, :].rearrange(W3, c=WC), src).then_inc(raw_in[n % 2], 16)

                bc = raw[0][:, :].rearrange(W3, c=WC)
                sp.wait_ge(w_split[0], g * 3 + N_SSM // 2)
                sp.dma_start(bc[:, :, 0:P], cols(w, g * P + C_B, P)).then_inc(raw_in[0], 16)
                sp.dma_start(bc[:, :, P:WC], cols(w, g * P + C_C, P)).then_inc(c_cols_in, 16)
                load_g(1, cols(w, g * DG + C_X))
                load_g(2, cols(w, g * DG + (C_X + WC)))
                load_g(3, cols(w, g * DG + C_Z))
                load_g(4, cols(w, g * DG + (C_Z + WC)))
                load_g(5, cols(w, g * WC + C_GA))

            def load_gates(j, tile, turn=None):
                v = 4 * (j - 1)
                if j >= 2 or turn is not None:
                    sp.wait_ge(gate_used, v if turn is None else turn * 16 + v)
                sp.dma_start(gates[j % 2][:, :, :], gate_d[bass.ds(tile, 2)].rearrange("a p s -> p a s")).then_inc(gates_in[j % 2], 16)

            for j in range(4):
                load(N_O + j, cols(w_o_att[0], j * WC))
                if j == 1:
                    sp.wait_ge(group_end, 3 * NG)
                    load_gates(0, 0)
                    load_gates(1, 2)
                elif j >= 2:
                    load_gates(j, 2 * j)
            with sp.Fori(0, 2) as i:
                rows_o = w_o_ssd[0][bass.ds(i * D, D), :]
                for j in range(4):
                    load(N_O + 4 + j, cols(rows_o, j * WC), turn=i, per=4)
                    load_gates(4 + j, KT + 2 * j, turn=i)
            for j in range(4):
                load(N_OUT + j, cols(w_out[0], j * WC))
            sp.wait_ge(met, 3 * 10)
            for t in range(NT):
                if t >= 4:
                    sp.wait_ge(x1_made, t - 3)
                sp.dma_start(x_in[t % 4][:, :], x[0, t * P:(t + 1) * P, :]).then_inc(res_in[t % 4], 16)

            def down(j):
                return w_down[0][bass.ds(j * WC, WC), :].rearrange("(k p) c -> p k c", p=P)

            def load_down(n, j, turn=None):
                load(n, down(j), raw[n % 2][:, :].rearrange(W3, c=D), turn=turn, per=4)

            load(N_MLP, cols(w_up[0], 0))
            with sp.Fori(0, NC // 2 - 1) as i:
                load(N_MLP + 1, cols(w_up[0], i * 2 * WC + WC), turn=i, per=4)
                load_down(N_MLP + 2, i * 2, turn=i)
                load(N_MLP + 3, cols(w_up[0], i * 2 * WC + 2 * WC), turn=i, per=4)
                load_down(N_MLP + 4, i * 2 + 1, turn=i)
            load(N_ALL - 3, cols(w_up[0], (NC - 1) * WC))
            load_down(N_ALL - 2, NC - 2)
            load_down(N_ALL - 1, NC - 1)
            sp.wait_ge(met, 3 * 13)
            for t in range(NT):
                if t >= 4:
                    sp.wait_ge(out_made, t - 3)
                sp.dma_start(x_in[t % 4][:, :], x1_d[t * P:(t + 1) * P, :]).then_inc(res_in[t % 4], 16)
            for t in range(NT):
                sp.wait_ge(out_made, t + 1)
                sp.dma_start(out[0, t * P:(t + 1) * P, :], x_tm[:, t, :]).then_inc(out_stored, 16)
            sp.wait_ge(out_stored, 16 * NT)

        @block.gpsimd
        def _(pool):
            nc.gpsimd.memset(ones[:, :], 1.0).then_inc(const_made, 1)
            nc.gpsimd.memset(ident[:, :], 0.0).then_inc(const_made, 1)
            nc.gpsimd.memset(future[:, :], 0.0).then_inc(const_made, 1)
            nc.gpsimd.memset(past_bf[:, :], 0.0).then_inc(const_made, 1)
            pool.wait_ge(const_made, 4)
            nc.gpsimd.affine_select(out=ident[:, :], in_=ident[:, :], compare_op=ALU.not_equal, fill=1.0,
                                    base=0, pattern=[[-1, P]], channel_multiplier=1).then_inc(const_made, 1)
            nc.gpsimd.affine_select(out=tri[:, :], in_=ones[:, :], compare_op=ALU.is_ge, fill=0.0,
                                    base=0, pattern=[[1, P]], channel_multiplier=-1).then_inc(const_made, 1)
            nc.gpsimd.affine_select(out=future[:, :], in_=future[:, :], compare_op=ALU.is_ge, fill=NEG,
                                    base=0, pattern=[[-1, P]], channel_multiplier=1).then_inc(const_made, 1)
            nc.gpsimd.affine_select(out=past_bf[:, :], in_=past_bf[:, :], compare_op=ALU.is_ge, fill=NEG,
                                    base=0, pattern=[[1, P]], channel_multiplier=-1).then_inc(const_made, 1)
            pool.wait_ge(const_made, 8)
            nc.gpsimd.tensor_copy(ident_bf[:, :], ident[:, :]).then_inc(const_made, 1)

            def split(n, width=KT * WC, turn=None, per=2, landed=16):
                s, v = n % 2, n // 2
                if turn is not None:
                    v = turn * (per // 2) + v
                pool.wait_ge(raw_in[s], v * 16 + (landed + (16 if n >= 2 and s == 1 else 0)))
                if n >= 2:
                    pool.wait_ge(w_used[s], v)
                pool.sem_inc(pool_own, 1)
                src, hi, lo = raw[s][:, 0:width], w_hi[s][:, 0:width], w_lo[s][:, 0:width]
                nc.gpsimd.tensor_copy(hi, src).then_inc(hi_made, 1)
                pool.wait_ge(hi_made, n + 1 if turn is None else turn * per + (n + 1))
                nc.gpsimd.tensor_tensor(lo, src, hi.bitcast(F32), ALU.subtract).then_inc(w_split[s], 1)

            split(0)
            split(1, width=KT * NSM, landed=32)
            with pool.Fori(0, (N_SSM - 2) // 2) as i:
                split(2, turn=i)
                split(3, turn=i)
            with pool.Fori(0, NG) as g:
                pool.wait_ge(c_cols_in, g * 16 + 16)
                for j in range(6):
                    split(N_SSM + j, turn=g, per=6)
            with pool.Fori(0, (N_ALL - N_O) // 2) as i:
                split(N_O, turn=i)
                split(N_O + 1, turn=i)
            pool.wait_ge(pool_own, N_ALL)

        @block.tensor
        def _(pe):
            def w_tile(t, s, k, c0, c1, width=WC):
                return t[s][:, k * width + c0:k * width + c1]

            def w_wait(n, extra=0):
                pe.wait_ge(w_split[n % 2], n // 2 + 1 + extra)

            def mm(o, a, b, start=False, stop=False):
                return nc.tensor.matmul(o, a, b, start=start, stop=stop)

            def fm_block(n, group, extra=0, act_ready=None, act_used=None):
                s = n % 2
                w_wait(n, extra)
                for k in range(KT):
                    if act_ready is not None:
                        act_ready(k)
                    for m in range(2):
                        wh = w_tile(w_hi, s, k, m * P, m * P + P)
                        wl = w_tile(w_lo, s, k, m * P, m * P + P)
                        for q in range(2):
                            o = ps[:, 4 * group + 2 * m + q, :]
                            r = slice(q * 512, q * 512 + 512)
                            mm(o, wh, a_hi[:, k, r], start=(k == 0))
                            mm(o, wh, a_lo[:, k, r])
                        for q in range(2):
                            last = mm(ps[:, 4 * group + 2 * m + q, :], wl, a_hi[:, k, q * 512:q * 512 + 512],
                                      stop=(k == KT - 1))
                    if act_used is not None:
                        last = act_used(k, last)
                return last

            def tm_token(n, t, o, width, stationary=None, nk=KT, c0=0, wwidth=None):
                s = n % 2
                sh, sl = stationary or (a_hi, a_lo)
                ww = wwidth or width
                for k in range(nk):
                    r = slice(t * P, t * P + P)
                    wh, wl = (w_tile(w, s, k, c0, c0 + width, ww) for w in (w_hi, w_lo))
                    mm(o, sh[:, k, r], wh, start=(k == 0))
                    mm(o, sh[:, k, r], wl)
                    last = mm(o, sl[:, k, r], wh, stop=(k == nk - 1))
                return last

            def norm_turn(j):
                for i in range(2 * KT):
                    g, k = divmod(i, KT)
                    pe.wait_ge(normed, 8 * j + 4 * (g + 1))
                    if i >= 4:
                        pe.wait_ge(h_ready, 16 * j + i - 3)
                    for t in range(4):
                        last = nc.tensor.transpose(ps[:, 4 + i % 4, t * P:(t + 1) * P],
                                                   x_tm[:, 4 * g + t, k * P:(k + 1) * P], ident[:, :])
                    last.then_inc(turned, 1)

            pe.wait_ge(const_made, 9)
            pe.wait_ge(small_in, 16 * 11)
            nc.tensor.transpose(ps[:, 0, 0:112], rows_a[:, :], ident[0:112, 0:112])
            nc.tensor.transpose(ps[:, 1, 0:112], rows_b[:, :], ident[0:112, 0:112]).then_inc(vec_turned, 1)
            pe.wait_ge(c_ready, 1)
            pe.wait_ge(ada_in, 16 * KT)
            for m in range(2 * KT):
                for k in range(KT):
                    last = mm(ps[:, 2, m:m + 1], ada0[:, k, m * P:(m + 1) * P], c_act[:, k:k + 1],
                              start=(k == 0), stop=(k == KT - 1))
            last.then_inc(mod0_done, 1)
            norm_turn(0)
            meet(pe, 0)

            w_wait(0)
            for t in range(NT):
                last = tm_token(0, t, ps[:, t, 0:R], R)
            last.then_inc(w_used[0], 1)
            w_wait(1)
            for t in range(NT):
                last = tm_token(1, t, ps[:, t, R:R + NSM], NSM)
            last.then_inc(w_used[1], 1)
            meet(pe, 1)
            meet(pe, 2)
            for b in range(2):
                fm_block(2 + b, b).then_inc(w_used[b], 1)
            pe.wait_ge(qi_out, 4)
            for g in range(2):
                for t in range(4):
                    last = nc.tensor.transpose(ps[:, g, t * P:(t + 1) * P], kidx_tm[:, 4 * g + t, :], ident[:, :])
            for r in range(2):
                for g in range(2):
                    for t in range(4):
                        last = nc.tensor.transpose(ps[:, 2 + 2 * r + g, t * P:(t + 1) * P],
                                                   ckv_tm[:, 4 * g + t, r * P:(r + 1) * P], ident[:, :])
            last.then_inc(kv_turned, 1)
            meet(pe, 3)
            i = 0
            for b in range(NT):
                for k0 in range(0, (b + 1) * P, 512):
                    n = min(512, (b + 1) * P - k0)
                    for h in range(HI):
                        if i >= 4:
                            pe.wait_ge(relu_done, i - 3)
                        o = DI * (h % 2)
                        mm(ps[:, i % 4, 0:n], q_idx[o:o + DI, h // 2, b * P:(b + 1) * P], k_idx[o:o + DI, k0:k0 + n],
                           start=True, stop=True).then_inc(logit_done, 1)
                        i += 1
            meet(pe, 4)

            def fm_unit_blocks(n, u, turns):
                with pe.Fori(0, turns) as i:
                    for j in range(2):
                        first = u + 2 * j
                        pe.wait_ge(unit_out, i * 4 + (first - 2) if first >= 2 else i * 4)
                        fm_block(n + j, (first % 4) // 2, extra=i).then_inc(w_used[(n + j) % 2], 1)

            fm_block(4, 0).then_inc(w_used[0], 1)
            fm_block(5, 1).then_inc(w_used[1], 1)
            pe.wait_ge(unit_out, 2)
            fm_block(6, 0).then_inc(w_used[0], 1)
            pe.wait_ge(unit_out, 4)
            fm_block(7, 1).then_inc(w_used[1], 1)
            u = 8
            s = N_UK % 2
            w_wait(N_UK)
            for h in range(NH):
                pe.wait_ge(unit_out, u - 3)
                for q in range(2):
                    o = ps[:, 2 * (u % 4) + q, :]
                    r = slice(q * 512, q * 512 + 512)
                    for k in range(2):
                        wh, wl = (w_tile(t, s, k, h * P, h * P + P, NH * HD) for t in (w_hi, w_lo))
                        mm(o, wh, ckv_hi[:, k, r], start=(k == 0))
                        mm(o, wh, ckv_lo[:, k, r])
                        last = mm(o, wl, ckv_hi[:, k, r], stop=(k == 1))
                last.then_inc(unit_done, 1)
                u += 1
            w_wait(N_UK + 1)
            for t in range(NT):
                pe.wait_ge(unit_out, u - 3)
                for q in range(2):
                    last = tm_token(N_UK + 1, t, ps[:, 2 * (u % 4) + q, :], 512, (ckv_hi, ckv_lo), 2, q * 512, NH * HD)
                last.then_inc(unit_done, 1)
                u += 1
            pe.drain().then_inc(w_used[0], 1)
            pe.drain().then_inc(w_used[1], 1)
            fm_unit_blocks(N_GS, u, 2)
            pe.wait_ge(unit_out, 32)
            with pe.Fori(0, 8) as i:
                for s in range(2):
                    pe.wait_ge(ada2_in[s], i * 16 + 16)
                    for m in range(2):
                        for k in range(KT):
                            last = mm(ps[:, 0, bass.ds(i * 4 + (2 * s + m), 1)], ada_raw[s][:, k, m * P:m * P + P],
                                      c_act[:, k:k + 1], start=(k == 0), stop=(k == KT - 1))
                    last.then_inc(ada2_used, 1)
            meet(pe, 5)

            STEPS = 2 * NT
            with pe.Fori(0, NH // 2) as i:
                turns = 0
                for t in range(STEPS + 2):
                    if t < STEPS:
                        p, b = divmod(t, NT)
                        if b == 0:
                            pe.wait_ge(head_in[p], i * 48 + 48)
                        if t >= 2:
                            pe.wait_ge(masked, i * STEPS + (t - 1))
                        for j, (k0, n) in enumerate(key_chunks(b)):
                            last = mm(ps[:, 2 * (t % 2) + j, 0:n], hq[p][:, b * P:(b + 1) * P], hk[p][:, k0:k0 + n],
                                      start=True, stop=True)
                        last.then_inc(qk_done, 1)
                    if t >= 5 and (t - 2) % 4 == 3:
                        g = (t - 2) // 4
                        p, half = divmod(g, 2)
                        pe.wait_ge(pt_out, i * 24 + 12 * p + (4, 12)[half])
                        if g >= 2:
                            pe.wait_ge(pv_out, i * 4 + (g - 1))
                        nk = 4 * half + 4
                        for k in range(nk):
                            q0 = max(0, k - 4 * half) * P
                            last = mm(ps[:, 6 + g % 2, q0:512], hv[p][:, k, :], probT[g % 2][:, k, q0:512],
                                      start=(k == 0), stop=(k == nk - 1))
                        last.then_inc(pv_done, 1)
                    if 1 <= t <= STEPS:
                        b = (t - 1) % NT
                        pe.wait_ge(p_ready, i * STEPS + t)
                        for k in range(b + 1):
                            if k % 4 == 0 and turns >= 2:
                                pe.wait_ge(pt_out, i * 24 + (turns - 1))
                            last = nc.tensor.transpose(ps[:, 4 + turns % 2, (k % 4) * P:(k % 4 + 1) * P],
                                                       prob[(t - 1) % 2][:, k * P:(k + 1) * P], ident[:, :])
                            if k % 4 == 3 or k == b:
                                last.then_inc(pt_done, 1)
                                turns += 1
            meet(pe, 6)

            pe.wait_ge(dta_ready, 1)
            flat = "p c h -> p (c h)"
            mm(ps[:, 0, 0:NT * NS], tri[:, :], dta[:, :, :].rearrange(flat), start=True, stop=True)
            mm(ps[:, 1, 0:NT * NS], ones[:, :], dta[:, :, :].rearrange(flat), start=True, stop=True).then_inc(acum_done, 1)
            meet(pe, 7)
            with pe.Fori(0, NG) as g:
                def turn_tile(r, src):
                    pe.wait_ge(silu_done, g * 6 + (1, 3, 4, 5, 6)[r])
                    if r >= 2:
                        pe.wait_ge(tile_out, g * 5 + (r - 1))
                    for t in range(NT):
                        last = nc.tensor.transpose(ps[:, 2 * (r % 2) + t // 4, (t % 4) * P:(t % 4 + 1) * P],
                                                   src[:, t * P:(t + 1) * P], ident[:, :])
                    last.then_inc(tile_turned, 1)

                def z_block(j):
                    n = N_SSM + 3 + j
                    w_wait(n, g * 3)
                    for t in range(NT):
                        v = NT * j + t
                        if v >= 4:
                            pe.wait_ge(z_out, g * 16 + (v - 3))
                        last = tm_token(n, t, ps[:, 4 + v % 4, 0:WC], WC)
                        last.then_inc(z_done, 1)
                    pe.drain().then_inc(w_used[n % 2], 1)

                fm_block(N_SSM, 0, extra=g * 3).then_inc(w_used[0], 1)
                fm_block(N_SSM + 1, 1, extra=g * 3).then_inc(w_used[1], 1)
                pe.wait_ge(conv_in, g * 6 + 2)
                fm_block(N_SSM + 2, 0, extra=g * 3).then_inc(w_used[0], 1)
                pe.wait_ge(conv_in, g * 6 + 4)
                z_block(0)
                pe.wait_ge(conv_in, g * 6 + 6)
                turn_tile(0, b_fm)
                turn_tile(1, c_out[0])
                turn_tile(2, c_out[1])
                z_block(1)
                turn_tile(3, c_out[0])
                turn_tile(4, c_out[1])
                pe.wait_ge(z_out, g * 16 + 16)
                fm_block(N_SSM + 5, 1, extra=g * 3).then_inc(w_used[1], 1)
                pe.wait_ge(tile_out, g * 5 + 5)
                pe.wait_ge(ga_out, g * 2 + 2)
                pe.wait_ge(dtag_ready, g + 1)

                def segments(k):
                    if k >= 1:
                        pe.wait_ge(cb_out, g * NT + k)
                    r = slice(k * P, k * P + P)
                    mm(ps[:, 7, 0:P], b_fm[:, r], c_fm[:, r], start=True, stop=True)
                    if k >= 2:
                        pe.wait_ge(seg_out, g * NT + (k - 1))
                    for j in range(2):
                        o = ps[:, 2 * (k % 2) + j, :]
                        mm(o.rearrange("p (h l) -> p h l", h=4), ident_bf[:, :],
                           past_bf[:, :].rearrange("p (o l) -> p o l", o=1).broadcast_to([P, 4, P]), start=True)
                        for h in range(4):
                            last = mm(o[:, h * P:(h + 1) * P],
                                      dta_g[:, k, 4 * j + h:4 * j + h + 1].broadcast_to([P, P]), tri[:, :], stop=(h == 3))
                    last.then_inc(seg_done, 1)

                segments(0)
                for k in range(NT):
                    if k + 1 < NT:
                        segments(k + 1)
                    pe.wait_ge(mix_ready, g * NT + (k + 1))
                    if k >= 1:
                        pe.wait_ge(y_ready, g * NT + k)
                    for h in range(HG):
                        mm(ps[:, 4, h * PD:(h + 1) * PD], decay[k % 2][:, h, :], xdt[k % 2][:, h, :], start=True, stop=True)
                    if k >= 1:
                        pe.wait_ge(state_ready, g * 7 + k)
                        mm(ps[:, 5, :], c_fm[:, k * P:(k + 1) * P], state[:, :, :].rearrange("p h d -> p (h d)"),
                           start=True, stop=True)
                    mm(ps[:, 6, :], b_tm[:, k, :], xde[k % 2][:, :, :].rearrange("p h d -> p (h d)"),
                       start=True, stop=True).then_inc(mix_done, 1)
                for f in range(4):
                    if f == 0:
                        pe.wait_ge(gn_ready, g * NT + NT)
                    if f >= 2:
                        pe.wait_ge(yt_out, g * 4 + (f - 1))
                    for t in range(NT):
                        last = nc.tensor.transpose(ps[:, 4 + 2 * (f % 2) + t // 4, (t % 4) * P:(t % 4 + 1) * P],
                                                   zy[:, t, f * P:(f + 1) * P], ident[:, :])
                    last.then_inc(yt_done, 1)
                pe.drain().then_inc(group_end, 1)
                pe.wait_ge(group_end, g * 3 + 3)

            def out_block(n, j, o, turn=None):
                def at_turn(v, per):
                    return v if turn is None else turn * per + v
                v = 4 * (4 * o + j - 1)
                if 4 * o + j >= 2:
                    pe.wait_ge(gate_used, at_turn(v, 16))
                ready = (lambda k: pe.wait_ge(act_split, at_turn(8 * o + k + 1, 8))) if j == 0 else None
                used = (lambda k, ins: ins.then_inc(act_used, 1)) if j == 3 else None
                last = fm_block(n, j % 2, extra=0 if turn is None else turn * 2, act_ready=ready, act_used=used)
                if j == 3:
                    pe.drain().then_inc(w_used[n % 2], 1)
                else:
                    last.then_inc(w_used[n % 2], 1)

            for j in range(4):
                out_block(N_O + j, j, 0)
            with pe.Fori(0, 2) as i:
                for j in range(4):
                    out_block(N_O + 4 + j, j, 1, turn=i)
            meet(pe, 8)
            for i in range(2 * KT):
                pe.wait_ge(diag_made, i + 1)
                mm(ps[:, i // 4, (i % 4) * P:(i % 4 + 1) * P], ones[:, :], diag[i % 2][:, :],
                   start=True, stop=True).then_inc(diag_used, 1)
            meet(pe, 9)
            pe.wait_ge(act_split, 4 * KT)
            for j in range(4):
                n = N_OUT + j
                w_wait(n)
                for t in range(NT):
                    if j:
                        pe.wait_ge(merge_out, 8 * j + t - 7)
                    last = tm_token(n, t, ps[:, t, 0:WC], WC)
                    last.then_inc(merge_done, 1)
                pe.drain().then_inc(w_used[n % 2], 1)
            meet(pe, 10)
            norm_turn(1)
            meet(pe, 11)

            def up(n, c, extra=0):
                if c is not None:
                    pe.wait_ge(up_out, c * 4)
                fm_block(n, 0, extra=extra).then_inc(w_used[n % 2], 1)

            def down(n, c, b, extra=0, first=False):
                w_wait(n, extra)
                pe.wait_ge(u_split, c * 4 + 4)
                for t in range(NT):
                    if t >= 2 or not first:
                        pe.wait_ge(down_out, c * 8 + (t - 1))
                    for q in range(2):
                        last = tm_token(n, t, ps[:, 4 + 2 * (t % 2) + q, :], 512, (u_hi[b], u_lo[b]), 2, q * 512, D)
                    last.then_inc(down_done, 1)
                pe.drain().then_inc(w_used[n % 2], 1)

            up(N_MLP, None)
            up(N_MLP + 1, 1)
            down(N_MLP + 2, 0, 0, first=True)
            up(N_MLP + 3, 2)
            down(N_MLP + 4, 1, 1)
            with pe.Fori(1, NC // 2 - 1) as i:
                up(N_MLP + 1, i * 2 + 1, extra=i * 2)
                down(N_MLP + 2, i * 2, 0, extra=i * 2)
                up(N_MLP + 3, i * 2 + 2, extra=i * 2)
                down(N_MLP + 4, i * 2 + 1, 1, extra=i * 2)
            up(N_ALL - 3, NC - 1)
            down(N_ALL - 2, NC - 2, 0)
            down(N_ALL - 1, NC - 1, 1)
            meet(pe, 12)

        @block.scalar
        def _(act):
            A = Count(act, act_own)

            def norm_stats(j, src, wait, sq):
                for t in range(NT):
                    wait(t)
                    ins = nc.scalar.activation(sq[:, :], src[:, t, :], ACT.Square, accum_out=stat[:, 16 * j + t:16 * j + t + 1])
                    A.link(ins)
                act.sem_inc(squares, 1)
                act.wait_ge(vars_ready, j + 1)
                nc.scalar.activation(stat[:, 16 * j:16 * j + NT], stat[:, 16 * j:16 * j + NT], ACT.Sqrt).then_inc(roots, 1)

            def norm_evac(j, shift):
                for i in range(2 * KT):
                    k = i % KT
                    act.wait_ge(turned, 16 * j + i + 1)
                    if i >= 4:
                        act.wait_ge(h_split, 16 * j + i - 3)
                    if i == 0 and j == 0:
                        act.wait_ge(gain_ready, 1)
                    nc.scalar.activation(h_tmp[i % 4][:, :], ps[:, 4 + i % 4, :], ACT.Identity,
                                         bias=mod[:, shift + k:shift + k + 1],
                                         scale=gain[:, j * KT + k:j * KT + k + 1]).then_inc(h_ready, 1)

            def rows(t, n):
                return t.rearrange("(a p) -> a p", p=P)

            act.dma_start(rows_a[0:48, :], rows(ada_b[0], 48)).then_inc(small_in, 16)
            act.dma_start(rows_a[48:56, :], rows(c[0], 8)).then_inc(small_in, 16)
            act.dma_start(rows_a[56:88, :], norm_g[0].rearrange("j (a p) -> (j a) p", p=P)).then_inc(small_in, 16)
            act.dma_start(rows_a[88:112, :], rows(conv_b[0], 24)).then_inc(small_in, 16)
            act.dma_start(rows_b[0:96, :], conv_w[0].rearrange("j (a p) -> (j a) p", p=P)).then_inc(small_in, 16)
            act.dma_start(rows_b[96:112, :], rows(ssm_norm_g[0], 16)).then_inc(small_in, 16)
            for dst, src, n in ((kv_row, kv_norm_g, R), (ki_row, kidx_norm_g, DI), (dtb_row, dt_bias, NS),
                                (alog_row, a_log, NS), (skip_row, d_skip, NS)):
                act.dma_start(dst[:, :], src[0:1, :].broadcast_to([P, n])).then_inc(small_in, 16)
            act.wait_ge(vec_turned, 1)
            A.add(nc.scalar.copy(vec_a[:, :], ps[:, 0, 0:112]))
            A.link(nc.scalar.copy(vec_b[:, :], ps[:, 1, 0:112]))
            nc.scalar.activation(c_act[:, :], vec_a[:, 48:56], ACT.Silu).then_inc(c_ready, 1)
            norm_stats(0, x_tm, lambda t: act.wait_ge(x_landed[t], 16), sq0)
            act.wait_ge(mod0_done, 1)
            nc.scalar.copy(mod[:, 0:16], ps[:, 2, 0:16]).then_inc(c_ready, 1)
            norm_evac(0, 0)
            meet(act, 0)

            meet(act, 1)
            for t in range(NT):
                A.link(nc.scalar.activation(sq0[:, 0:R], ps[:, t, 0:R], ACT.Square, accum_out=stat[:, 64 + t:65 + t]))
                A.link(nc.scalar.activation(sq0[:, 0:DI], ps[:, t, R:R + DI], ACT.Square, accum_out=stat[:, 72 + t:73 + t]))
            act.sem_inc(kv_sq, 1)
            act.wait_ge(kv_var, 1)
            nc.scalar.activation(stat[:, 64:80], stat[:, 64:80], ACT.Sqrt).then_inc(kv_root, 1)
            meet(act, 2)
            for b in range(2):
                act.wait_ge(w_used[b], 2)
                for m in range(2):
                    nc.scalar.copy(q_idx[:, 2 * b + m, :].rearrange("p (a b) -> p a b", a=2),
                                   ps[:, 4 * b + 2 * m:4 * b + 2 * m + 2, :]).then_inc(qi_out, 1)
            act.wait_ge(kv_turned, 1)
            nc.scalar.copy(k_idx[:, :].rearrange("p (a b) -> p a b", a=2), ps[:, 0:2, :])
            for r in range(2):
                nc.scalar.copy(sq0[:, :].rearrange("p (a b) -> p a b", a=2), ps[:, 2 + 2 * r:4 + 2 * r, :]).then_inc(kv_out, 1)
                act.wait_ge(kv_out_split, r + 1)
            meet(act, 3)
            i = 0
            for b in range(NT):
                for k0 in range(0, (b + 1) * P, 512):
                    n = min(512, (b + 1) * P - k0)
                    for h in range(HI):
                        act.wait_ge(logit_done, i + 1)
                        if i >= 4:
                            act.wait_ge(relu_used, i - 3)
                        nc.scalar.activation(relu_buf[:, i % 4, 0:n], ps[:, i % 4, 0:n], ACT.Relu).then_inc(relu_done, 1)
                        i += 1
            meet(act, 4)

            def unit(u, func, dst, turn=None, per=0):
                b = u % 4
                if u >= 4 or turn is not None:
                    act.wait_ge(spilled[b], 16 * (u // 4) + (0 if turn is None else turn * (4 * per)))
                nc.scalar.activation(spill[b][:, :].rearrange("p (a b) -> p a b", a=2),
                                     ps[:, 2 * b:2 * b + 2, :], func).then_inc(unit_out, 1)
                act.wait_ge(unit_out, u + 1 + (0 if turn is None else turn * per))
                act.dma_start(dst, spill[b][:, :]).then_inc(spilled[b], 16)

            def fm_units(n, u, func, dst, turns):
                with act.Fori(0, turns) as i:
                    for j in range(4):
                        if j % 2 == 0:
                            act.wait_ge(w_used[(n + j // 2) % 2], (n + j // 2) // 2 + 1 + i)
                        unit(u + j, func, dst(i, j), turn=i, per=4)

            for j in range(8):
                if j % 2 == 0:
                    act.wait_ge(w_used[(j // 2) % 2], 3 + j // 4)
                unit(j, ACT.Copy, q_d[j])
            for u in range(8, 24):
                act.wait_ge(unit_done, u - 7)
                unit(u, ACT.Copy, k_d[u - 8] if u < 16 else v_d[(u - 16) * P:(u - 15) * P, :])
            fm_units(N_GS, 24, ACT.Sigmoid, lambda i, j: gate_d[bass.ds(i * 4 + (KT + j), 1)].rearrange("a p s -> p (a s)"), 2)
            act.wait_ge(ada2_used, 16)
            nc.scalar.copy(mod[:, 16:48], ps[:, 0, 0:32]).then_inc(mod_ready, 1)
            meet(act, 5)

            STEPS = 2 * NT
            with act.Fori(0, NH // 2) as i:
                turns = 0
                for t in range(STEPS + 2):
                    if t < STEPS:
                        b = t % NT
                        n = (b + 1) * P
                        act.wait_ge(masked, i * STEPS + (t + 1))
                        st = 4 * (t % 4)
                        nc.scalar.activation(prob[t % 2][:, 0:n], prob[t % 2][:, 0:n], ACT.Exp, scale=SCALE,
                                             bias=att_stat[:, st + 1:st + 2],
                                             accum_out=att_stat[:, st + 2:st + 3]).then_inc(exp_done, 1)
                    if t >= 5 and (t - 2) % 4 == 3:
                        g = (t - 2) // 4
                        act.wait_ge(pv_done, i * 4 + (g + 1))
                        if g >= 2:
                            act.wait_ge(att_stored[g % 2], i * 32 + 16)
                        nc.scalar.copy(att_o[g % 2][:, :], ps[:, 6 + g % 2, :]).then_inc(pv_out, 1)
                        act.wait_ge(pv_out, i * 4 + (g + 1))
                        dst = acts_d[bass.ds(i * 2 + g // 2, 1)].rearrange("a p s -> p (a s)")
                        act.dma_start(dst[:, (g % 2) * 512:(g % 2) * 512 + 512], att_o[g % 2][:, :]).then_inc(att_stored[g % 2], 16)
                    if 1 <= t <= STEPS:
                        b = (t - 1) % NT
                        g = (t - 1) // 4
                        q0 = (b % 4) * P
                        for k0 in range(0, b + 1, 4):
                            m = min(4, b + 1 - k0)
                            act.wait_ge(pt_done, i * 24 + (turns + 1))
                            if g >= 2:
                                act.wait_ge(pv_done, i * 4 + (g - 1))
                            nc.scalar.copy(probT[g % 2][:, k0:k0 + m, q0:q0 + P],
                                           ps[:, 4 + turns % 2, 0:m * P].rearrange("p (k q) -> p k q", k=m)).then_inc(pt_out, 1)
                            turns += 1
                for p in range(2):
                    act.wait_ge(att_stored[p], i * 32 + 32)
            meet(act, 6)

            flat = "p c h -> p (c h)"
            act.wait_ge(dt_abs, 1)
            nc.scalar.activation(ea[:, :, :], acum[:, :, :], ACT.Exp, scale=-1.0).then_inc(dt_exp, 1)
            nc.scalar.activation(alog_row[:, :], alog_row[:, :], ACT.Exp).then_inc(dt_exp, 1)
            act.wait_ge(dt_plus, 1)
            nc.scalar.activation(dec[:, :, :], dte[:, :, :], ACT.Ln).then_inc(dt_ln, 1)
            act.wait_ge(acum_done, 1)
            nc.scalar.copy(acum[:, :, :].rearrange(flat), ps[:, 0, 0:NT * NS]).then_inc(aend_out, 1)
            nc.scalar.activation(ea[:, :, :].rearrange(flat), ps[:, 0, 0:NT * NS], ACT.Exp).then_inc(aend_out, 1)
            nc.scalar.activation(dec[:, :, :].rearrange(flat), ps[:, 1, 0:NT * NS], ACT.Exp).then_inc(aend_out, 1)
            act.wait_ge(dte_ready, 1)
            nc.scalar.activation(dte[:, :, :], dte[:, :, :], ACT.Exp)
            meet(act, 7)
            with act.Fori(0, NG) as g:
                A.enter(g, 1)

                def evac(T):
                    if T >= 2:
                        act.wait_ge(conv_done, g * 6 + (T - 1))
                    nc.scalar.copy(c_in[T % 2][:, TAPS - 1:TAPS - 1 + SEQ].rearrange("p (a b) -> p a b", a=2),
                                   ps[:, 2 * (T % 4):2 * (T % 4) + 2, :]).then_inc(conv_in, 1)

                def silu(T):
                    act.wait_ge(conv_done, g * 6 + (T + 1))
                    dst = (b_fm, c_fm, *c_out, *c_out)[T]
                    col = (g + (88 + 16), g + (88 + 20))[T] if T < 2 else g * 4 + (88 + T - 2)
                    nc.scalar.activation(dst[:, :], c_out[T % 2][:, :], ACT.Silu,
                                         bias=vec_a[:, bass.ds(col, 1)]).then_inc(silu_done, 1)

                def z_evac(j):
                    for t in range(NT):
                        v = NT * j + t
                        act.wait_ge(z_done, g * 16 + (v + 1))
                        nc.scalar.activation(zy[:, t, WC * j:WC * j + WC], ps[:, 4 + v % 4, 0:WC], ACT.Silu).then_inc(z_out, 1)

                def tile_evac(r):
                    act.wait_ge(tile_turned, g * 5 + (r + 1))
                    dst = b_tm[:, :, :] if r == 0 else xs_tm[:, :, (r - 1) * P:r * P]
                    nc.scalar.copy(dst, ps[:, 2 * (r % 2):2 * (r % 2) + 2, :].rearrange("p a (b f) -> p (a b) f", f=P)).then_inc(tile_out, 1)

                act.wait_ge(w_used[0], g * 3 + (N_SSM // 2 + 1))
                evac(0)
                evac(1)
                silu(0)
                silu(1)
                act.wait_ge(w_used[1], g * 3 + (N_SSM // 2 + 1))
                evac(2)
                evac(3)
                silu(2)
                silu(3)
                act.wait_ge(w_used[0], g * 3 + (N_SSM // 2 + 2))
                evac(4)
                evac(5)
                z_evac(0)
                tile_evac(0)
                tile_evac(1)
                tile_evac(2)
                silu(4)
                silu(5)
                z_evac(1)
                tile_evac(3)
                tile_evac(4)
                act.wait_ge(w_used[1], g * 3 + (N_SSM // 2 + 3))
                for m in range(2):
                    nc.scalar.activation(c_in[m][:, TAPS - 1:TAPS - 1 + SEQ].rearrange("p (a b) -> p a b", a=2),
                                         ps[:, 4 + 2 * m:6 + 2 * m, :], ACT.Sigmoid).then_inc(ga_out, 1)
                for m in range(2):
                    act.wait_ge(ga_out, g * 2 + (m + 1))
                    act.dma_start(gate_d[bass.ds(g * 2 + m, 1)].rearrange("a p s -> p (a s)"),
                                  c_in[m][:, TAPS - 1:TAPS - 1 + SEQ]).then_inc(ga_stored[m], 16)

                def squares_of(k):
                    act.wait_ge(y_ready, g * NT + (k + 1))
                    nc.scalar.activation(c_out[k % 2][:, 0:DG], zy[:, k, :], ACT.Square,
                                         accum_out=stat[:, 96 + k:97 + k]).then_inc(gn_squares, 1)
                    act.wait_ge(gn_squares, g * NT + (k + 1))

                for k in range(NT):
                    act.wait_ge(seg_done, g * NT + (k + 1))
                    if k >= 1:
                        act.wait_ge(mix_ready, g * NT + k)
                    nc.scalar.copy(cb_sb[:, :], ps[:, 7, 0:P]).then_inc(cb_out, 1)
                    act.wait_ge(seg_out, g * NT + (k + 1))
                    nc.scalar.activation(decay[k % 2][:, :, :], decay[k % 2][:, :, :], ACT.Exp).then_inc(decay_done, 1)
                    if k >= 1:
                        squares_of(k - 1)
                squares_of(NT - 1)
                act.wait_ge(gn_var, g + 1)
                nc.scalar.activation(stat[:, 96:104], stat[:, 96:104], ACT.Sqrt).then_inc(gn_root, 1)
                for f in range(4):
                    act.wait_ge(yt_done, g * 4 + (f + 1))
                    if f >= 2:
                        act.wait_ge(y_stored[f % 2], g * 32 + 16)
                    nc.scalar.activation(c_out[f % 2][:, :].rearrange("p (a b) -> p a b", a=2),
                                         ps[:, 4 + 2 * (f % 2):6 + 2 * (f % 2), :], ACT.Copy,
                                         scale=vec_b[:, bass.ds(g * 4 + (96 + f), 1)]).then_inc(yt_out, 1)
                    act.wait_ge(yt_out, g * 4 + (f + 1))
                    act.dma_start(acts_d[bass.ds(g * 4 + (KT + f), 1)].rearrange("a p s -> p (a s)"),
                                  c_out[f % 2][:, :]).then_inc(y_stored[f % 2], 16)
                for m in range(2):
                    act.wait_ge(ga_stored[m], g * 16 + 16)
                    act.wait_ge(y_stored[m], g * 32 + 32)
                A.step()
                act.drain().then_inc(group_end, 1)
                A.leave(NG)
                act.wait_ge(group_end, g * 3 + 3)

            def act_load(k, tile):
                act.dma_start(act_raw[k % 2][:, :], acts_d[bass.ds(tile, 1)].rearrange("a p s -> p (a s)")).then_inc(act_in[k % 2], 16)

            for k in range(2):
                act_load(k, k)
            for k in range(KT):
                act.wait_ge(act_in[k % 2], 16 * (k // 2 + 1))
                nc.scalar.copy(a_hi[:, k, :], act_raw[k % 2][:, :]).then_inc(hi_copied, 1)
                if k < KT - 2:
                    act.wait_ge(act_split, k + 1)
                    act_load(k, k + 2)
            with act.Fori(0, 2) as i:
                for k in range(2):
                    act.wait_ge(act_split, i * 8 + (KT - 1 + k))
                    act_load(k, i * 8 + (KT + k))
                for k in range(KT):
                    act.wait_ge(act_used, i * 8 + (k + 1))
                    act.wait_ge(act_in[k % 2], i * 64 + (64 + 16 * (k // 2 + 1)))
                    nc.scalar.copy(a_hi[:, k, :], act_raw[k % 2][:, :]).then_inc(hi_copied, 1)
                    if k < KT - 2:
                        act.wait_ge(act_split, i * 8 + (8 + k + 1))
                        act_load(k, i * 8 + (8 + k + 2))
            meet(act, 8)
            for k in range(KT):
                nc.scalar.copy(a_hi[:, k, :], acc[:, k, :]).then_inc(hi_copied, 1)
            for i in range(2):
                act.wait_ge(diag_used, KT * (i + 1))
                nc.scalar.copy(row[i][:, :].rearrange("p (a b) -> p a b", a=2), ps[:, 2 * i:2 * i + 2, :])
            act.wait_ge(act_split, 4 * KT)
            meet(act, 9)
            for j in range(4):
                for t in range(NT):
                    act.wait_ge(merge_done, 8 * j + t + 1)
                    nc.scalar.copy(x_tm[:, t, j * WC:(j + 1) * WC], ps[:, t, 0:WC]).then_inc(merge_out, 1)
            norm_stats(1, x_tm, lambda t: act.wait_ge(merge_out, 25 + t), sq)
            for t in range(NT):
                act.wait_ge(x1_made, t + 1)
                act.dma_start(x1_d[t * P:(t + 1) * P, :], x_tm[:, t, :]).then_inc(x1_stored, 16)
            norm_stats(2, x_tm, lambda t: None, sq)
            meet(act, 10)
            norm_evac(1, 24)
            meet(act, 11)

            def hidden(n, c, extra=0, first=False):
                act.wait_ge(w_used[n % 2], n // 2 + 1 + extra)
                for j in range(4):
                    if not first:
                        act.wait_ge(u_split, c * 4 + (j - 3))
                    nc.scalar.activation(u_tmp[j][:, :], ps[:, j, :], ACT.Relu).then_inc(up_out, 1)
                    act.wait_ge(up_out, c * 4 + (j + 1))
                    nc.scalar.activation(u_tmp[j][:, :], u_tmp[j][:, :], ACT.Square).then_inc(u_squared, 1)

            hidden(N_MLP, 0, first=True)
            with act.Fori(0, NC // 2 - 1) as i:
                hidden(N_MLP + 1, i * 2 + 1, extra=i * 2)
                hidden(N_MLP + 3, i * 2 + 2, extra=i * 2)
            hidden(N_ALL - 3, NC - 1)
            norm_stats(3, x_tm, lambda t: act.wait_ge(down_out, 8 * (NC - 1) + t + 1), sq)
            meet(act, 12)

        @block.vector
        def _(dve):
            V = Count(dve, dve_own)
            ve = nc.vector

            def norm_roots(j):
                st = stat[:, 16 * j:16 * j + NT]
                rs = stat[:, 16 * j + 8:16 * j + 16]
                dve.wait_ge(squares, j + 1)
                ve.tensor_scalar(st, st, 1.0 / D, EPS, ALU.mult, ALU.add).then_inc(vars_ready, 1)
                dve.wait_ge(roots, j + 1)
                V.link(ve.reciprocal(rs, st))
                return rs

            def norm_scale(j):
                rs = norm_roots(j)
                for t in range(NT):
                    ve.tensor_scalar(x_tm[:, t, :], x_tm[:, t, :], rs[:, t:t + 1], None, ALU.mult).then_inc(normed, 1)

            def norm_split(j):
                for i in range(2 * KT):
                    g, k = divmod(i, KT)
                    dve.wait_ge(h_ready, 16 * j + i + 1)
                    r = slice(g * 512, g * 512 + 512)
                    V.link(ve.tensor_copy(a_hi[:, k, r], h_tmp[i % 4][:, :]))
                    ve.tensor_tensor(a_lo[:, k, r], h_tmp[i % 4][:, :], a_hi[:, k, r].bitcast(F32),
                                     ALU.subtract).then_inc(h_split, 1)

            norm_scale(0)
            dve.wait_ge(c_ready, 2)
            V.link(ve.tensor_tensor(mod[:, 0:16], mod[:, 0:16], vec_a[:, 0:16], ALU.add))
            V.link(ve.tensor_scalar(gain[:, 0:KT], mod[:, 8:16], 1.0, None, ALU.add))
            ve.tensor_tensor(gain[:, 0:KT], gain[:, 0:KT], vec_a[:, 56:64], ALU.mult).then_inc(gain_ready, 1)
            norm_split(0)
            meet(dve, 0)

            meet(dve, 1)
            dve.wait_ge(kv_sq, 1)
            V.link(ve.tensor_scalar(stat[:, 64:72], stat[:, 64:72], 1.0 / R, EPS, ALU.mult, ALU.add))
            ve.tensor_scalar(stat[:, 72:80], stat[:, 72:80], 1.0 / DI, EPS, ALU.mult, ALU.add).then_inc(kv_var, 1)
            dve.wait_ge(kv_root, 1)
            V.link(ve.reciprocal(stat[:, 80:96], stat[:, 64:80]))
            for t in range(NT):
                ve.scalar_tensor_tensor(ckv_tm[:, t, :], ps[:, t, 0:R], stat[:, 80 + t:81 + t], kv_row[:, :],
                                        ALU.mult, ALU.mult)
                for half in range(2):
                    ve.scalar_tensor_tensor(kidx_tm[:, t, half * DI:half * DI + DI], ps[:, t, R:R + DI],
                                            stat[:, 88 + t:89 + t], ki_row[:, :], ALU.mult, ALU.mult)
                ve.tensor_scalar(w_idx[:, t, :], ps[:, t, R + DI:R + DI + HI], HI ** -0.5, None, ALU.mult)
                ve.tensor_copy(dt[:, t, :], ps[:, t, R + DI + HI:R + NSM])
            meet(dve, 2)
            for r in range(2):
                dve.wait_ge(kv_out, r + 1)
                V.link(ve.tensor_copy(ckv_hi[:, r, :], sq0[:, :]))
                V.link(ve.tensor_tensor(ckv_lo[:, r, :], sq0[:, :], ckv_hi[:, r, :].bitcast(F32), ALU.subtract))
                dve.sem_inc(kv_out_split, 1)
            meet(dve, 3)
            i = 0
            for b in range(NT):
                for k0 in range(0, (b + 1) * P, 512):
                    n = min(512, (b + 1) * P - k0)
                    s = score[:, b, k0:k0 + n]
                    for h in range(HI):
                        dve.wait_ge(relu_done, i + 1)
                        r = relu_buf[:, i % 4, 0:n]
                        w = w_idx[:, b, h:h + 1]
                        if h:
                            dve.wait_ge(relu_used, i)
                            ins = ve.scalar_tensor_tensor(s, r, w, s, ALU.mult, ALU.add)
                        else:
                            ins = ve.tensor_scalar(s, r, w, None, ALU.mult)
                        ins.then_inc(relu_used, 1)
                        i += 1
            meet(dve, 4)

            ROUNDS = TOPK // 8
            for b in range(2):
                if b:
                    V.link(ve.memset(bias_bf[:, b, 0:b * P], 0.0))
                V.link(ve.tensor_copy(bias_bf[:, b, b * P:(b + 1) * P], future[:, :]))
            for b in range(2, NT):
                n = (b + 1) * P
                d = score[:, b, b * P:n]
                V.link(ve.tensor_tensor(d, d, future[:, :], ALU.add))
                with dve.Fori(0, ROUNDS) as i:
                    V.enter(i, 3)
                    V.link(ve.max(top8[:, :], score[:, b, 0:n]))
                    V.step()
                    V.link(ve.match_replace(score[:, b, 0:n], top8[:, :], score[:, b, 0:n], TAKEN))
                    V.leave(ROUNDS)
                V.link(ve.tensor_scalar(bias_bf[:, b, 0:n], score[:, b, 0:n], TAKEN, NEG, ALU.not_equal, ALU.mult))
            dve.wait_ge(mod_ready, 1)
            V.link(ve.tensor_tensor(mod[:, 16:48], mod[:, 16:48], vec_a[:, 16:48], ALU.add))
            V.link(ve.tensor_scalar(gain[:, KT:2 * KT], mod[:, 32:40], 1.0, None, ALU.add))
            V.link(ve.tensor_tensor(gain[:, KT:2 * KT], gain[:, KT:2 * KT], vec_a[:, 72:80], ALU.mult))
            V.link(ve.tensor_tensor(gate_cols[:, 0:KT], mod[:, 16:24], vec_a[:, 64:72], ALU.mult))
            V.link(ve.tensor_tensor(gate_cols[:, KT:2 * KT], mod[:, 40:48], vec_a[:, 80:88], ALU.mult))
            meet(dve, 5)

            STEPS = 2 * NT
            with dve.Fori(0, NH // 2) as i:
                V.enter(i, 3 * STEPS)
                for t in range(STEPS + 1):
                    if t < STEPS:
                        b = t % NT
                        n = (b + 1) * P
                        st = 4 * (t % 4)
                        dve.wait_ge(qk_done, i * STEPS + (t + 1))
                        s = ps[:, 2 * (t % 2):2 * (t % 2) + 2, :].rearrange("p a b -> p (a b)")[:, 0:n]
                        V.step()
                        V.link(ve.tensor_tensor_reduce(out=prob[t % 2][:, 0:n], in0=s, in1=bias_bf[:, b, 0:n], scale=1.0,
                                                       scalar=TAKEN, op0=ALU.add, op1=ALU.max,
                                                       accum_out=att_stat[:, st:st + 1]))
                        ve.tensor_scalar(att_stat[:, st + 1:st + 2], att_stat[:, st:st + 1], -SCALE, None, ALU.mult).then_inc(masked, 1)
                    if t >= 1:
                        b = (t - 1) % NT
                        n = (b + 1) * P
                        st = 4 * ((t - 1) % 4)
                        dve.wait_ge(exp_done, i * STEPS + t)
                        V.link(ve.reciprocal(att_stat[:, st + 3:st + 4], att_stat[:, st + 2:st + 3]))
                        ve.tensor_scalar(prob[(t - 1) % 2][:, 0:n], prob[(t - 1) % 2][:, 0:n], att_stat[:, st + 3:st + 4],
                                         None, ALU.mult).then_inc(p_ready, 1)
                V.leave(NH // 2)
            meet(dve, 6)

            rows8 = [P, NT, NS]

            def every_chunk(row):
                return row[:, :].rearrange("p (o h) -> p o h", o=1).broadcast_to(rows8)

            V.link(ve.tensor_tensor(dt[:, :, :], dt[:, :, :], every_chunk(dtb_row), ALU.add))
            ve.scalar_tensor_tensor(acum[:, :, :], dt[:, :, :], -1.0, dt[:, :, :], ALU.mult, ALU.max).then_inc(dt_abs, 1)
            dve.wait_ge(dt_exp, 2)
            ve.tensor_scalar(dte[:, :, :], ea[:, :, :], 1.0, None, ALU.add).then_inc(dt_plus, 1)
            dve.wait_ge(dt_plus, 1)
            V.link(ve.tensor_scalar(dta[:, :, :], dte[:, :, :], 1.0, None, ALU.is_equal))
            dve.wait_ge(dt_ln, 1)
            V.link(ve.tensor_tensor(dec[:, :, :], dec[:, :, :], dta[:, :, :], ALU.add))
            V.link(ve.scalar_tensor_tensor(dte[:, :, :], dte[:, :, :], -1.0, dta[:, :, :], ALU.add, ALU.add))
            V.link(ve.reciprocal(dte[:, :, :], dte[:, :, :]))
            V.link(ve.tensor_tensor(dec[:, :, :], dec[:, :, :], dte[:, :, :], ALU.mult))
            V.link(ve.tensor_tensor(dec[:, :, :], dec[:, :, :], ea[:, :, :], ALU.mult))
            V.link(ve.scalar_tensor_tensor(dt[:, :, :], dt[:, :, :], 0.0, dec[:, :, :], ALU.max, ALU.add))
            V.link(ve.tensor_scalar(alog_row[:, :], alog_row[:, :], -1.0, None, ALU.mult))
            ve.tensor_tensor(dta[:, :, :], dt[:, :, :], every_chunk(alog_row), ALU.mult).then_inc(dta_ready, 1)
            dve.wait_ge(aend_out, 3)
            V.link(ve.tensor_tensor(dte[:, :, :].rearrange("p c h -> p (c h)"), ps[:, 1, 0:NT * NS],
                                    acum[:, :, :].rearrange("p c h -> p (c h)"), ALU.subtract))
            dve.sem_inc(dte_ready, 1)
            for m in range(2):
                V.link(ve.memset(c_in[m][:, 0:TAPS - 1], 0.0))
            meet(dve, 7)
            with dve.Fori(0, NG) as g:
                V.enter(g, 6 * (TAPS - 1) + 7 * NT - 2)
                ve.tensor_copy(dta_g[:, :, :], dta[:, :, bass.ds(g * HG, HG)]).then_inc(dtag_ready, 1)
                for T in range(6):
                    dve.wait_ge(conv_in, g * 6 + (T + 1))
                    if T >= 2:
                        dve.wait_ge(silu_done, g * 6 + (T - 1)) if T < 4 else dve.wait_ge(tile_turned, g * 5 + (T - 2))
                    o = c_out[T % 2][:, :]
                    for j in range(TAPS):
                        col = (g + (24 * j + 16), g + (24 * j + 20))[T] if T < 2 else g * 4 + (24 * j + T - 2)
                        wj = vec_b[:, bass.ds(col, 1)]
                        src = c_in[T % 2][:, j:j + SEQ]
                        if j == 0:
                            V.link(ve.tensor_scalar(o, src, wj, None, ALU.mult))
                        elif j < TAPS - 1:
                            V.link(ve.scalar_tensor_tensor(o, src, wj, o, ALU.mult, ALU.add))
                        else:
                            ve.scalar_tensor_tensor(o, src, wj, o, ALU.mult, ALU.add).then_inc(conv_done, 1)

                def heads(t, k):
                    return t[:, k, bass.ds(g * HG, HG)]

                dve.wait_ge(tile_out, g * 5 + 5)

                def xs3(k):
                    return xs_tm[:, k, :].rearrange("p (h d) -> p h d", h=HG)

                def mix_in(k):
                    dve.wait_ge(seg_done, g * NT + (k + 1))
                    ve.tensor_tensor(decay[k % 2][:, :, :], ps[:, 2 * (k % 2):2 * (k % 2) + 2, :].rearrange("p a (b l) -> p (a b) l", l=P),
                                     spread(heads(acum, k), P), ALU.subtract).then_inc(seg_out, 1)
                    V.link(ve.tensor_tensor(xdt[k % 2][:, :, :], xs3(k), spread(heads(dt, k), PD), ALU.mult))
                    V.link(ve.tensor_tensor(xde[k % 2][:, :, :], xdt[k % 2][:, :, :], spread(heads(dte, k), PD), ALU.mult))
                    dve.wait_ge(decay_done, g * NT + (k + 1))
                    ve.tensor_tensor(decay[k % 2][:, :, :], decay[k % 2][:, :, :],
                                     cb_sb[:, :].rearrange("p (o l) -> p o l", o=1).broadcast_to([P, HG, P]), ALU.mult).then_inc(mix_ready, 1)

                def bank(b):
                    return ps[:, b, :].rearrange("p (h d) -> p h d", h=HG)

                mix_in(0)
                for k in range(NT):
                    dve.wait_ge(mix_done, g * NT + (k + 1))
                    if k == 0:
                        ve.tensor_copy(state[:, :, :], bank(6)).then_inc(state_ready, 1)
                    elif k < NT - 1:
                        V.link(ve.tensor_tensor(state[:, :, :], state[:, :, :], spread(heads(dec, k), PD), ALU.mult))
                        ve.tensor_tensor(state[:, :, :], state[:, :, :], bank(6), ALU.add).then_inc(state_ready, 1)
                    y = y_t[k % 2][:, :, :]
                    if k == 0:
                        V.link(ve.tensor_copy(y, bank(4)))
                    else:
                        V.link(ve.tensor_tensor(y, bank(5), spread(heads(ea, k), PD), ALU.mult))
                        V.link(ve.tensor_tensor(y, y, bank(4), ALU.add))
                    V.link(ve.tensor_tensor(xs3(k), xs3(k), spread(skip_row[:, bass.ds(g * HG, HG)], PD), ALU.mult))
                    V.link(ve.tensor_tensor(y, y, xs3(k), ALU.add))
                    z = zy[:, k, :].rearrange("p (h d) -> p h d", h=HG)
                    ve.tensor_tensor(z, z, y, ALU.mult).then_inc(y_ready, 1)
                    if k + 1 < NT:
                        mix_in(k + 1)
                dve.wait_ge(gn_squares, g * NT + NT)
                ve.tensor_scalar(stat[:, 96:104], stat[:, 96:104], 1.0 / DG, EPS, ALU.mult, ALU.add).then_inc(gn_var, 1)
                dve.wait_ge(gn_root, g + 1)
                V.link(ve.reciprocal(stat[:, 104:112], stat[:, 96:104]))
                for k in range(NT):
                    ve.tensor_scalar(zy[:, k, :], zy[:, k, :], stat[:, 104 + k:105 + k], None, ALU.mult).then_inc(gn_ready, 1)
                V.leave(NG)
                dve.drain().then_inc(group_end, 1)
                dve.wait_ge(group_end, g * 3 + 3)

            V.link(ve.memset(acc[:, :, :], 0.0))

            def act_lo(first, src=None):
                for k in range(KT):
                    dve.wait_ge(hi_copied, first + (k + 1))
                    raw_k = act_raw[k % 2][:, :] if src is None else src[:, k, :]
                    ve.tensor_tensor(a_lo[:, k, :], raw_k, a_hi[:, k, :].bitcast(F32), ALU.subtract).then_inc(act_split, 1)

            def gate_block(n, j, turn):
                dve.wait_ge(w_used[n % 2], turn * 2 + (n // 2 + 1))
                dve.wait_ge(gates_in[j % 2], turn * 32 + 16 * (j // 2 + 1))
                for b in range(4):
                    m, q = divmod(b, 2)
                    r = slice(q * 512, q * 512 + 512)
                    ve.tensor_tensor(gated[b % 2][:, :], ps[:, 4 * (j % 2) + b, :], gates[j % 2][:, m, r], ALU.mult).then_inc(gate_used, 1)
                    dve.wait_ge(gate_used, turn * 16 + (4 * j + b + 1))
                    V.link(ve.tensor_tensor(acc[:, 2 * j + m, r], acc[:, 2 * j + m, r], gated[b % 2][:, :], ALU.add))

            act_lo(0)
            with dve.Fori(0, 2) as i:
                V.enter(i, 16)
                for j in range(3):
                    gate_block(N_O + j, j, i)
                act_lo(i * 8 + 8)
                gate_block(N_O + 3, 3, i)
                V.leave(2)
            for j in range(4):
                gate_block(N_O + j, j, 2)
            meet(dve, 8)
            for i in range(2 * KT):
                if i >= 2:
                    dve.wait_ge(diag_used, i - 1)
                ve.tensor_scalar(diag[i % 2][:, :], ident[:, :], gate_cols[:, i:i + 1], None, ALU.mult).then_inc(diag_made, 1)
            act_lo(3 * KT, acc)
            meet(dve, 9)
            rs = norm_roots(1)
            for t in range(NT):
                V.link(ve.scalar_tensor_tensor(x_tm[:, t, :], x_tm[:, t, :], rs[:, t:t + 1], row[0][:, :], ALU.mult, ALU.mult))
                dve.wait_ge(res_in[t % 4], 16 * (t // 4 + 1))
                ve.tensor_tensor(x_tm[:, t, :], x_tm[:, t, :], x_in[t % 4][:, :], ALU.add).then_inc(x1_made, 1)
            dve.wait_ge(x1_stored, 16 * NT)
            norm_scale(2)
            meet(dve, 10)
            norm_split(1)
            V.link(ve.memset(x_tm[:, :, :], 0.0))
            meet(dve, 11)

            def u_part(c, b, j):
                m, q = divmod(j, 2)
                r = slice(q * 512, q * 512 + 512)
                dve.wait_ge(u_squared, c * 4 + (j + 1))
                V.link(ve.tensor_copy(u_hi[b][:, m, r], u_tmp[j][:, :]))
                ve.tensor_tensor(u_lo[b][:, m, r], u_tmp[j][:, :], u_hi[b][:, m, r].bitcast(F32), ALU.subtract).then_inc(u_split, 1)

            def add_down(c, t, first=False):
                dve.wait_ge(down_done, c * 8 + (t + 1))
                if not first:
                    dve.wait_ge(down_out, c * 8 + (t - 7))
                ve.tensor_tensor(x_tm[:, t, :].rearrange("p (a b) -> p a b", a=2), x_tm[:, t, :].rearrange("p (a b) -> p a b", a=2),
                                 ps[:, 4 + 2 * (t % 2):6 + 2 * (t % 2), :], ALU.add).then_inc(down_out, 1)

            def chunk(c, b, last=False, first=False, down_before=None):
                if down_before is not None:
                    dve.wait_ge(*down_before)
                for t in range(NT):
                    if t < 4 and not last:
                        u_part(c + 1, 1 - b, t)
                    add_down(c, t, first)

            for j in range(4):
                u_part(0, 0, j)
            chunk(0, 0, first=True)
            chunk(1, 1, down_before=(w_used[0], (N_MLP + 2) // 2 + 1))
            with dve.Fori(1, NC // 2 - 1) as i:
                V.enter(i - 1, 8)
                chunk(i * 2, 0, down_before=(w_used[0], i * 2 + (N_MLP // 2 + 1)))
                chunk(i * 2 + 1, 1, down_before=(w_used[0], i * 2 + (N_MLP // 2 + 2)))
                V.leave(NC // 2 - 2)
            chunk(NC - 2, 0, down_before=(w_used[0], (N_ALL - 4) // 2 + 1))
            chunk(NC - 1, 1, last=True)
            rs = norm_roots(3)
            meet(dve, 12)
            for t in range(NT):
                V.link(ve.scalar_tensor_tensor(x_tm[:, t, :], x_tm[:, t, :], rs[:, t:t + 1], row[1][:, :], ALU.mult, ALU.mult))
                dve.wait_ge(res_in[t % 4], 16 * (t // 4 + 3))
                ve.tensor_tensor(x_tm[:, t, :], x_tm[:, t, :], x_in[t % 4][:, :], ALU.add).then_inc(out_made, 1)


_INS = ['x', 'c', 'ada_w', 'ada_b', 'norm_g', 'w_in', 'kv_norm_g', 'kidx_norm_g', 'w_uk', 'w_uv', 'conv_w', 'conv_b',
        'dt_bias', 'a_log', 'd_skip', 'ssm_norm_g', 'w_o_att', 'w_o_ssd', 'w_out', 'w_up', 'w_down']
_OUTS = [((1, 1024, 1024), 'float32')]


def kernel(**inputs):
    import numpy as _np
    import concourse.bacc as _bacc
    from concourse import mybir as _mybir
    from concourse.bass_utils import run_bass_kernel_spmd as _run

    nc = _bacc.Bacc("TRN2", target_bir_lowering=False, num_devices=1)
    arrays, args = {}, []
    for name in _INS:
        a = _np.ascontiguousarray(inputs[name])
        arrays[f"in_{name}_dram"] = a
        args.append(nc.dram_tensor(f"in_{name}_dram", a.shape, _mybir.dt.from_np(a.dtype), kind="ExternalInput").ap())
    for i, (shape, dtype) in enumerate(_OUTS):
        dt = _mybir.dt.from_np(_np.dtype(dtype))
        args.append(nc.dram_tensor(f"out_{i}_dram", shape, dt, kind="ExternalOutput").ap())
    hybrid_block(nc, *args)
    r = _run(nc, [arrays], core_ids=[0])
    return r.results[0]["out_0_dram"]
```

```python
from contextlib import ExitStack

import concourse.bass as bass
from concourse import mybir

P = 128
F32 = mybir.dt.float32
F32R = mybir.dt.float32r
BF16 = mybir.dt.bfloat16
ALU = mybir.AluOpType
ACT = mybir.ActivationFunctionType
AX_X = mybir.AxisListType.X


class Count:

    def __init__(self, engine, sem):
        self.engine, self.sem, self.n, self.turn, self.per = engine, sem, 0, None, 0

    def add(self, ins):
        ins.then_inc(self.sem, 1)
        self.n += 1
        return ins

    def value(self):
        return self.n if self.turn is None else self.n + self.turn * self.per

    def wait(self):
        self.engine.wait_ge(self.sem, self.value())

    def link(self, ins):
        self.add(ins)
        self.wait()

    def step(self):
        self.engine.sem_inc(self.sem, 1)
        self.n += 1

    def enter(self, turn, per):
        self.turn, self.per, self.base = turn, per, self.n

    def leave(self, turns):
        assert self.n - self.base == self.per, (self.n - self.base, self.per)
        self.turn = None
        self.n = self.base + turns * self.per


def hybrid_block(nc, x, c, ada_w, ada_b, norm_g, w_in, kv_norm_g, kidx_norm_g, w_uk, w_uv, conv_w, conv_b,
                 dt_bias, a_log, d_skip, ssm_norm_g, w_o_att, w_o_ssd, w_out, w_up, w_down, out):
    SEQ, D = x.shape[1], x.shape[2]
    R = kv_norm_g.shape[1]
    DI = kidx_norm_g.shape[1]
    NH, HD = w_uk.shape[2], w_uk.shape[3]
    NS = dt_bias.shape[1]
    CD = conv_w.shape[2]
    DIN = ssm_norm_g.shape[1]
    DFF = w_up.shape[2]
    HI = 8
    NG = 4
    HG = NS // NG
    PD = DIN // NS
    DG = DIN // NG
    TAPS = conv_w.shape[1]
    TOPK = 256
    EPS = 1e-6
    SCALE = float(HD) ** -0.5
    KT = D // P
    NT = SEQ // P
    HALF = SEQ // 2
    WC = 256
    NEG = -1e30
    TAKEN = -3e38
    C_Q = 0
    C_KV = C_Q + NH * HD
    C_QI = C_KV + R
    C_KI = C_QI + HI * DI
    C_Z = C_KI + DI + HI
    C_X = C_Z + DIN
    C_B = C_X + DIN
    C_C = C_B + NG * P
    C_DT = C_X + CD
    C_GA = C_DT + NS
    C_GS = C_GA + D
    NSM = DI + HI + NS
    assert SEQ == D == 1024 and C_GS + D == w_in.shape[2] and HD == P and R == WC and 2 * DI == P
    assert DG == 4 * P and HG * PD == DG

    N_Q, N_UK, N_GS, N_SSM = 4, 8, 10, 14
    N_O = N_SSM + 6 * NG
    N_OUT = N_O + 12
    N_MLP = N_OUT + 4
    NC = DFF // WC
    N_ALL = N_MLP + 2 * NC

    at = [16512]

    def place(name, shape, dt, offset=None):
        size = 1
        for s in shape[1:]:
            size *= s
        size = (size * (2 if dt == BF16 else 4) + 31) // 32 * 32
        if offset is None:
            offset = at[0]
            at[0] += size
        assert offset + size <= 229344, (name, offset + size)
        return nc.alloc_sbuf_tensor_at(name, shape, dt, offset=offset)

    raw = [place(f"raw{s}", [P, KT * WC], F32) for s in range(2)]
    w_hi = [place(f"w_hi{s}", [P, KT * WC], F32R) for s in range(2)]
    w_lo = [place(f"w_lo{s}", [P, KT * WC], F32R) for s in range(2)]
    ACT_AT = at[0]
    a_hi = place("a_hi", [P, KT, SEQ], F32R)
    a_lo = place("a_lo", [P, KT, SEQ], F32R)
    R1 = at[0]
    x_tm = place("x_tm", [P, NT, D], F32)
    ident = place("ident", [P, P], F32)
    ident_bf = place("ident_bf", [P, P], BF16)
    ones = place("ones", [P, P], F32)
    tri = place("tri", [P, P], F32)
    future = place("future", [P, P], F32)
    past_bf = place("past_bf", [P, P], BF16)
    vec_a = place("vec_a", [P, 112], F32)
    vec_b = place("vec_b", [P, 112], F32)
    mod = place("mod", [P, 48], F32)
    gain = place("gain", [P, 2 * KT], F32)
    gate_cols = place("gate_cols", [P, 2 * KT], F32)
    c_act = place("c_act", [P, KT], F32)
    stat = place("stat", [P, 16 * KT], F32)
    kv_row = place("kv_row", [P, R], F32)
    ki_row = place("ki_row", [P, DI], F32)
    dtb_row = place("dtb_row", [P, NS], F32)
    alog_row = place("alog_row", [P, NS], F32)
    skip_row = place("skip_row", [P, NS], F32)
    w_idx = place("w_idx", [P, NT, HI], F32)
    att_stat = place("att_stat", [P, 16 * 4], F32)
    top8 = [place(f"top8_{i}", [P, 8], F32) for i in range(2)]
    R2 = at[0]
    K = 1024
    rows_a = place("rows_a", [112, P], F32, R2)
    rows_b = place("rows_b", [112, P], F32, R2 + 512)
    h_tmp = [place(f"h_tmp{i}", [P, 512], F32, R2 + (16 + 2 * i) * K) for i in range(4)]
    sq0 = place("sq0", [P, D], F32, R2 + 44 * K)
    ada0 = place("ada0", [P, KT, 2 * D], F32, ACT_AT)
    mod_row = place("mod_row", [1, 4 * D], F32, R2 + 24 * K)
    q_idx = place("q_idx", [P, 4, SEQ], F32, R2)
    ckv_hi = place("ckv_hi", [P, 2, SEQ], F32R, R2 + 16 * K)
    ckv_lo = place("ckv_lo", [P, 2, SEQ], F32R, R2 + 24 * K)
    ckv_tm = place("ckv_tm", [P, NT, R], F32, R2 + 32 * K)
    kidx_tm = place("kidx_tm", [P, NT, P], F32, R2 + 40 * K)
    relu_buf = place("relu_buf", [P, 4, 512], F32, R2 + 40 * K)
    k_idx_half = [place(f"k_idx_half{i}", [P, SEQ], F32, R2 + (48 + 4 * i) * K) for i in range(2)]
    score = place("score", [P, NT, SEQ], F32, R1)
    bias_bf = place("bias_bf", [P, NT, SEQ], BF16, R2)
    spill = [place(f"spill{i}", [P, SEQ], F32, R2 + (32 + 4 * i) * K) for i in range(4)]
    ada_raw = [place(f"ada_raw{i}", [P, KT, WC], F32, R2 + (16 + 8 * i) * K) for i in range(2)]
    DT0 = R2 + 51 * K
    dta = place("dta", [P, NT, NS], F32, DT0)
    acum = place("acum", [P, NT, NS], F32, DT0 + K)
    ea = place("ea", [P, NT, NS], F32, DT0 + 2 * K)
    dte = place("dte", [P, NT, NS], F32, DT0 + 3 * K)
    dec = place("dec", [P, NT, NS], F32, DT0 + 4 * K)
    dt = place("dt", [P, NT, NS], F32, DT0 + 5 * K)
    dta_g = place("dta_g", [P, NT, HG], F32, DT0 + 6 * K)
    hq = [place(f"hq{i}", [P, SEQ], F32, R2 + (16 + 12 * i) * K) for i in range(2)]
    hk = [place(f"hk{i}", [P, SEQ], F32, R2 + (20 + 12 * i) * K) for i in range(2)]
    hv = [place(f"hv{i}", [P, NT, P], F32, R2 + (24 + 12 * i) * K) for i in range(2)]
    prob = [place(f"prob{i}", [P, SEQ], F32, (R2 + 40 * K, R2 + 44 * K, R1 + 8 * K, R1 + 12 * K)[i]) for i in range(4)]
    att_o = [place(f"att_o{i}", [P, 512], F32, R2 + (48 + 2 * i) * K) for i in range(2)]
    probT = [place(f"probT{i}", [P, (NT // 2, NT)[i], 512], F32, R1 + 16 * i * K) for i in range(2)]
    xs_tm = place("xs_tm", [P, NT, DG], F32, R1)
    zy = place("zy", [P, NT, DG], F32, R1 + 16 * K)
    PADW = SEQ + 8
    c_in = [place(f"c_in{i}", [P, PADW], F32, R2 + 4128 * i) for i in range(2)]
    o = R2 + 2 * 4128
    c_out = [place(f"c_out{i}", [P, SEQ], F32, o + 4 * K * i) for i in range(2)]
    o += 8 * K
    b_fm = place("b_fm", [P, SEQ], F32, o)
    c_fm = place("c_fm", [P, SEQ], F32, o + 4 * K)
    b_tm = place("b_tm", [P, NT, P], F32, o + 8 * K)
    o += 12 * K
    decay = [place(f"decay{i}", [P, HG, P], F32, o + 4 * K * i) for i in range(2)]
    o += 8 * K
    xdt = [place(f"xdt{i}", [P, HG, PD], F32, o + 2 * K * i) for i in range(2)]
    xde = [place(f"xde{i}", [P, HG, PD], F32, o + 4 * K + 2 * K * i) for i in range(2)]
    o += 8 * K
    state = place("state", [P, HG, PD], F32, o)
    y_t = [place(f"y_t{i}", [P, HG, PD], F32, o + 2 * K + 2 * K * i) for i in range(2)]
    assert o + 6 * K + 512 <= DT0, (o + 6 * K, DT0)
    cb_sb = place("cb_sb", [P, P], F32, o + 6 * K)
    acc = place("acc", [P, KT, SEQ], F32, R1)
    act_raw = [place(f"act_raw{i}", [P, SEQ], F32, R2 + 4 * i * K) for i in range(2)]
    gates = [place(f"gates{i}", [P, 2, SEQ], F32, R2 + (8 + 8 * i) * K) for i in range(2)]
    gated = [place(f"gated{i}", [P, 512], F32, R2 + (24 + 2 * i) * K) for i in range(2)]
    row = [place(f"row{i}", [P, D], F32, R2 + (32 + 4 * i) * K) for i in range(2)]
    diag = [place(f"diag{i}", [P, P], F32, R2 + 40 * K + 512 * i) for i in range(2)]
    x_in = [place(f"x_in{i}", [P, D], F32, R2 + 4 * i * K) for i in range(4)]
    sq = place("sq", [P, D], F32, R2 + 50 * K)
    u_hi = [place(f"u_hi{i}", [P, 2, SEQ], F32R, R2 + 16 * i * K) for i in range(2)]
    u_lo = [place(f"u_lo{i}", [P, 2, SEQ], F32R, R2 + (8 + 16 * i) * K) for i in range(2)]
    u_tmp = [place(f"u_tmp{i}", [P, 512], F32, R2 + (40 + 2 * i) * K) for i in range(4)]

    q_d = nc.dram_tensor("q_d", (NH, P, SEQ), F32, kind="Internal").ap()
    k_d = nc.dram_tensor("k_d", (NH, P, SEQ), F32, kind="Internal").ap()
    v_d = nc.dram_tensor("v_d", (SEQ, NH * HD), F32, kind="Internal").ap()
    gate_d = nc.dram_tensor("gate_d", (2 * KT, P, SEQ), F32, kind="Internal").ap()
    acts_d = nc.dram_tensor("acts_d", (3 * KT, P, SEQ), F32, kind="Internal").ap()
    x1_d = nc.dram_tensor("x1_d", (SEQ, D), F32, kind="Internal").ap()

    ctx = ExitStack()
    with ctx:
        ps = ctx.enter_context(nc.psum_tensor("ps", [P, 8, 512], F32))

        def sem(name):
            return ctx.enter_context(nc.semaphore(name))

        raw_in = [sem(f"raw_in{s}") for s in range(2)]
        w_split = [sem(f"w_split{s}") for s in range(2)]
        w_used = [sem(f"w_used{s}") for s in range(2)]
        c_cols_in = sem("c_cols_in")
        hi_made = sem("hi_made")
        act_own, dve_own, pool_own = sem("act_own"), sem("dve_own"), sem("pool_own")
        met = sem("met")
        const_made = sem("const_made")
        small_in = sem("small_in")
        x_landed = [sem(f"x_landed{t}") for t in range(NT)]
        ada_in = [sem(f"ada_in{k}") for k in range(KT)]
        row_out = sem("row_out")
        vec_turned = sem("vec_turned")
        c_ready = sem("c_ready")
        mod0_done = sem("mod0_done")
        gain_ready = sem("gain_ready")
        squares = sem("squares")
        vars_ready = sem("vars_ready")
        roots = sem("roots")
        normed = sem("normed")
        turned = sem("turned")
        h_ready = sem("h_ready")
        h_split = sem("h_split")
        kv_sq, kv_var, kv_root, kv_turned, kv_out, kv_out_split = (
            sem(n) for n in ("kv_sq", "kv_var", "kv_root", "kv_turned", "kv_out", "kv_out_split"))
        qi_out = sem("qi_out")
        logit_done, relu_done, relu_used = sem("logit_done"), sem("relu_done"), sem("relu_used")
        weighted = sem("weighted")

        unit_done, unit_out = sem("unit_done"), sem("unit_out")
        spilled = [sem(f"spilled{i}") for i in range(4)]
        ada2_in = [sem(f"ada2_in{i}") for i in range(2)]
        ada2_used, mod_ready = sem("ada2_used"), sem("mod_ready")
        topk_step = sem("topk_step")
        head_in = [sem(f"head_in{i}") for i in range(2)]
        qk_done, masked, exp_done, p_ready = (sem(n) for n in ("qk_done", "masked", "exp_done", "p_ready"))
        pt_done, pt_out, pv_done, pv_out = (sem(n) for n in ("pt_done", "pt_out", "pv_done", "pv_out"))
        att_stored = [sem(f"att_stored{i}") for i in range(2)]
        dta_ready, acum_done, aend_out, dte_ready = (sem(n) for n in ("dta_ready", "acum_done", "aend_out", "dte_ready"))
        dt_abs, dt_exp, dt_plus, dt_ln = (sem(n) for n in ("dt_abs", "dt_exp", "dt_plus", "dt_ln"))
        conv_in, conv_done, silu_done, tile_turned, tile_out = (sem(n) for n in ("conv_in", "conv_done", "silu_done", "tile_turned", "tile_out"))
        z_done, z_out, ga_out = sem("z_done"), sem("z_out"), sem("ga_out")
        ga_stored = [sem(f"ga_stored{i}") for i in range(2)]
        dtag_ready, seg_done, decay_done, cb_out = (sem(n) for n in ("dtag_ready", "seg_done", "decay_done", "cb_out"))
        xs_dt, xs_dte, xs_skip = sem("xs_dt"), sem("xs_dte"), sem("xs_skip")
        mix_ready, mix_done, state_ready, y_ready = (sem(n) for n in ("mix_ready", "mix_done", "state_ready", "y_ready"))
        gn_squares, gn_var, gn_root, gn_ready, yt_done, yt_out = (
            sem(n) for n in ("gn_squares", "gn_var", "gn_root", "gn_ready", "yt_done", "yt_out"))
        y_stored = [sem(f"y_stored{i}") for i in range(2)]
        group_end = sem("group_end")
        act_in = [sem(f"act_in{i}") for i in range(2)]
        gates_in = [sem(f"gates_in{i}") for i in range(2)]
        hi_copied, act_split, act_used, gate_used = (sem(n) for n in ("hi_copied", "act_split", "act_used", "gate_used"))
        diag_made, diag_used, merge_done, merge_out = (sem(n) for n in ("diag_made", "diag_used", "merge_done", "merge_out"))
        res_in = [sem(f"res_in{i}") for i in range(4)]
        x1_made, x1_stored, out_made, out_stored = (sem(n) for n in ("x1_made", "x1_stored", "out_made", "out_stored"))
        up_out, u_squared, u_split, down_done, down_out = (sem(n) for n in ("up_out", "u_squared", "u_split", "down_done", "down_out"))

        block = ctx.enter_context(nc.Block())

        def key_chunks(b):
            return [(k0, min(512, (b + 1) * P - k0)) for k0 in range(0, (b + 1) * P, 512)]

        def spread(ap, n):
            return ap.rearrange("p (h o) -> p h o", o=1).broadcast_to([P, HG, n])

        SCORED = NT - 1

        def scores(e, b0, b1, first, add):
            i = HI * sum(len(key_chunks(b)) for b in range(b0))
            for b in range(b0, b1):
                for k0, n in key_chunks(b):
                    s = score[:, b, k0:k0 + n]
                    for h in range(HI):
                        e.wait_ge(relu_done, i + 1)
                        if i:
                            e.wait_ge(relu_used, i)
                        weigh = add if h else first
                        weigh(s, relu_buf[:, i % 4, 0:n], w_idx[:, b, h:h + 1]).then_inc(relu_used, 1)
                        i += 1

        def meet(e, i):
            e.drain().then_inc(met, 1)
            e.wait_ge(met, 3 * (i + 1))

        def cols(w, c0, n=WC):
            return w[:, bass.ds(c0, n)].rearrange("(k p) c -> p k c", p=P)

        STEPS = 2 * NT
        W3 = "p (k c) -> p k c"

        @block.sync
        def _(sp):
            def load(n, src, dst=None, turn=None, per=0):
                s = n % 2
                if n >= 2 or turn is not None:
                    sp.wait_ge(w_split[s], n // 2 + (0 if turn is None else turn * (per // 2)))
                dst = raw[s][:, :].rearrange(W3, c=WC) if dst is None else dst
                sp.dma_start(dst, src).then_inc(raw_in[s], 16)

            for t in range(NT):
                sp.dma_start(x_tm[:, t, :], x[0, t * P:(t + 1) * P, :]).then_inc(x_landed[t], 16)
            for k in range(KT):
                sp.dma_start(ada0[:, k, :], ada_w[0, k * P:(k + 1) * P, 0:2 * D]).then_inc(ada_in[k], 16)
            w = w_in[0]
            load(0, cols(w, C_KV))
            small_w = raw[1][:, 0:KT * NSM].rearrange(W3, c=NSM)
            sp.dma_start(small_w[:, :, 0:DI + HI], cols(w, C_KI, DI + HI)).then_inc(raw_in[1], 16)
            sp.dma_start(small_w[:, :, DI + HI:NSM], cols(w, C_DT, NS)).then_inc(raw_in[1], 16)
            load(2, cols(w, C_QI))
            load(3, cols(w, C_QI + WC))
            with sp.Fori(0, 2) as i:
                load(4, cols(w, C_Q + i * 2 * WC), turn=i, per=2)
                load(5, cols(w, C_Q + i * 2 * WC + WC), turn=i, per=2)
            for n, w_u in ((N_UK, w_uk), (N_UK + 1, w_uv)):
                load(n, w_u[0].rearrange("(k p) h d -> p k (h d)", p=P),
                     raw[n % 2][:, :].rearrange(W3, c=NH * HD))
            with sp.Fori(0, 2) as i:
                load(N_GS, cols(w, C_GS + i * 2 * WC), turn=i, per=2)
                load(N_GS + 1, cols(w, C_GS + i * 2 * WC + WC), turn=i, per=2)
            sp.wait_ge(unit_done, 2 * NH)
            for s in range(2):
                sp.dma_start(ada_raw[s][:, :, :], cols(ada_w[0], 2 * D + s * WC)).then_inc(ada2_in[s], 16)
            with sp.Fori(0, 7) as i:
                for s in range(2):
                    sp.wait_ge(ada2_used, 2 * i + s + 1)
                    sp.dma_start(ada_raw[s][:, :, :], cols(ada_w[0], (i * 2 + 2 + s) * WC + 2 * D)).then_inc(ada2_in[s], 16)
            for b in range(4):
                sp.wait_ge(spilled[b], 16 * 8)

            def load_head(h, p):
                def one(t):
                    return t[bass.ds(h, 1)].rearrange("a p s -> p (a s)")
                sp.dma_start(hq[p][:, :], one(q_d)).then_inc(head_in[p], 16)
                sp.dma_start(hk[p][:, :], one(k_d)).then_inc(head_in[p], 16)
                sp.dma_start(hv[p][:, :, :], v_d[:, bass.ds(h * P, P)].rearrange("(t p) d -> p t d", p=P)).then_inc(head_in[p], 16)

            sp.wait_ge(met, 3 * 6)
            for p in range(2):
                load_head(p, p)
            with sp.Fori(1, NH // 2) as i:
                for p in range(2):
                    sp.wait_ge(pv_done, 4 * i + (2 * p - 2))
                    load_head(i * 2 + p, p)
            with sp.Fori(0, NG) as g:
                def load_g(j, src):
                    n = N_SSM + j
                    sp.wait_ge(w_split[n % 2], g * 3 + n // 2)
                    return sp.dma_start(raw[n % 2][:, :].rearrange(W3, c=WC), src).then_inc(raw_in[n % 2], 16)

                bc = raw[0][:, :].rearrange(W3, c=WC)
                sp.wait_ge(w_split[0], g * 3 + N_SSM // 2)
                sp.dma_start(bc[:, :, 0:P], cols(w, g * P + C_B, P)).then_inc(raw_in[0], 16)
                sp.dma_start(bc[:, :, P:WC], cols(w, g * P + C_C, P)).then_inc(c_cols_in, 16)
                load_g(1, cols(w, g * DG + C_X))
                load_g(2, cols(w, g * DG + (C_X + WC)))
                load_g(3, cols(w, g * DG + C_Z))
                load_g(4, cols(w, g * DG + (C_Z + WC)))
                load_g(5, cols(w, g * WC + C_GA))

            def load_gates(j, tile, turn=None):
                v = 4 * (j - 1)
                if j >= 2 or turn is not None:
                    sp.wait_ge(gate_used, v if turn is None else turn * 16 + v)
                sp.dma_start(gates[j % 2][:, :, :], gate_d[bass.ds(tile, 2)].rearrange("a p s -> p a s")).then_inc(gates_in[j % 2], 16)

            for j in range(4):
                load(N_O + j, cols(w_o_att[0], j * WC))
                if j == 1:
                    sp.wait_ge(group_end, 3 * NG)
                    load_gates(0, 0)
                    load_gates(1, 2)
                elif j >= 2:
                    load_gates(j, 2 * j)
            with sp.Fori(0, 2) as i:
                rows_o = w_o_ssd[0][bass.ds(i * D, D), :]
                for j in range(4):
                    load(N_O + 4 + j, cols(rows_o, j * WC), turn=i, per=4)
                    load_gates(4 + j, KT + 2 * j, turn=i)
            for j in range(4):
                load(N_OUT + j, cols(w_out[0], j * WC))
            sp.wait_ge(met, 3 * 10)
            for t in range(NT):
                if t >= 4:
                    sp.wait_ge(x1_made, t - 3)
                sp.dma_start(x_in[t % 4][:, :], x[0, t * P:(t + 1) * P, :]).then_inc(res_in[t % 4], 16)

            def down(j):
                return w_down[0][bass.ds(j * WC, WC), :].rearrange("(k p) c -> p k c", p=P)

            def load_down(n, j, turn=None):
                load(n, down(j), raw[n % 2][:, :].rearrange(W3, c=D), turn=turn, per=4)

            load(N_MLP, cols(w_up[0], 0))
            with sp.Fori(0, NC // 2 - 1) as i:
                load(N_MLP + 1, cols(w_up[0], i * 2 * WC + WC), turn=i, per=4)
                load_down(N_MLP + 2, i * 2, turn=i)
                load(N_MLP + 3, cols(w_up[0], i * 2 * WC + 2 * WC), turn=i, per=4)
                load_down(N_MLP + 4, i * 2 + 1, turn=i)
            load(N_ALL - 3, cols(w_up[0], (NC - 1) * WC))
            load_down(N_ALL - 2, NC - 2)
            load_down(N_ALL - 1, NC - 1)
            sp.wait_ge(met, 3 * 13)
            for t in range(NT):
                if t >= 4:
                    sp.wait_ge(out_made, t - 3)
                sp.dma_start(x_in[t % 4][:, :], x1_d[t * P:(t + 1) * P, :]).then_inc(res_in[t % 4], 16)
            for t in range(NT):
                sp.wait_ge(out_made, t + 1)
                sp.dma_start(out[0, t * P:(t + 1) * P, :], x_tm[:, t, :]).then_inc(out_stored, 16)
            sp.wait_ge(out_stored, 16 * NT)

        @block.gpsimd
        def _(pool):
            nc.gpsimd.memset(ones[:, :], 1.0).then_inc(const_made, 1)
            nc.gpsimd.memset(ident[:, :], 0.0).then_inc(const_made, 1)
            nc.gpsimd.memset(future[:, :], 0.0).then_inc(const_made, 1)
            nc.gpsimd.memset(past_bf[:, :], 0.0).then_inc(const_made, 1)
            pool.wait_ge(const_made, 4)
            nc.gpsimd.affine_select(out=ident[:, :], in_=ident[:, :], compare_op=ALU.not_equal, fill=1.0,
                                    base=0, pattern=[[-1, P]], channel_multiplier=1).then_inc(const_made, 1)
            nc.gpsimd.affine_select(out=tri[:, :], in_=ones[:, :], compare_op=ALU.is_ge, fill=0.0,
                                    base=0, pattern=[[1, P]], channel_multiplier=-1).then_inc(const_made, 1)
            nc.gpsimd.affine_select(out=future[:, :], in_=future[:, :], compare_op=ALU.is_ge, fill=NEG,
                                    base=0, pattern=[[-1, P]], channel_multiplier=1).then_inc(const_made, 1)
            nc.gpsimd.affine_select(out=past_bf[:, :], in_=past_bf[:, :], compare_op=ALU.is_ge, fill=NEG,
                                    base=0, pattern=[[1, P]], channel_multiplier=-1).then_inc(const_made, 1)
            pool.wait_ge(const_made, 8)
            nc.gpsimd.tensor_copy(ident_bf[:, :], ident[:, :]).then_inc(const_made, 1)

            def split(n, width=KT * WC, turn=None, per=2, landed=16):
                s, v = n % 2, n // 2
                if turn is not None:
                    v = turn * (per // 2) + v
                pool.wait_ge(raw_in[s], v * 16 + (landed + (16 if n >= 2 and s == 1 else 0)))
                if n >= 2:
                    pool.wait_ge(w_used[s], v)
                pool.sem_inc(pool_own, 1)
                src, hi, lo = raw[s][:, 0:width], w_hi[s][:, 0:width], w_lo[s][:, 0:width]
                nc.gpsimd.tensor_copy(hi, src).then_inc(hi_made, 1)
                pool.wait_ge(hi_made, n + 1 if turn is None else turn * per + (n + 1))
                nc.gpsimd.tensor_tensor(lo, src, hi.bitcast(F32), ALU.subtract).then_inc(w_split[s], 1)

            split(0)
            split(1, width=KT * NSM, landed=32)
            with pool.Fori(0, 2) as i:
                split(2, turn=i)
                split(3, turn=i)

            weights = Count(pool, weighted)

            def weigh_add(s, r, w):
                weights.link(nc.gpsimd.tensor_scalar(r, r, w, None, ALU.mult))
                return nc.gpsimd.tensor_tensor(s, s, r, ALU.add)

            scores(pool, SCORED, NT, lambda s, r, w: nc.gpsimd.tensor_scalar(s, r, w, None, ALU.mult), weigh_add)
            with pool.Fori(2, (N_SSM - 2) // 2) as i:
                split(2, turn=i)
                split(3, turn=i)
            with pool.Fori(0, NG) as g:
                pool.wait_ge(c_cols_in, g * 16 + 16)
                for j in range(6):
                    split(N_SSM + j, turn=g, per=6)

                def heads(t, k):
                    return spread(t[:, k, bass.ds(g * HG, HG)], PD)

                pool.wait_ge(tile_out, g * 5 + 5)
                for k in range(NT):
                    if k >= 2:
                        pool.wait_ge(mix_done, g * NT + (k - 1))
                    pool.sem_inc(pool_own, 1)
                    xs_k = xs_tm[:, k, :].rearrange("p (h d) -> p h d", h=HG)
                    nc.gpsimd.tensor_tensor(xdt[k % 2][:, :, :], xs_k, heads(dt, k), ALU.mult).then_inc(xs_dt, 1)
                    pool.wait_ge(xs_dt, g * NT + (k + 1))
                    pool.sem_inc(pool_own, 1)
                    nc.gpsimd.tensor_tensor(xde[k % 2][:, :, :], xdt[k % 2][:, :, :], heads(dte, k), ALU.mult).then_inc(xs_dte, 1)
                    nc.gpsimd.tensor_tensor(xs_k, xs_k, spread(skip_row[:, bass.ds(g * HG, HG)], PD), ALU.mult).then_inc(xs_skip, 1)
            with pool.Fori(0, (N_ALL - N_O) // 2) as i:
                split(N_O, turn=i)
                split(N_O + 1, turn=i)
            pool.wait_ge(pool_own, N_ALL + NG * NT * 2)

        @block.tensor
        def _(pe):
            def w_tile(t, s, k, c0, c1, width=WC):
                return t[s][:, k * width + c0:k * width + c1]

            def w_wait(n, extra=0):
                pe.wait_ge(w_split[n % 2], n // 2 + 1 + extra)

            def mm(o, a, b, start=False, stop=False):
                return nc.tensor.matmul(o, a, b, start=start, stop=stop)

            def fm_block(n, group, extra=0, act_ready=None, act_used=None):
                s = n % 2
                w_wait(n, extra)
                for k in range(KT):
                    if act_ready is not None:
                        act_ready(k)
                    for m in range(2):
                        wh = w_tile(w_hi, s, k, m * P, m * P + P)
                        wl = w_tile(w_lo, s, k, m * P, m * P + P)
                        for q in range(2):
                            o = ps[:, 4 * group + 2 * m + q, :]
                            r = slice(q * 512, q * 512 + 512)
                            mm(o, wh, a_hi[:, k, r], start=(k == 0))
                            mm(o, wh, a_lo[:, k, r])
                        for q in range(2):
                            last = mm(ps[:, 4 * group + 2 * m + q, :], wl, a_hi[:, k, q * 512:q * 512 + 512],
                                      stop=(k == KT - 1))
                    if act_used is not None:
                        last = act_used(k, last)
                return last

            def tm_token(n, t, o, width, stationary=None, nk=KT, c0=0, wwidth=None):
                s = n % 2
                sh, sl = stationary or (a_hi, a_lo)
                ww = wwidth or width
                for k in range(nk):
                    r = slice(t * P, t * P + P)
                    wh, wl = (w_tile(w, s, k, c0, c0 + width, ww) for w in (w_hi, w_lo))
                    mm(o, sh[:, k, r], wh, start=(k == 0))
                    mm(o, sh[:, k, r], wl)
                    last = mm(o, sl[:, k, r], wh, stop=(k == nk - 1))
                return last

            def norm_turn(j):
                for i in range(2 * KT):
                    g, k = divmod(i, KT)
                    pe.wait_ge(normed, 8 * j + 4 * (g + 1))
                    if i >= 4:
                        pe.wait_ge(h_ready, 16 * j + i - 3)
                    for t in range(4):
                        last = nc.tensor.transpose(ps[:, 4 + i % 4, t * P:(t + 1) * P],
                                                   x_tm[:, 4 * g + t, k * P:(k + 1) * P], ident[:, :])
                    last.then_inc(turned, 1)

            pe.wait_ge(const_made, 9)
            pe.wait_ge(small_in, 16 * 11)
            nc.tensor.transpose(ps[:, 0, 0:112], rows_a[:, :], ident[0:112, 0:112])
            nc.tensor.transpose(ps[:, 1, 0:112], rows_b[:, :], ident[0:112, 0:112]).then_inc(vec_turned, 1)
            pe.wait_ge(c_ready, 1)
            for k in range(KT):
                pe.wait_ge(ada_in[k], 16)
                for q in range(4):
                    last = mm(ps[0:1, q, :], c_act[:, k:k + 1], ada0[:, k, q * 512:q * 512 + 512],
                              start=(k == 0), stop=(k == KT - 1))
            last.then_inc(mod0_done, 1)
            pe.wait_ge(row_out, 1)
            for m in range(2 * KT):
                last = mm(ps[:, 4, m:m + 1], mod_row[0:1, m * P:(m + 1) * P], ones[0:1, 0:1], start=True, stop=True)
            last.then_inc(mod0_done, 1)
            pe.wait_ge(c_ready, 2)
            norm_turn(0)
            meet(pe, 0)

            w_wait(0)
            for t in range(NT):
                last = tm_token(0, t, ps[:, t, 0:R], R)
            last.then_inc(w_used[0], 1)
            w_wait(1)
            for t in range(NT):
                last = tm_token(1, t, ps[:, t, R:R + NSM], NSM)
            last.then_inc(w_used[1], 1)
            meet(pe, 1)
            meet(pe, 2)
            for b in range(2):
                fm_block(2 + b, b).then_inc(w_used[b], 1)
            pe.wait_ge(qi_out, 4)
            for g in range(2):
                for t in range(4):
                    last = nc.tensor.transpose(ps[:, g, t * P:(t + 1) * P], kidx_tm[:, 4 * g + t, :], ident[:, :])
            for r in range(2):
                for g in range(2):
                    for t in range(4):
                        last = nc.tensor.transpose(ps[:, 2 + 2 * r + g, t * P:(t + 1) * P],
                                                   ckv_tm[:, 4 * g + t, r * P:(r + 1) * P], ident[:, :])
            last.then_inc(kv_turned, 1)
            meet(pe, 3)
            i = 0
            for b in range(NT):
                for k0 in range(0, (b + 1) * P, 512):
                    n = min(512, (b + 1) * P - k0)
                    for h in range(HI):
                        if i >= 4:
                            pe.wait_ge(relu_done, i - 3)
                        mm(ps[:, i % 4, 0:n], q_idx[:, h // 2, b * P:(b + 1) * P], k_idx_half[h % 2][:, k0:k0 + n],
                           start=True, stop=True).then_inc(logit_done, 1)
                        i += 1
            meet(pe, 4)

            def fm_unit_blocks(n, u, turns):
                with pe.Fori(0, turns) as i:
                    for j in range(2):
                        first = u + 2 * j
                        pe.wait_ge(unit_out, i * 4 + (first - 2) if first >= 2 else i * 4)
                        fm_block(n + j, (first % 4) // 2, extra=i).then_inc(w_used[(n + j) % 2], 1)

            fm_block(4, 0).then_inc(w_used[0], 1)
            fm_block(5, 1).then_inc(w_used[1], 1)
            pe.wait_ge(unit_out, 2)
            fm_block(6, 0).then_inc(w_used[0], 1)
            pe.wait_ge(unit_out, 4)
            fm_block(7, 1).then_inc(w_used[1], 1)
            u = 8
            s = N_UK % 2
            w_wait(N_UK)
            for h in range(NH):
                pe.wait_ge(unit_out, u - 3)
                for q in range(2):
                    o = ps[:, 2 * (u % 4) + q, :]
                    r = slice(q * 512, q * 512 + 512)
                    for k in range(2):
                        wh, wl = (w_tile(t, s, k, h * P, h * P + P, NH * HD) for t in (w_hi, w_lo))
                        mm(o, wh, ckv_hi[:, k, r], start=(k == 0))
                        mm(o, wh, ckv_lo[:, k, r])
                        last = mm(o, wl, ckv_hi[:, k, r], stop=(k == 1))
                last.then_inc(unit_done, 1)
                u += 1
            w_wait(N_UK + 1)
            for t in range(NT):
                pe.wait_ge(unit_out, u - 3)
                for q in range(2):
                    last = tm_token(N_UK + 1, t, ps[:, 2 * (u % 4) + q, :], 512, (ckv_hi, ckv_lo), 2, q * 512, NH * HD)
                last.then_inc(unit_done, 1)
                u += 1
            pe.drain().then_inc(w_used[0], 1)
            pe.drain().then_inc(w_used[1], 1)
            fm_unit_blocks(N_GS, u, 2)
            pe.wait_ge(unit_out, 32)
            with pe.Fori(0, 8) as i:
                for s in range(2):
                    pe.wait_ge(ada2_in[s], i * 16 + 16)
                    for k in range(KT):
                        last = mm(ps[0:1, bass.ds(i, 1), s * WC:s * WC + WC], c_act[:, k:k + 1], ada_raw[s][:, k, :],
                                  start=(k == 0), stop=(k == KT - 1))
                    last.then_inc(ada2_used, 1)
            pe.wait_ge(row_out, 2)
            for m in range(4 * KT):
                last = mm(ps[:, 0, m:m + 1], mod_row[0:1, m * P:(m + 1) * P], ones[0:1, 0:1], start=True, stop=True)
            last.then_inc(mod0_done, 1)
            meet(pe, 5)

            def attend(i, positions, turns, last=False):
                for t in positions:
                    if t < STEPS or not last:
                        p, b = t // NT % 2, t % NT
                        if b == 0:
                            pe.wait_ge(head_in[p], i * 48 + 48 * (1 + t // STEPS))
                        if t >= 2:
                            pe.wait_ge(masked, i * STEPS + (t - 1))
                        for j, (k0, n) in enumerate(key_chunks(b)):
                            ins = mm(ps[:, 2 * (t % 2) + j, 0:n], hq[p][:, b * P:(b + 1) * P], hk[p][:, k0:k0 + n],
                                     start=True, stop=True)
                        ins.then_inc(qk_done, 1)
                    if t >= 6 and (t - 3) % 4 == 3:
                        g = (t - 3) // 4
                        p, half = divmod(g, 2)
                        pe.wait_ge(pt_out, i * 24 + 12 * p + (4, 12)[half])
                        if g >= 2:
                            pe.wait_ge(pv_out, i * 4 + (g - 1))
                        nk = 4 * half + 4
                        for k in range(nk):
                            q0 = max(0, k - 4 * half) * P
                            ins = mm(ps[:, 6 + g % 2, q0:512], hv[p][:, k, :], probT[g % 2][:, k, q0:512],
                                     start=(k == 0), stop=(k == nk - 1))
                        ins.then_inc(pv_done, 1)
                    if t >= 2 and (t < STEPS + 2 or not last):
                        b = (t - 2) % NT
                        pe.wait_ge(p_ready, i * STEPS + (t - 1))
                        for k in range(b + 1):
                            if k % 4 == 0 and turns >= 2:
                                pe.wait_ge(pt_out, i * 24 + (turns - 1))
                            ins = nc.tensor.transpose(ps[:, 4 + turns % 2, (k % 4) * P:(k % 4 + 1) * P],
                                                      prob[(t - 2) % 4][:, k * P:(k + 1) * P], ident[:, :])
                            if k % 4 == 3 or k == b:
                                ins.then_inc(pt_done, 1)
                                turns += 1

            attend(0, range(3), 0)
            with pe.Fori(0, NH // 2 - 1) as i:
                attend(i, range(3, STEPS + 3), 1)
            attend(NH // 2 - 1, range(3, STEPS + 3), 1, last=True)
            meet(pe, 6)

            pe.wait_ge(dta_ready, 1)
            flat = "p c h -> p (c h)"
            mm(ps[:, 0, 0:NT * NS], tri[:, :], dta[:, :, :].rearrange(flat), start=True, stop=True)
            mm(ps[:, 1, 0:NT * NS], ones[:, :], dta[:, :, :].rearrange(flat), start=True, stop=True).then_inc(acum_done, 1)
            meet(pe, 7)
            with pe.Fori(0, NG) as g:
                def turn_tile(r, src):
                    pe.wait_ge(silu_done, g * 6 + (1, 3, 4, 5, 6)[r])
                    if r >= 2:
                        pe.wait_ge(tile_out, g * 5 + (r - 1))
                    for t in range(NT):
                        last = nc.tensor.transpose(ps[:, 2 * (r % 2) + t // 4, (t % 4) * P:(t % 4 + 1) * P],
                                                   src[:, t * P:(t + 1) * P], ident[:, :])
                    last.then_inc(tile_turned, 1)

                def z_block(j):
                    n = N_SSM + 3 + j
                    w_wait(n, g * 3)
                    for t in range(NT):
                        v = NT * j + t
                        if v >= 4:
                            pe.wait_ge(z_out, g * 16 + (v - 3))
                        last = tm_token(n, t, ps[:, 4 + v % 4, 0:WC], WC)
                        last.then_inc(z_done, 1)
                    pe.drain().then_inc(w_used[n % 2], 1)

                fm_block(N_SSM, 0, extra=g * 3).then_inc(w_used[0], 1)
                fm_block(N_SSM + 1, 1, extra=g * 3).then_inc(w_used[1], 1)
                pe.wait_ge(conv_in, g * 6 + 2)
                fm_block(N_SSM + 2, 0, extra=g * 3).then_inc(w_used[0], 1)
                pe.wait_ge(conv_in, g * 6 + 4)
                z_block(0)
                pe.wait_ge(conv_in, g * 6 + 6)
                turn_tile(0, b_fm)
                turn_tile(1, c_out[0])
                turn_tile(2, c_out[1])
                z_block(1)
                turn_tile(3, c_out[0])
                turn_tile(4, c_out[1])
                pe.wait_ge(tile_out, g * 5 + 5)
                pe.wait_ge(dtag_ready, g + 1)

                def segments(k):
                    if k >= 1:
                        pe.wait_ge(cb_out, g * NT + k)
                    r = slice(k * P, k * P + P)
                    mm(ps[:, 7, 0:P], b_fm[:, r], c_fm[:, r], start=True, stop=True)
                    if k >= 1:
                        pe.wait_ge(decay_done, g * NT + k)
                    for j in range(2):
                        o = ps[:, j, :]
                        mm(o.rearrange("p (h l) -> p h l", h=4), ident_bf[:, :],
                           past_bf[:, :].rearrange("p (o l) -> p o l", o=1).broadcast_to([P, 4, P]), start=True)
                        for h in range(4):
                            last = mm(o[:, h * P:(h + 1) * P],
                                      dta_g[:, k, 4 * j + h:4 * j + h + 1].broadcast_to([P, P]), tri[:, :], stop=(h == 3))
                    last.then_inc(seg_done, 1)

                segments(0)
                segments(1)
                for k in range(NT):
                    pe.wait_ge(mix_ready, g * NT + (k + 1))
                    pe.wait_ge(xs_dte, g * NT + (k + 1))
                    if k >= 2:
                        pe.wait_ge(y_ready, g * NT + (k - 1))
                    for h in range(HG):
                        mm(ps[:, 2 + 2 * (k % 2), h * PD:(h + 1) * PD], decay[k % 2][:, h, :], xdt[k % 2][:, h, :], start=True, stop=True)
                    if k >= 1:
                        pe.wait_ge(state_ready, g * 7 + k)
                        mm(ps[:, 3 + 2 * (k % 2), :], c_fm[:, k * P:(k + 1) * P], state[:, :, :].rearrange("p h d -> p (h d)"),
                           start=True, stop=True)
                    mm(ps[:, 6, :], b_tm[:, k, :], xde[k % 2][:, :, :].rearrange("p h d -> p (h d)"),
                       start=True, stop=True).then_inc(mix_done, 1)
                    if k + 2 < NT:
                        segments(k + 2)
                pe.wait_ge(y_ready, g * NT + NT - 1)
                fm_block(N_SSM + 5, 0, extra=g * 3).then_inc(w_used[1], 1)
                pe.wait_ge(y_ready, g * NT + NT)
                for f in range(4):
                    if f == 0:
                        pe.wait_ge(gn_ready, g * NT + NT)
                    if f >= 2:
                        pe.wait_ge(yt_out, g * 4 + (f - 1))
                    for t in range(NT):
                        last = nc.tensor.transpose(ps[:, 4 + 2 * (f % 2) + t // 4, (t % 4) * P:(t % 4 + 1) * P],
                                                   zy[:, t, f * P:(f + 1) * P], ident[:, :])
                    last.then_inc(yt_done, 1)
                pe.drain().then_inc(group_end, 1)
                pe.wait_ge(group_end, g * 3 + 3)

            def out_block(n, j, o, turn=None):
                def at_turn(v, per):
                    return v if turn is None else turn * per + v
                v = 4 * (4 * o + j - 1)
                if 4 * o + j >= 2:
                    pe.wait_ge(gate_used, at_turn(v, 16))
                ready = (lambda k: pe.wait_ge(act_split, at_turn(8 * o + k + 1, 8))) if j == 0 else None
                used = (lambda k, ins: ins.then_inc(act_used, 1)) if j == 3 else None
                last = fm_block(n, j % 2, extra=0 if turn is None else turn * 2, act_ready=ready, act_used=used)
                if j == 3:
                    pe.drain().then_inc(w_used[n % 2], 1)
                else:
                    last.then_inc(w_used[n % 2], 1)

            for j in range(4):
                out_block(N_O + j, j, 0)
            with pe.Fori(0, 2) as i:
                for j in range(4):
                    out_block(N_O + 4 + j, j, 1, turn=i)
            meet(pe, 8)
            for i in range(2 * KT):
                pe.wait_ge(diag_made, i + 1)
                mm(ps[:, i // 4, (i % 4) * P:(i % 4 + 1) * P], ones[:, :], diag[i % 2][:, :],
                   start=True, stop=True).then_inc(diag_used, 1)
            meet(pe, 9)
            pe.wait_ge(act_split, 4 * KT)
            for j in range(4):
                n = N_OUT + j
                w_wait(n)
                for t in range(NT):
                    if j:
                        pe.wait_ge(merge_out, 8 * j + t - 7)
                    last = tm_token(n, t, ps[:, t, 0:WC], WC)
                    last.then_inc(merge_done, 1)
                pe.drain().then_inc(w_used[n % 2], 1)
            meet(pe, 10)
            norm_turn(1)
            meet(pe, 11)

            def up(n, c, extra=0):
                if c is not None:
                    pe.wait_ge(up_out, c * 4)
                fm_block(n, 0, extra=extra).then_inc(w_used[n % 2], 1)

            def down(n, c, b, extra=0, first=False):
                w_wait(n, extra)
                pe.wait_ge(u_split, c * 4 + 4)
                for t in range(NT):
                    if t >= 2 or not first:
                        pe.wait_ge(down_out, c * 8 + (t - 1))
                    for q in range(2):
                        last = tm_token(n, t, ps[:, 4 + 2 * (t % 2) + q, :], 512, (u_hi[b], u_lo[b]), 2, q * 512, D)
                    last.then_inc(down_done, 1)
                pe.drain().then_inc(w_used[n % 2], 1)

            up(N_MLP, None)
            up(N_MLP + 1, 1)
            down(N_MLP + 2, 0, 0, first=True)
            up(N_MLP + 3, 2)
            down(N_MLP + 4, 1, 1)
            with pe.Fori(1, NC // 2 - 1) as i:
                up(N_MLP + 1, i * 2 + 1, extra=i * 2)
                down(N_MLP + 2, i * 2, 0, extra=i * 2)
                up(N_MLP + 3, i * 2 + 2, extra=i * 2)
                down(N_MLP + 4, i * 2 + 1, 1, extra=i * 2)
            up(N_ALL - 3, NC - 1)
            down(N_ALL - 2, NC - 2, 0)
            down(N_ALL - 1, NC - 1, 1)
            meet(pe, 12)

        @block.scalar
        def _(act):
            A = Count(act, act_own)

            def norm_stats(j, src, wait, sq):
                for t in range(NT):
                    wait(t)
                    ins = nc.scalar.activation(sq[:, :], src[:, t, :], ACT.Square, accum_out=stat[:, 16 * j + t:16 * j + t + 1])
                    A.link(ins)
                act.sem_inc(squares, 1)
                act.wait_ge(vars_ready, j + 1)
                nc.scalar.activation(stat[:, 16 * j:16 * j + NT], stat[:, 16 * j:16 * j + NT], ACT.Sqrt).then_inc(roots, 1)

            def norm_evac(j, shift):
                for i in range(2 * KT):
                    k = i % KT
                    act.wait_ge(turned, 16 * j + i + 1)
                    if i >= 4:
                        act.wait_ge(h_split, 16 * j + i - 3)
                    if i == 0 and j == 0:
                        act.wait_ge(gain_ready, 1)
                    nc.scalar.activation(h_tmp[i % 4][:, :], ps[:, 4 + i % 4, :], ACT.Identity,
                                         bias=mod[:, shift + k:shift + k + 1],
                                         scale=gain[:, j * KT + k:j * KT + k + 1]).then_inc(h_ready, 1)

            def rows(t, n):
                return t.rearrange("(a p) -> a p", p=P)

            act.dma_start(rows_a[0:48, :], rows(ada_b[0], 48)).then_inc(small_in, 16)
            act.dma_start(rows_a[48:56, :], rows(c[0], 8)).then_inc(small_in, 16)
            act.dma_start(rows_a[56:88, :], norm_g[0].rearrange("j (a p) -> (j a) p", p=P)).then_inc(small_in, 16)
            act.dma_start(rows_a[88:112, :], rows(conv_b[0], 24)).then_inc(small_in, 16)
            act.dma_start(rows_b[0:96, :], conv_w[0].rearrange("j (a p) -> (j a) p", p=P)).then_inc(small_in, 16)
            act.dma_start(rows_b[96:112, :], rows(ssm_norm_g[0], 16)).then_inc(small_in, 16)
            for dst, src, n in ((kv_row, kv_norm_g, R), (ki_row, kidx_norm_g, DI), (dtb_row, dt_bias, NS),
                                (alog_row, a_log, NS), (skip_row, d_skip, NS)):
                act.dma_start(dst[:, :], src[0:1, :].broadcast_to([P, n])).then_inc(small_in, 16)
            act.wait_ge(vec_turned, 1)
            A.add(nc.scalar.copy(vec_a[:, :], ps[:, 0, 0:112]))
            A.link(nc.scalar.copy(vec_b[:, :], ps[:, 1, 0:112]))
            nc.scalar.activation(c_act[:, :], vec_a[:, 48:56], ACT.Silu).then_inc(c_ready, 1)
            norm_stats(0, x_tm, lambda t: act.wait_ge(x_landed[t], 16), sq0)
            act.wait_ge(mod0_done, 1)
            nc.scalar.copy(mod_row[0:1, 0:2 * D].rearrange("p (a b) -> p a b", a=4), ps[0:1, 0:4, :]).then_inc(row_out, 1)
            act.wait_ge(mod0_done, 2)
            nc.scalar.copy(mod[:, 0:16], ps[:, 4, 0:16]).then_inc(c_ready, 1)
            norm_evac(0, 0)
            meet(act, 0)

            meet(act, 1)
            for t in range(NT):
                A.link(nc.scalar.activation(sq0[:, 0:R], ps[:, t, 0:R], ACT.Square, accum_out=stat[:, 64 + t:65 + t]))
                A.link(nc.scalar.activation(sq0[:, 0:DI], ps[:, t, R:R + DI], ACT.Square, accum_out=stat[:, 72 + t:73 + t]))
            act.sem_inc(kv_sq, 1)
            act.wait_ge(kv_var, 1)
            nc.scalar.activation(stat[:, 64:80], stat[:, 64:80], ACT.Sqrt).then_inc(kv_root, 1)
            meet(act, 2)
            for b in range(2):
                act.wait_ge(w_used[b], 2)
                for m in range(2):
                    nc.scalar.copy(q_idx[:, 2 * b + m, :].rearrange("p (a b) -> p a b", a=2),
                                   ps[:, 4 * b + 2 * m:4 * b + 2 * m + 2, :]).then_inc(qi_out, 1)
            act.wait_ge(kv_turned, 1)
            for i in range(2):
                half = slice(DI * i, DI * i + DI)
                nc.scalar.copy(k_idx_half[i][half, :].rearrange("p (a b) -> p a b", a=2), ps[half, 0:2, :])
            for r in range(2):
                nc.scalar.copy(sq0[:, :].rearrange("p (a b) -> p a b", a=2), ps[:, 2 + 2 * r:4 + 2 * r, :]).then_inc(kv_out, 1)
                act.wait_ge(kv_out_split, r + 1)
            meet(act, 3)
            i = 0
            for b in range(NT):
                for k0 in range(0, (b + 1) * P, 512):
                    n = min(512, (b + 1) * P - k0)
                    for h in range(HI):
                        act.wait_ge(logit_done, i + 1)
                        if i >= 4:
                            act.wait_ge(relu_used, i - 3)
                        nc.scalar.activation(relu_buf[:, i % 4, 0:n], ps[:, i % 4, 0:n], ACT.Relu).then_inc(relu_done, 1)
                        i += 1
            meet(act, 4)

            def unit(u, func, dst, turn=None, per=0):
                b = u % 4
                if u >= 4 or turn is not None:
                    act.wait_ge(spilled[b], 16 * (u // 4) + (0 if turn is None else turn * (4 * per)))
                nc.scalar.activation(spill[b][:, :].rearrange("p (a b) -> p a b", a=2),
                                     ps[:, 2 * b:2 * b + 2, :], func).then_inc(unit_out, 1)
                act.wait_ge(unit_out, u + 1 + (0 if turn is None else turn * per))
                act.dma_start(dst, spill[b][:, :]).then_inc(spilled[b], 16)

            def fm_units(n, u, func, dst, turns):
                with act.Fori(0, turns) as i:
                    for j in range(4):
                        if j % 2 == 0:
                            act.wait_ge(w_used[(n + j // 2) % 2], (n + j // 2) // 2 + 1 + i)
                        unit(u + j, func, dst(i, j), turn=i, per=4)

            act.wait_ge(relu_used, HI * sum(len(key_chunks(b)) for b in range(NT)))
            for j in range(8):
                if j % 2 == 0:
                    act.wait_ge(w_used[(j // 2) % 2], 3 + j // 4)
                unit(j, ACT.Copy, q_d[j])
            for u in range(8, 24):
                act.wait_ge(unit_done, u - 7)
                unit(u, ACT.Copy, k_d[u - 8] if u < 16 else v_d[(u - 16) * P:(u - 15) * P, :])
            fm_units(N_GS, 24, ACT.Sigmoid, lambda i, j: gate_d[bass.ds(i * 4 + (KT + j), 1)].rearrange("a p s -> p (a s)"), 2)
            act.wait_ge(ada2_used, 16)
            for b in range(4):
                act.wait_ge(spilled[b], 16 * 8)
            nc.scalar.copy(mod_row[0:1, :].rearrange("p (a b) -> p a b", a=8), ps[0:1, :, :]).then_inc(row_out, 1)
            act.wait_ge(mod0_done, 3)
            nc.scalar.copy(mod[:, 16:48], ps[:, 0, 0:32]).then_inc(mod_ready, 1)
            meet(act, 5)

            def attend(i, positions, turns, last=False):
                for t in positions:
                    if t < STEPS or not last:
                        n = (t % NT + 1) * P
                        act.wait_ge(masked, i * STEPS + (t + 1))
                        st = 4 * (t % 4)
                        nc.scalar.activation(prob[t % 4][:, 0:n], prob[t % 4][:, 0:n], ACT.Exp, scale=SCALE,
                                             bias=att_stat[:, st + 1:st + 2],
                                             accum_out=att_stat[:, st + 2:st + 3]).then_inc(exp_done, 1)
                    if t >= 6 and (t - 3) % 4 == 3:
                        g = (t - 3) // 4
                        act.wait_ge(pv_done, i * 4 + (g + 1))
                        act.wait_ge(att_stored[g % 2], i * 32 + 16 * (g // 2 + 1))
                        nc.scalar.copy(att_o[g % 2][:, :], ps[:, 6 + g % 2, :]).then_inc(pv_out, 1)
                        act.wait_ge(pv_out, i * 4 + (g + 1))
                        dst = acts_d[bass.ds(i * 2 + g // 2, 1)].rearrange("a p s -> p (a s)")
                        act.dma_start(dst[:, (g % 2) * 512:(g % 2) * 512 + 512], att_o[g % 2][:, :]).then_inc(att_stored[g % 2], 16)
                    if t >= 2 and (t < STEPS + 2 or not last):
                        b = (t - 2) % NT
                        g = (t - 2) // 4
                        q0 = (b % 4) * P
                        for k0 in range(0, b + 1, 4):
                            m = min(4, b + 1 - k0)
                            act.wait_ge(pt_done, i * 24 + (turns + 1))
                            if g >= 2:
                                act.wait_ge(pv_done, i * 4 + (g - 1))
                            nc.scalar.copy(probT[g % 2][:, k0:k0 + m, q0:q0 + P],
                                           ps[:, 4 + turns % 2, 0:m * P].rearrange("p (k q) -> p k q", k=m)).then_inc(pt_out, 1)
                            turns += 1

            for p in range(2):
                act.sem_inc(att_stored[p], 16)
            attend(0, range(3), 0)
            with act.Fori(0, NH // 2 - 1) as i:
                attend(i, range(3, STEPS + 3), 1)
            attend(NH // 2 - 1, range(3, STEPS + 3), 1, last=True)
            for p in range(2):
                act.wait_ge(att_stored[p], 16 * (NH + 1))
            meet(act, 6)

            flat = "p c h -> p (c h)"
            act.wait_ge(dt_abs, 1)
            nc.scalar.activation(ea[:, :, :], acum[:, :, :], ACT.Exp, scale=-1.0).then_inc(dt_exp, 1)
            nc.scalar.activation(alog_row[:, :], alog_row[:, :], ACT.Exp).then_inc(dt_exp, 1)
            act.wait_ge(dt_plus, 1)
            nc.scalar.activation(dec[:, :, :], dte[:, :, :], ACT.Ln).then_inc(dt_ln, 1)
            act.wait_ge(acum_done, 1)
            nc.scalar.activation(acum[:, :, :].rearrange(flat), ps[:, 0, 0:NT * NS], ACT.Copy, scale=-1.0).then_inc(aend_out, 1)
            nc.scalar.activation(ea[:, :, :].rearrange(flat), ps[:, 0, 0:NT * NS], ACT.Exp).then_inc(aend_out, 1)
            nc.scalar.activation(dec[:, :, :].rearrange(flat), ps[:, 1, 0:NT * NS], ACT.Exp).then_inc(aend_out, 1)
            act.wait_ge(dte_ready, 1)
            nc.scalar.activation(dte[:, :, :], dte[:, :, :], ACT.Exp)
            meet(act, 7)
            with act.Fori(0, NG) as g:
                A.enter(g, 1)

                def evac(T):
                    if T >= 2:
                        act.wait_ge(conv_done, g * 6 + (T - 1))
                    nc.scalar.copy(c_in[T % 2][:, TAPS - 1:TAPS - 1 + SEQ].rearrange("p (a b) -> p a b", a=2),
                                   ps[:, 2 * (T % 4):2 * (T % 4) + 2, :]).then_inc(conv_in, 1)

                def silu(T):
                    act.wait_ge(conv_done, g * 6 + (T + 1))
                    dst = (b_fm, c_fm, *c_out, *c_out)[T]
                    col = (g + (88 + 16), g + (88 + 20))[T] if T < 2 else g * 4 + (88 + T - 2)
                    nc.scalar.activation(dst[:, :], c_out[T % 2][:, :], ACT.Silu,
                                         bias=vec_a[:, bass.ds(col, 1)]).then_inc(silu_done, 1)

                def z_evac(j):
                    for t in range(NT):
                        v = NT * j + t
                        act.wait_ge(z_done, g * 16 + (v + 1))
                        nc.scalar.activation(zy[:, t, WC * j:WC * j + WC], ps[:, 4 + v % 4, 0:WC], ACT.Silu).then_inc(z_out, 1)

                def tile_evac(r):
                    act.wait_ge(tile_turned, g * 5 + (r + 1))
                    dst = b_tm[:, :, :] if r == 0 else xs_tm[:, :, (r - 1) * P:r * P]
                    nc.scalar.copy(dst, ps[:, 2 * (r % 2):2 * (r % 2) + 2, :].rearrange("p a (b f) -> p (a b) f", f=P)).then_inc(tile_out, 1)

                act.wait_ge(w_used[0], g * 3 + (N_SSM // 2 + 1))
                evac(0)
                evac(1)
                silu(0)
                silu(1)
                act.wait_ge(w_used[1], g * 3 + (N_SSM // 2 + 1))
                evac(2)
                evac(3)
                silu(2)
                silu(3)
                act.wait_ge(w_used[0], g * 3 + (N_SSM // 2 + 2))
                evac(4)
                evac(5)
                z_evac(0)
                tile_evac(0)
                tile_evac(1)
                tile_evac(2)
                silu(4)
                silu(5)
                z_evac(1)
                tile_evac(3)
                tile_evac(4)
                def squares_of(k):
                    act.wait_ge(y_ready, g * NT + (k + 1))
                    nc.scalar.activation(c_out[k % 2][:, 0:DG], zy[:, k, :], ACT.Square,
                                         accum_out=stat[:, 96 + k:97 + k]).then_inc(gn_squares, 1)
                    act.wait_ge(gn_squares, g * NT + (k + 1))

                for k in range(NT):
                    act.wait_ge(seg_done, g * NT + (k + 1))
                    if k >= 1:
                        act.wait_ge(mix_ready, g * NT + k)
                    nc.scalar.copy(cb_sb[:, :], ps[:, 7, 0:P]).then_inc(cb_out, 1)
                    if k >= 2:
                        act.wait_ge(mix_done, g * NT + (k - 1))
                    for h in range(HG):
                        ins = nc.scalar.activation(decay[k % 2][:, h, :], ps[:, h // 4, (h % 4) * P:(h % 4 + 1) * P], ACT.Exp,
                                                   bias=acum[:, k, bass.ds(g * HG + h, 1)])
                    ins.then_inc(decay_done, 1)
                    if k >= 2:
                        squares_of(k - 2)
                squares_of(NT - 2)
                squares_of(NT - 1)
                act.wait_ge(gn_var, g + 1)
                nc.scalar.activation(stat[:, 96:104], stat[:, 96:104], ACT.Sqrt).then_inc(gn_root, 1)
                act.wait_ge(w_used[1], g * 3 + (N_SSM // 2 + 3))
                for m in range(2):
                    nc.scalar.activation(c_in[m][:, TAPS - 1:TAPS - 1 + SEQ].rearrange("p (a b) -> p a b", a=2),
                                         ps[:, 2 * m:2 * m + 2, :], ACT.Sigmoid).then_inc(ga_out, 1)
                for m in range(2):
                    act.wait_ge(ga_out, g * 2 + (m + 1))
                    act.dma_start(gate_d[bass.ds(g * 2 + m, 1)].rearrange("a p s -> p (a s)"),
                                  c_in[m][:, TAPS - 1:TAPS - 1 + SEQ]).then_inc(ga_stored[m], 16)
                for f in range(4):
                    act.wait_ge(yt_done, g * 4 + (f + 1))
                    if f >= 2:
                        act.wait_ge(y_stored[f % 2], g * 32 + 16)
                    nc.scalar.activation(c_out[f % 2][:, :].rearrange("p (a b) -> p a b", a=2),
                                         ps[:, 4 + 2 * (f % 2):6 + 2 * (f % 2), :], ACT.Copy,
                                         scale=vec_b[:, bass.ds(g * 4 + (96 + f), 1)]).then_inc(yt_out, 1)
                    act.wait_ge(yt_out, g * 4 + (f + 1))
                    act.dma_start(acts_d[bass.ds(g * 4 + (KT + f), 1)].rearrange("a p s -> p (a s)"),
                                  c_out[f % 2][:, :]).then_inc(y_stored[f % 2], 16)
                for m in range(2):
                    act.wait_ge(ga_stored[m], g * 16 + 16)
                    act.wait_ge(y_stored[m], g * 32 + 32)
                A.step()
                act.drain().then_inc(group_end, 1)
                A.leave(NG)
                act.wait_ge(group_end, g * 3 + 3)

            def act_load(k, tile):
                act.dma_start(act_raw[k % 2][:, :], acts_d[bass.ds(tile, 1)].rearrange("a p s -> p (a s)")).then_inc(act_in[k % 2], 16)

            for k in range(2):
                act_load(k, k)
            for k in range(KT):
                act.wait_ge(act_in[k % 2], 16 * (k // 2 + 1))
                nc.scalar.copy(a_hi[:, k, :], act_raw[k % 2][:, :]).then_inc(hi_copied, 1)
                if k < KT - 2:
                    act.wait_ge(act_split, k + 1)
                    act_load(k, k + 2)
            with act.Fori(0, 2) as i:
                for k in range(2):
                    act.wait_ge(act_split, i * 8 + (KT - 1 + k))
                    act_load(k, i * 8 + (KT + k))
                for k in range(KT):
                    act.wait_ge(act_used, i * 8 + (k + 1))
                    act.wait_ge(act_in[k % 2], i * 64 + (64 + 16 * (k // 2 + 1)))
                    nc.scalar.copy(a_hi[:, k, :], act_raw[k % 2][:, :]).then_inc(hi_copied, 1)
                    if k < KT - 2:
                        act.wait_ge(act_split, i * 8 + (8 + k + 1))
                        act_load(k, i * 8 + (8 + k + 2))
            meet(act, 8)
            for k in range(KT):
                nc.scalar.copy(a_hi[:, k, :], acc[:, k, :]).then_inc(hi_copied, 1)
            for i in range(2):
                act.wait_ge(diag_used, KT * (i + 1))
                nc.scalar.copy(row[i][:, :].rearrange("p (a b) -> p a b", a=2), ps[:, 2 * i:2 * i + 2, :])
            act.wait_ge(act_split, 4 * KT)
            meet(act, 9)
            for j in range(4):
                for t in range(NT):
                    act.wait_ge(merge_done, 8 * j + t + 1)
                    nc.scalar.copy(x_tm[:, t, j * WC:(j + 1) * WC], ps[:, t, 0:WC]).then_inc(merge_out, 1)
            norm_stats(1, x_tm, lambda t: act.wait_ge(merge_out, 25 + t), sq)
            for t in range(NT):
                act.wait_ge(x1_made, t + 1)
                act.dma_start(x1_d[t * P:(t + 1) * P, :], x_tm[:, t, :]).then_inc(x1_stored, 16)
            norm_stats(2, x_tm, lambda t: None, sq)
            meet(act, 10)
            norm_evac(1, 24)
            meet(act, 11)

            def hidden(n, c, extra=0, first=False):
                act.wait_ge(w_used[n % 2], n // 2 + 1 + extra)
                for j in range(4):
                    if not first:
                        act.wait_ge(u_split, c * 4 + (j - 3))
                    nc.scalar.activation(u_tmp[j][:, :], ps[:, j, :], ACT.Relu).then_inc(up_out, 1)
                    act.wait_ge(up_out, c * 4 + (j + 1))
                    nc.scalar.activation(u_tmp[j][:, :], u_tmp[j][:, :], ACT.Square).then_inc(u_squared, 1)

            hidden(N_MLP, 0, first=True)
            with act.Fori(0, NC // 2 - 1) as i:
                hidden(N_MLP + 1, i * 2 + 1, extra=i * 2)
                hidden(N_MLP + 3, i * 2 + 2, extra=i * 2)
            hidden(N_ALL - 3, NC - 1)
            norm_stats(3, x_tm, lambda t: act.wait_ge(down_out, 8 * (NC - 1) + t + 1), sq)
            meet(act, 12)

        @block.vector
        def _(dve):
            V = Count(dve, dve_own)
            ve = nc.vector

            def norm_roots(j):
                st = stat[:, 16 * j:16 * j + NT]
                rs = stat[:, 16 * j + 8:16 * j + 16]
                dve.wait_ge(squares, j + 1)
                ve.tensor_scalar(st, st, 1.0 / D, EPS, ALU.mult, ALU.add).then_inc(vars_ready, 1)
                dve.wait_ge(roots, j + 1)
                V.link(ve.reciprocal(rs, st))
                return rs

            def norm_scale(j):
                rs = norm_roots(j)
                for t in range(NT):
                    ve.tensor_scalar(x_tm[:, t, :], x_tm[:, t, :], rs[:, t:t + 1], None, ALU.mult).then_inc(normed, 1)

            def norm_split(j):
                for i in range(2 * KT):
                    g, k = divmod(i, KT)
                    dve.wait_ge(h_ready, 16 * j + i + 1)
                    r = slice(g * 512, g * 512 + 512)
                    V.link(ve.tensor_copy(a_hi[:, k, r], h_tmp[i % 4][:, :]))
                    ve.tensor_tensor(a_lo[:, k, r], h_tmp[i % 4][:, :], a_hi[:, k, r].bitcast(F32),
                                     ALU.subtract).then_inc(h_split, 1)

            norm_scale(0)
            dve.wait_ge(c_ready, 2)
            V.link(ve.tensor_tensor(mod[:, 0:16], mod[:, 0:16], vec_a[:, 0:16], ALU.add))
            V.link(ve.tensor_scalar(gain[:, 0:KT], mod[:, 8:16], 1.0, None, ALU.add))
            ve.tensor_tensor(gain[:, 0:KT], gain[:, 0:KT], vec_a[:, 56:64], ALU.mult).then_inc(gain_ready, 1)
            norm_split(0)
            meet(dve, 0)

            meet(dve, 1)
            dve.wait_ge(kv_sq, 1)
            V.link(ve.tensor_scalar(stat[:, 64:72], stat[:, 64:72], 1.0 / R, EPS, ALU.mult, ALU.add))
            ve.tensor_scalar(stat[:, 72:80], stat[:, 72:80], 1.0 / DI, EPS, ALU.mult, ALU.add).then_inc(kv_var, 1)
            dve.wait_ge(kv_root, 1)
            V.link(ve.reciprocal(stat[:, 80:96], stat[:, 64:80]))
            for t in range(NT):
                ve.scalar_tensor_tensor(ckv_tm[:, t, :], ps[:, t, 0:R], stat[:, 80 + t:81 + t], kv_row[:, :],
                                        ALU.mult, ALU.mult)
                for half in range(2):
                    ve.scalar_tensor_tensor(kidx_tm[:, t, half * DI:half * DI + DI], ps[:, t, R:R + DI],
                                            stat[:, 88 + t:89 + t], ki_row[:, :], ALU.mult, ALU.mult)
                ve.tensor_scalar(w_idx[:, t, :], ps[:, t, R + DI:R + DI + HI], HI ** -0.5, None, ALU.mult)
                ve.tensor_copy(dt[:, t, :], ps[:, t, R + DI + HI:R + NSM])
            meet(dve, 2)
            for i in range(2):
                V.link(ve.memset(k_idx_half[1 - i][DI * i:DI * i + DI, :], 0.0))
            for r in range(2):
                dve.wait_ge(kv_out, r + 1)
                V.link(ve.tensor_copy(ckv_hi[:, r, :], sq0[:, :]))
                V.link(ve.tensor_tensor(ckv_lo[:, r, :], sq0[:, :], ckv_hi[:, r, :].bitcast(F32), ALU.subtract))
                dve.sem_inc(kv_out_split, 1)
            meet(dve, 3)
            scores(dve, 0, SCORED, lambda s, r, w: ve.tensor_scalar(s, r, w, None, ALU.mult),
                   lambda s, r, w: ve.scalar_tensor_tensor(s, r, w, s, ALU.mult, ALU.add))
            meet(dve, 4)

            ROUNDS = TOPK // 8
            for b in range(2):
                if b:
                    V.link(ve.memset(bias_bf[:, b, 0:b * P], 0.0))
                V.link(ve.tensor_copy(bias_bf[:, b, b * P:(b + 1) * P], future[:, :]))
            done = 0
            for b0 in range(2, NT, 2):
                if b0 + 1 >= SCORED:
                    dve.wait_ge(relu_used, HI * sum(len(key_chunks(b)) for b in range(NT)))
                pair = [score[:, b, 0:(b + 1) * P] for b in (b0, b0 + 1)]
                for j, b in enumerate((b0, b0 + 1)):
                    d = score[:, b, b * P:(b + 1) * P]
                    ve.tensor_tensor(d, d, future[:, :], ALU.add).then_inc(topk_step, 1)
                done += 2
                with dve.Fori(0, ROUNDS) as i:
                    V.enter(i, 4)
                    for j in range(2):
                        dve.wait_ge(topk_step, i * 4 + (done - 1 + j))
                        V.step()
                        ve.max(top8[j][:, :], pair[j]).then_inc(topk_step, 1)
                    for j in range(2):
                        dve.wait_ge(topk_step, i * 4 + (done + 1 + j))
                        V.step()
                        ve.match_replace(pair[j], top8[j][:, :], pair[j], TAKEN).then_inc(topk_step, 1)
                    V.leave(ROUNDS)
                done += 4 * ROUNDS
                dve.wait_ge(topk_step, done)
                for j, b in enumerate((b0, b0 + 1)):
                    V.link(ve.tensor_scalar(bias_bf[:, b, 0:(b + 1) * P], pair[j], TAKEN, NEG, ALU.not_equal, ALU.mult))
            dve.wait_ge(mod_ready, 1)
            V.link(ve.tensor_tensor(mod[:, 16:48], mod[:, 16:48], vec_a[:, 16:48], ALU.add))
            V.link(ve.tensor_scalar(gain[:, KT:2 * KT], mod[:, 32:40], 1.0, None, ALU.add))
            V.link(ve.tensor_tensor(gain[:, KT:2 * KT], gain[:, KT:2 * KT], vec_a[:, 72:80], ALU.mult))
            V.link(ve.tensor_tensor(gate_cols[:, 0:KT], mod[:, 16:24], vec_a[:, 64:72], ALU.mult))
            V.link(ve.tensor_tensor(gate_cols[:, KT:2 * KT], mod[:, 40:48], vec_a[:, 80:88], ALU.mult))
            meet(dve, 5)

            def attend(i, positions, last=False):
                for t in positions:
                    if t < STEPS or not last:
                        b = t % NT
                        n = (b + 1) * P
                        st = 4 * (t % 4)
                        dve.wait_ge(qk_done, i * STEPS + (t + 1))
                        s = ps[:, 2 * (t % 2):2 * (t % 2) + 2, :].rearrange("p a b -> p (a b)")[:, 0:n]
                        V.step()
                        V.link(ve.tensor_tensor_reduce(out=prob[t % 4][:, 0:n], in0=s, in1=bias_bf[:, b, 0:n], scale=1.0,
                                                       scalar=TAKEN, op0=ALU.add, op1=ALU.max,
                                                       accum_out=att_stat[:, st:st + 1]))
                        ve.tensor_scalar(att_stat[:, st + 1:st + 2], att_stat[:, st:st + 1], -SCALE, None, ALU.mult).then_inc(masked, 1)
                    if t >= 1:
                        n = ((t - 1) % NT + 1) * P
                        st = 4 * ((t - 1) % 4)
                        dve.wait_ge(exp_done, i * STEPS + t)
                        V.link(ve.reciprocal(att_stat[:, st + 3:st + 4], att_stat[:, st + 2:st + 3]))
                        ve.tensor_scalar(prob[(t - 1) % 4][:, 0:n], prob[(t - 1) % 4][:, 0:n], att_stat[:, st + 3:st + 4],
                                         None, ALU.mult).then_inc(p_ready, 1)

            attend(0, range(1))
            with dve.Fori(0, NH // 2 - 1) as i:
                V.enter(i, 3 * STEPS)
                attend(i, range(1, STEPS + 1))
                V.leave(NH // 2 - 1)
            attend(NH // 2 - 1, range(1, STEPS + 1), last=True)
            meet(dve, 6)

            rows8 = [P, NT, NS]

            def every_chunk(row):
                return row[:, :].rearrange("p (o h) -> p o h", o=1).broadcast_to(rows8)

            V.link(ve.tensor_tensor(dt[:, :, :], dt[:, :, :], every_chunk(dtb_row), ALU.add))
            ve.scalar_tensor_tensor(acum[:, :, :], dt[:, :, :], -1.0, dt[:, :, :], ALU.mult, ALU.max).then_inc(dt_abs, 1)
            dve.wait_ge(dt_exp, 2)
            ve.tensor_scalar(dte[:, :, :], ea[:, :, :], 1.0, None, ALU.add).then_inc(dt_plus, 1)
            dve.wait_ge(dt_plus, 1)
            V.link(ve.tensor_scalar(dta[:, :, :], dte[:, :, :], 1.0, None, ALU.is_equal))
            dve.wait_ge(dt_ln, 1)
            V.link(ve.tensor_tensor(dec[:, :, :], dec[:, :, :], dta[:, :, :], ALU.add))
            V.link(ve.scalar_tensor_tensor(dte[:, :, :], dte[:, :, :], -1.0, dta[:, :, :], ALU.add, ALU.add))
            V.link(ve.reciprocal(dte[:, :, :], dte[:, :, :]))
            V.link(ve.tensor_tensor(dec[:, :, :], dec[:, :, :], dte[:, :, :], ALU.mult))
            V.link(ve.tensor_tensor(dec[:, :, :], dec[:, :, :], ea[:, :, :], ALU.mult))
            V.link(ve.scalar_tensor_tensor(dt[:, :, :], dt[:, :, :], 0.0, dec[:, :, :], ALU.max, ALU.add))
            V.link(ve.tensor_scalar(alog_row[:, :], alog_row[:, :], -1.0, None, ALU.mult))
            ve.tensor_tensor(dta[:, :, :], dt[:, :, :], every_chunk(alog_row), ALU.mult).then_inc(dta_ready, 1)
            dve.wait_ge(aend_out, 3)
            V.link(ve.tensor_tensor(dte[:, :, :].rearrange("p c h -> p (c h)"), ps[:, 1, 0:NT * NS],
                                    acum[:, :, :].rearrange("p c h -> p (c h)"), ALU.add))
            dve.sem_inc(dte_ready, 1)
            for m in range(2):
                V.link(ve.memset(c_in[m][:, 0:TAPS - 1], 0.0))
            meet(dve, 7)
            with dve.Fori(0, NG) as g:
                V.enter(g, 6 * (TAPS - 1) + 4 * NT - 2)
                ve.tensor_copy(dta_g[:, :, :], dta[:, :, bass.ds(g * HG, HG)]).then_inc(dtag_ready, 1)
                for T in range(6):
                    dve.wait_ge(conv_in, g * 6 + (T + 1))
                    if T >= 2:
                        dve.wait_ge(silu_done, g * 6 + (T - 1)) if T < 4 else dve.wait_ge(tile_turned, g * 5 + (T - 2))
                    o = c_out[T % 2][:, :]
                    for j in range(TAPS):
                        col = (g + (24 * j + 16), g + (24 * j + 20))[T] if T < 2 else g * 4 + (24 * j + T - 2)
                        wj = vec_b[:, bass.ds(col, 1)]
                        src = c_in[T % 2][:, j:j + SEQ]
                        if j == 0:
                            V.link(ve.tensor_scalar(o, src, wj, None, ALU.mult))
                        elif j < TAPS - 1:
                            V.link(ve.scalar_tensor_tensor(o, src, wj, o, ALU.mult, ALU.add))
                        else:
                            ve.scalar_tensor_tensor(o, src, wj, o, ALU.mult, ALU.add).then_inc(conv_done, 1)

                def heads(t, k):
                    return t[:, k, bass.ds(g * HG, HG)]

                dve.wait_ge(tile_out, g * 5 + 5)

                def xs3(k):
                    return xs_tm[:, k, :].rearrange("p (h d) -> p h d", h=HG)

                def mix_in(k):
                    dve.wait_ge(decay_done, g * NT + (k + 1))
                    ve.tensor_tensor(decay[k % 2][:, :, :], decay[k % 2][:, :, :],
                                     cb_sb[:, :].rearrange("p (o l) -> p o l", o=1).broadcast_to([P, HG, P]), ALU.mult).then_inc(mix_ready, 1)

                def bank(b):
                    return ps[:, b, :].rearrange("p (h d) -> p h d", h=HG)

                mix_in(0)
                for k in range(NT):
                    if k + 1 < NT:
                        mix_in(k + 1)
                    dve.wait_ge(mix_done, g * NT + (k + 1))
                    if k == 0:
                        ve.tensor_copy(state[:, :, :], bank(6)).then_inc(state_ready, 1)
                    elif k < NT - 1:
                        V.link(ve.tensor_tensor(state[:, :, :], state[:, :, :], spread(heads(dec, k), PD), ALU.mult))
                        ve.tensor_tensor(state[:, :, :], state[:, :, :], bank(6), ALU.add).then_inc(state_ready, 1)
                    y = y_t[k % 2][:, :, :]
                    if k == 0:
                        V.link(ve.tensor_copy(y, bank(2)))
                    else:
                        V.link(ve.tensor_tensor(y, bank(3 + 2 * (k % 2)), spread(heads(ea, k), PD), ALU.mult))
                        V.link(ve.tensor_tensor(y, y, bank(2 + 2 * (k % 2)), ALU.add))
                    dve.wait_ge(xs_skip, g * NT + (k + 1))
                    V.link(ve.tensor_tensor(y, y, xs3(k), ALU.add))
                    z = zy[:, k, :].rearrange("p (h d) -> p h d", h=HG)
                    ve.tensor_tensor(z, z, y, ALU.mult).then_inc(y_ready, 1)
                dve.wait_ge(gn_squares, g * NT + NT)
                ve.tensor_scalar(stat[:, 96:104], stat[:, 96:104], 1.0 / DG, EPS, ALU.mult, ALU.add).then_inc(gn_var, 1)
                dve.wait_ge(gn_root, g + 1)
                V.link(ve.reciprocal(stat[:, 104:112], stat[:, 96:104]))
                for k in range(NT):
                    ve.tensor_scalar(zy[:, k, :], zy[:, k, :], stat[:, 104 + k:105 + k], None, ALU.mult).then_inc(gn_ready, 1)
                V.leave(NG)
                dve.drain().then_inc(group_end, 1)
                dve.wait_ge(group_end, g * 3 + 3)

            V.link(ve.memset(acc[:, :, :], 0.0))

            def act_lo(first, src=None):
                for k in range(KT):
                    dve.wait_ge(hi_copied, first + (k + 1))
                    raw_k = act_raw[k % 2][:, :] if src is None else src[:, k, :]
                    ve.tensor_tensor(a_lo[:, k, :], raw_k, a_hi[:, k, :].bitcast(F32), ALU.subtract).then_inc(act_split, 1)

            def gate_block(n, j, turn):
                dve.wait_ge(w_used[n % 2], turn * 2 + (n // 2 + 1))
                dve.wait_ge(gates_in[j % 2], turn * 32 + 16 * (j // 2 + 1))
                for b in range(4):
                    m, q = divmod(b, 2)
                    r = slice(q * 512, q * 512 + 512)
                    ve.tensor_tensor(gated[b % 2][:, :], ps[:, 4 * (j % 2) + b, :], gates[j % 2][:, m, r], ALU.mult).then_inc(gate_used, 1)
                    dve.wait_ge(gate_used, turn * 16 + (4 * j + b + 1))
                    V.link(ve.tensor_tensor(acc[:, 2 * j + m, r], acc[:, 2 * j + m, r], gated[b % 2][:, :], ALU.add))

            act_lo(0)
            with dve.Fori(0, 2) as i:
                V.enter(i, 16)
                for j in range(3):
                    gate_block(N_O + j, j, i)
                act_lo(i * 8 + 8)
                gate_block(N_O + 3, 3, i)
                V.leave(2)
            for j in range(4):
                gate_block(N_O + j, j, 2)
            meet(dve, 8)
            for i in range(2 * KT):
                if i >= 2:
                    dve.wait_ge(diag_used, i - 1)
                ve.tensor_scalar(diag[i % 2][:, :], ident[:, :], gate_cols[:, i:i + 1], None, ALU.mult).then_inc(diag_made, 1)
            act_lo(3 * KT, acc)
            meet(dve, 9)
            rs = norm_roots(1)
            for t in range(NT):
                V.link(ve.scalar_tensor_tensor(x_tm[:, t, :], x_tm[:, t, :], rs[:, t:t + 1], row[0][:, :], ALU.mult, ALU.mult))
                dve.wait_ge(res_in[t % 4], 16 * (t // 4 + 1))
                ve.tensor_tensor(x_tm[:, t, :], x_tm[:, t, :], x_in[t % 4][:, :], ALU.add).then_inc(x1_made, 1)
            dve.wait_ge(x1_stored, 16 * NT)
            norm_scale(2)
            meet(dve, 10)
            norm_split(1)
            V.link(ve.memset(x_tm[:, :, :], 0.0))
            meet(dve, 11)

            def u_part(c, b, j):
                m, q = divmod(j, 2)
                r = slice(q * 512, q * 512 + 512)
                dve.wait_ge(u_squared, c * 4 + (j + 1))
                V.link(ve.tensor_copy(u_hi[b][:, m, r], u_tmp[j][:, :]))
                ve.tensor_tensor(u_lo[b][:, m, r], u_tmp[j][:, :], u_hi[b][:, m, r].bitcast(F32), ALU.subtract).then_inc(u_split, 1)

            def add_down(c, t, first=False):
                dve.wait_ge(down_done, c * 8 + (t + 1))
                if not first:
                    dve.wait_ge(down_out, c * 8 + (t - 7))
                ve.tensor_tensor(x_tm[:, t, :].rearrange("p (a b) -> p a b", a=2), x_tm[:, t, :].rearrange("p (a b) -> p a b", a=2),
                                 ps[:, 4 + 2 * (t % 2):6 + 2 * (t % 2), :], ALU.add).then_inc(down_out, 1)

            def chunk(c, b, last=False, first=False, down_before=None):
                if down_before is not None:
                    dve.wait_ge(*down_before)
                for t in range(NT):
                    if t < 4 and not last:
                        u_part(c + 1, 1 - b, t)
                    add_down(c, t, first)

            for j in range(4):
                u_part(0, 0, j)
            chunk(0, 0, first=True)
            chunk(1, 1, down_before=(w_used[0], (N_MLP + 2) // 2 + 1))
            with dve.Fori(1, NC // 2 - 1) as i:
                V.enter(i - 1, 8)
                chunk(i * 2, 0, down_before=(w_used[0], i * 2 + (N_MLP // 2 + 1)))
                chunk(i * 2 + 1, 1, down_before=(w_used[0], i * 2 + (N_MLP // 2 + 2)))
                V.leave(NC // 2 - 2)
            chunk(NC - 2, 0, down_before=(w_used[0], (N_ALL - 4) // 2 + 1))
            chunk(NC - 1, 1, last=True)
            rs = norm_roots(3)
            meet(dve, 12)
            for t in range(NT):
                V.link(ve.scalar_tensor_tensor(x_tm[:, t, :], x_tm[:, t, :], rs[:, t:t + 1], row[1][:, :], ALU.mult, ALU.mult))
                dve.wait_ge(res_in[t % 4], 16 * (t // 4 + 3))
                ve.tensor_tensor(x_tm[:, t, :], x_tm[:, t, :], x_in[t % 4][:, :], ALU.add).then_inc(out_made, 1)


_INS = ['x', 'c', 'ada_w', 'ada_b', 'norm_g', 'w_in', 'kv_norm_g', 'kidx_norm_g', 'w_uk', 'w_uv', 'conv_w', 'conv_b',
        'dt_bias', 'a_log', 'd_skip', 'ssm_norm_g', 'w_o_att', 'w_o_ssd', 'w_out', 'w_up', 'w_down']
_OUTS = [((1, 1024, 1024), 'float32')]


def kernel(**inputs):
    import numpy as _np
    import concourse.bacc as _bacc
    from concourse import mybir as _mybir
    from concourse.bass_utils import run_bass_kernel_spmd as _run

    nc = _bacc.Bacc("TRN2", target_bir_lowering=False, num_devices=1)
    arrays, args = {}, []
    for name in _INS:
        a = _np.ascontiguousarray(inputs[name])
        arrays[f"in_{name}_dram"] = a
        args.append(nc.dram_tensor(f"in_{name}_dram", a.shape, _mybir.dt.from_np(a.dtype), kind="ExternalInput").ap())
    for i, (shape, dtype) in enumerate(_OUTS):
        dt = _mybir.dt.from_np(_np.dtype(dtype))
        args.append(nc.dram_tensor(f"out_{i}_dram", shape, dt, kind="ExternalOutput").ap())
    hybrid_block(nc, *args)
    r = _run(nc, [arrays], core_ids=[0])
    return r.results[0]["out_0_dram"]
```

```python
from contextlib import ExitStack

import concourse.bass as bass
from concourse import mybir

P = 128
F32 = mybir.dt.float32
F32R = mybir.dt.float32r
BF16 = mybir.dt.bfloat16
ALU = mybir.AluOpType
ACT = mybir.ActivationFunctionType
AX_X = mybir.AxisListType.X


class Count:

    def __init__(self, engine, sem):
        self.engine, self.sem, self.n, self.turn, self.per = engine, sem, 0, None, 0

    def add(self, ins):
        ins.then_inc(self.sem, 1)
        self.n += 1
        return ins

    def value(self):
        return self.n if self.turn is None else self.n + self.turn * self.per

    def wait(self):
        self.engine.wait_ge(self.sem, self.value())

    def link(self, ins):
        self.add(ins)
        self.wait()

    def step(self):
        self.engine.sem_inc(self.sem, 1)
        self.n += 1

    def enter(self, turn, per):
        self.turn, self.per, self.base = turn, per, self.n

    def leave(self, turns):
        assert self.n - self.base == self.per, (self.n - self.base, self.per)
        self.turn = None
        self.n = self.base + turns * self.per


def hybrid_block(nc, x, c, ada_w, ada_b, norm_g, w_in, kv_norm_g, kidx_norm_g, w_uk, w_uv, conv_w, conv_b,
                 dt_bias, a_log, d_skip, ssm_norm_g, w_o_att, w_o_ssd, w_out, w_up, w_down, out):
    SEQ, D = x.shape[1], x.shape[2]
    R = kv_norm_g.shape[1]
    DI = kidx_norm_g.shape[1]
    NH, HD = w_uk.shape[2], w_uk.shape[3]
    NS = dt_bias.shape[1]
    CD = conv_w.shape[2]
    DIN = ssm_norm_g.shape[1]
    DFF = w_up.shape[2]
    HI = 8
    NG = 4
    HG = NS // NG
    PD = DIN // NS
    DG = DIN // NG
    TAPS = conv_w.shape[1]
    TOPK = 256
    EPS = 1e-6
    SCALE = float(HD) ** -0.5
    KT = D // P
    NT = SEQ // P
    WC = 256
    NEG = -1e30
    TAKEN = -3e38
    C_Q = 0
    C_KV = C_Q + NH * HD
    C_QI = C_KV + R
    C_KI = C_QI + HI * DI
    C_Z = C_KI + DI + HI
    C_X = C_Z + DIN
    C_B = C_X + DIN
    C_C = C_B + NG * P
    C_DT = C_X + CD
    C_GA = C_DT + NS
    C_GS = C_GA + D
    NSM = DI + HI + NS
    assert SEQ == D == 1024 and C_GS + D == w_in.shape[2] and HD == P and R == WC and 2 * DI == P
    assert DG == 4 * P and HG * PD == DG

    N_Q, N_UK, N_GS, N_SSM = 4, 8, 10, 14
    N_O = N_SSM + 6 * NG
    N_OUT = N_O + 12
    N_MLP = N_OUT + 4
    NC = DFF // WC
    N_ALL = N_MLP + 2 * NC

    at = [16512]

    def place(name, shape, dt, offset=None):
        size = 1
        for s in shape[1:]:
            size *= s
        size = (size * (2 if dt == BF16 else 4) + 31) // 32 * 32
        if offset is None:
            offset = at[0]
            at[0] += size
        assert offset + size <= 229344, (name, offset + size)
        return nc.alloc_sbuf_tensor_at(name, shape, dt, offset=offset)

    raw = [place(f"raw{s}", [P, KT * WC], F32) for s in range(2)]
    w_hi = [place(f"w_hi{s}", [P, KT * WC], F32R) for s in range(2)]
    w_lo = [place(f"w_lo{s}", [P, KT * WC], F32R) for s in range(2)]
    ACT_AT = at[0]
    a_hi = place("a_hi", [P, KT, SEQ], F32R)
    a_lo = place("a_lo", [P, KT, SEQ], F32R)
    R1 = at[0]
    x_tm = place("x_tm", [P, NT, D], F32)
    ident = place("ident", [P, P], F32)
    ident_bf = place("ident_bf", [P, P], BF16)
    ones = place("ones", [P, P], F32)
    tri = place("tri", [P, P], F32)
    future = place("future", [P, P], F32)
    past_bf = place("past_bf", [P, P], BF16)
    vec_a = place("vec_a", [P, 112], F32)
    vec_b = place("vec_b", [P, 112], F32)
    mod = place("mod", [P, 48], F32)
    gain = place("gain", [P, 2 * KT], F32)
    gate_cols = place("gate_cols", [P, 2 * KT], F32)
    c_act = place("c_act", [P, KT], F32)
    stat = place("stat", [P, 16 * KT], F32)
    kv_row = place("kv_row", [P, R], F32)
    ki_row = place("ki_row", [P, DI], F32)
    dtb_row = place("dtb_row", [P, NS], F32)
    alog_row = place("alog_row", [P, NS], F32)
    skip_row = place("skip_row", [P, NS], F32)
    w_idx = place("w_idx", [P, NT, HI], F32)
    att_stat = place("att_stat", [P, 16 * 4], F32)
    top8 = [place(f"top8_{i}", [P, 8], F32) for i in range(2)]
    R2 = at[0]
    K = 1024
    rows_a = place("rows_a", [112, P], F32, R2)
    rows_b = place("rows_b", [112, P], F32, R2 + 512)
    h_tmp = [place(f"h_tmp{i}", [P, 512], F32, R2 + (16 + 2 * i) * K) for i in range(4)]
    sq0 = place("sq0", [P, D], F32, R2 + 44 * K)
    ada0 = place("ada0", [P, KT, 2 * D], F32, ACT_AT)
    mod_row = place("mod_row", [1, 4 * D], F32, R2 + 32 * K)
    q_idx = place("q_idx", [P, 4, SEQ], F32, R2)
    ckv_hi = place("ckv_hi", [P, 2, SEQ], F32R, R2 + 16 * K)
    ckv_lo = place("ckv_lo", [P, 2, SEQ], F32R, R2 + 24 * K)
    ckv_tm = place("ckv_tm", [P, NT, R], F32, R2 + 32 * K)
    kidx_tm = place("kidx_tm", [P, NT, P], F32, R2 + 40 * K)
    relu_buf = place("relu_buf", [P, 4, 512], F32, R2 + 40 * K)
    k_idx_half = [place(f"k_idx_half{i}", [P, SEQ], F32, R2 + (48 + 4 * i) * K) for i in range(2)]
    score = place("score", [P, NT, SEQ], F32, R1)
    bias_bf = place("bias_bf", [P, NT, SEQ], BF16, R2)
    spill = [place(f"spill{i}", [P, SEQ], F32, R2 + (32 + 4 * i) * K) for i in range(4)]
    ada_raw = [place(f"ada_raw{i}", [P, KT, WC], F32, R2 + (16 + 8 * i) * K) for i in range(2)]
    DT0 = R2 + 51 * K
    dta = place("dta", [P, NT, NS], F32, DT0)
    acum = place("acum", [P, NT, NS], F32, DT0 + K)
    ea = place("ea", [P, NT, NS], F32, DT0 + 2 * K)
    dte = place("dte", [P, NT, NS], F32, DT0 + 3 * K)
    dec = place("dec", [P, NT, NS], F32, DT0 + 4 * K)
    dt = place("dt", [P, NT, NS], F32, DT0 + 5 * K)
    dta_g = place("dta_g", [P, NT, HG], F32, DT0 + 6 * K)
    hq = [place(f"hq{i}", [P, SEQ], F32, R2 + (16 + 12 * i) * K) for i in range(2)]
    hk = [place(f"hk{i}", [P, SEQ], F32, R2 + (20 + 12 * i) * K) for i in range(2)]
    hv = [place(f"hv{i}", [P, NT, P], F32, R2 + (24 + 12 * i) * K) for i in range(2)]
    prob = [place(f"prob{i}", [P, SEQ], F32, (R2 + 40 * K, R2 + 44 * K, R1 + 8 * K, R1 + 12 * K)[i]) for i in range(4)]
    att_o = place("att_o", [P, 512], F32, R2 + 48 * K)
    probT = [place(f"probT{i}", [P, (NT // 2, NT)[i], 512], F32, R1 + 16 * i * K) for i in range(2)]
    xs_tm = place("xs_tm", [P, NT, DG], F32, R1)
    zy = place("zy", [P, NT, DG], F32, R1 + 16 * K)
    PADW = SEQ + 8
    c_in = [place(f"c_in{i}", [P, PADW], F32, R2 + 4128 * i) for i in range(2)]
    o = R2 + 2 * 4128
    c_out = [place(f"c_out{i}", [P, SEQ], F32, o + 4 * K * i) for i in range(2)]
    o += 8 * K
    b_fm = place("b_fm", [P, SEQ], F32, o)
    c_fm = place("c_fm", [P, SEQ], F32, o + 4 * K)
    b_tm = place("b_tm", [P, NT, P], F32, o + 8 * K)
    o += 12 * K
    decay = [place(f"decay{i}", [P, HG, P], F32, o + 4 * K * i) for i in range(2)]
    o += 8 * K
    xdt = [place(f"xdt{i}", [P, HG, PD], F32, o + 2 * K * i) for i in range(2)]
    xde = [place(f"xde{i}", [P, HG, PD], F32, o + 4 * K + 2 * K * i) for i in range(2)]
    o += 8 * K
    state = place("state", [P, HG, PD], F32, o)
    y_t = [place(f"y_t{i}", [P, HG, PD], F32, o + 2 * K + 2 * K * i) for i in range(2)]
    assert o + 6 * K + 512 <= DT0, (o + 6 * K, DT0)
    cb_sb = place("cb_sb", [P, P], F32, o + 6 * K)
    acc = place("acc", [P, KT, SEQ], F32, R1)
    act_raw = [place(f"act_raw{i}", [P, SEQ], F32, R2 + (0, 4, 48, 52)[i] * K) for i in range(4)]
    gates = [place(f"gates{i}", [P, 2, SEQ], F32, R2 + (8 + 8 * i) * K) for i in range(2)]
    gated = [place(f"gated{i}", [P, 512], F32, R2 + (24 + 2 * i) * K) for i in range(2)]
    row = [place(f"row{i}", [P, D], F32, R2 + (32 + 4 * i) * K) for i in range(2)]
    diag = place("diag", [P, 2 * KT, P], F32, R2 + 40 * K)
    x_in = [place(f"x_in{i}", [P, D], F32, R2 + 4 * i * K) for i in range(4)]
    sq = place("sq", [P, D], F32, R2 + 50 * K)
    u_hi = [place(f"u_hi{i}", [P, 2, SEQ], F32R, R2 + 16 * i * K) for i in range(2)]
    u_lo = [place(f"u_lo{i}", [P, 2, SEQ], F32R, R2 + (8 + 16 * i) * K) for i in range(2)]
    u_tmp = [place(f"u_tmp{i}", [P, 512], F32, R2 + (40 + 2 * i) * K) for i in range(4)]

    q_d = nc.dram_tensor("q_d", (NH, P, SEQ), F32, kind="Internal").ap()
    k_d = nc.dram_tensor("k_d", (NH, P, SEQ), F32, kind="Internal").ap()
    v_d = nc.dram_tensor("v_d", (SEQ, NH * HD), F32, kind="Internal").ap()
    gate_d = nc.dram_tensor("gate_d", (2 * KT, P, SEQ), F32, kind="Internal").ap()
    acts_d = nc.dram_tensor("acts_d", (3 * KT, P, SEQ), F32, kind="Internal").ap()
    x1_d = nc.dram_tensor("x1_d", (SEQ, D), F32, kind="Internal").ap()

    ctx = ExitStack()
    with ctx:
        ps = ctx.enter_context(nc.psum_tensor("ps", [P, 8, 512], F32))

        def sem(name):
            return ctx.enter_context(nc.semaphore(name))

        raw_in = [sem(f"raw_in{s}") for s in range(2)]
        w_split = [sem(f"w_split{s}") for s in range(2)]
        w_used = [sem(f"w_used{s}") for s in range(2)]
        c_cols_in = sem("c_cols_in")
        hi_made = sem("hi_made")
        act_own, dve_own, pool_own = sem("act_own"), sem("dve_own"), sem("pool_own")
        met = sem("met")
        const_made = sem("const_made")
        small_in, rows_in = sem("small_in"), sem("rows_in")
        x_landed = [sem(f"x_landed{t}") for t in range(NT)]
        ada_in = [sem(f"ada_in{k}") for k in range(KT)]
        row_out = sem("row_out")
        vec_turned = sem("vec_turned")
        c_ready = sem("c_ready")
        mod0_done = sem("mod0_done")
        gain_ready = sem("gain_ready")
        squares = sem("squares")
        vars_ready = sem("vars_ready")
        roots = sem("roots")
        normed = sem("normed")
        turned = sem("turned")
        h_ready = sem("h_ready")
        h_split = sem("h_split")
        kv_sq, kv_var, kv_root, kv_turned, kv_out, kv_out_split = (
            sem(n) for n in ("kv_sq", "kv_var", "kv_root", "kv_turned", "kv_out", "kv_out_split"))
        qi_out, k_idx_out, kv_read = sem("qi_out"), sem("k_idx_out"), sem("kv_read")
        logit_done, relu_done, relu_used = sem("logit_done"), sem("relu_done"), sem("relu_used")

        unit_done, unit_out = sem("unit_done"), sem("unit_out")
        spilled = [sem(f"spilled{i}") for i in range(4)]
        ada2_in = [sem(f"ada2_in{i}") for i in range(2)]
        ada2_used, mod_ready = sem("ada2_used"), sem("mod_ready")
        topk_step = sem("topk_step")
        head_in = [sem(f"head_in{i}") for i in range(2)]
        qk_done, masked, exp_done, p_ready = (sem(n) for n in ("qk_done", "masked", "exp_done", "p_ready"))
        pt_done, pt_out, pv_done, pv_out = (sem(n) for n in ("pt_done", "pt_out", "pv_done", "pv_out"))
        att_stored = sem("att_stored")
        dta_ready, acum_done, aend_out, dte_ready = (sem(n) for n in ("dta_ready", "acum_done", "aend_out", "dte_ready"))
        dt_abs, dt_exp, dt_plus, dt_ln = (sem(n) for n in ("dt_abs", "dt_exp", "dt_plus", "dt_ln"))
        conv_in, conv_done, silu_done, tile_turned, tile_out = (sem(n) for n in ("conv_in", "conv_done", "silu_done", "tile_turned", "tile_out"))
        z_done, z_out, ga_out = sem("z_done"), sem("z_out"), sem("ga_out")
        ga_stored = [sem(f"ga_stored{i}") for i in range(2)]
        dtag_ready, seg_done, decay_done, cb_out = (sem(n) for n in ("dtag_ready", "seg_done", "decay_done", "cb_out"))
        xs_dt, xs_dte, xs_skip = sem("xs_dt"), sem("xs_dte"), sem("xs_skip")
        mix_ready, mix_done, state_ready, y_ready = (sem(n) for n in ("mix_ready", "mix_done", "state_ready", "y_ready"))
        gn_squares, gn_var, gn_root, gn_ready, yt_done, yt_out = (
            sem(n) for n in ("gn_squares", "gn_var", "gn_root", "gn_ready", "yt_done", "yt_out"))
        y_stored = [sem(f"y_stored{i}") for i in range(2)]
        act_in = [sem(f"act_in{i}") for i in range(4)]
        gates_in = [sem(f"gates_in{i}") for i in range(2)]
        hi_copied, act_split, act_used, gate_used = (sem(n) for n in ("hi_copied", "act_split", "act_used", "gate_used"))
        diag_made, diag_used, merge_done, merge_out = (sem(n) for n in ("diag_made", "diag_used", "merge_done", "merge_out"))
        res_in = [sem(f"res_in{i}") for i in range(4)]
        x1_made, out_made, out_stored, acc_final = (sem(n) for n in ("x1_made", "out_made", "out_stored", "acc_final"))
        y_var, y_root, x1_square, x1_var, x1_root, x1_scale = (
            sem(n) for n in ("y_var", "y_root", "x1_square", "x1_var", "x1_root", "x1_scale"))
        z_square, z_var, z_root = sem("z_square"), sem("z_var"), sem("z_root")
        up_out, u_squared, u_split, down_done, down_out = (sem(n) for n in ("up_out", "u_squared", "u_split", "down_done", "down_out"))

        block = ctx.enter_context(nc.Block())

        def key_chunks(b):
            return [(k0, min(512, (b + 1) * P - k0)) for k0 in range(0, (b + 1) * P, 512)]

        def spread(ap, n):
            return ap.rearrange("p (h o) -> p h o", o=1).broadcast_to([P, HG, n])

        LOGITS = HI * sum(len(key_chunks(b)) for b in range(NT))

        def meet(e, i):
            e.drain().then_inc(met, 1)
            e.wait_ge(met, 3 * (i + 1))

        def cols(w, c0, n=WC):
            return w[:, bass.ds(c0, n)].rearrange("(k p) c -> p k c", p=P)

        STEPS = 2 * NT
        W3 = "p (k c) -> p k c"

        @block.sync
        def _(sp):
            def load(n, src, dst=None, turn=None, per=0):
                s = n % 2
                if n >= 2 or turn is not None:
                    sp.wait_ge(w_split[s], n // 2 + (0 if turn is None else turn * (per // 2)))
                dst = raw[s][:, :].rearrange(W3, c=WC) if dst is None else dst
                sp.dma_start(dst, src).then_inc(raw_in[s], 16)

            for t in range(NT):
                sp.dma_start(x_tm[:, t, :], x[0, t * P:(t + 1) * P, :]).then_inc(x_landed[t], 16)
            for k in range(KT):
                sp.dma_start(ada0[:, k, :], ada_w[0, k * P:(k + 1) * P, 0:2 * D]).then_inc(ada_in[k], 16)
            w = w_in[0]
            load(0, cols(w, C_KV))
            small_w = raw[1][:, 0:KT * NSM].rearrange(W3, c=NSM)
            sp.dma_start(small_w[:, :, 0:DI + HI], cols(w, C_KI, DI + HI)).then_inc(raw_in[1], 16)
            sp.dma_start(small_w[:, :, DI + HI:NSM], cols(w, C_DT, NS)).then_inc(raw_in[1], 16)
            load(2, cols(w, C_QI))
            load(3, cols(w, C_QI + WC))
            with sp.Fori(0, 2) as i:
                load(4, cols(w, C_Q + i * 2 * WC), turn=i, per=2)
                load(5, cols(w, C_Q + i * 2 * WC + WC), turn=i, per=2)
            for n, w_u in ((N_UK, w_uk), (N_UK + 1, w_uv)):
                load(n, w_u[0].rearrange("(k p) h d -> p k (h d)", p=P),
                     raw[n % 2][:, :].rearrange(W3, c=NH * HD))
            with sp.Fori(0, 2) as i:
                load(N_GS, cols(w, C_GS + i * 2 * WC), turn=i, per=2)
                load(N_GS + 1, cols(w, C_GS + i * 2 * WC + WC), turn=i, per=2)
            sp.wait_ge(unit_done, 2 * NH)
            for s in range(2):
                sp.dma_start(ada_raw[s][:, :, :], cols(ada_w[0], 2 * D + s * WC)).then_inc(ada2_in[s], 16)
            with sp.Fori(0, 7) as i:
                for s in range(2):
                    sp.wait_ge(ada2_used, 2 * i + s + 1)
                    sp.dma_start(ada_raw[s][:, :, :], cols(ada_w[0], (i * 2 + 2 + s) * WC + 2 * D)).then_inc(ada2_in[s], 16)
            for b in range(4):
                sp.wait_ge(spilled[b], 16 * 8)

            def load_head(h, p):
                def one(t):
                    return t[bass.ds(h, 1)].rearrange("a p s -> p (a s)")
                sp.dma_start(hq[p][:, :], one(q_d)).then_inc(head_in[p], 16)
                sp.dma_start(hk[p][:, :], one(k_d)).then_inc(head_in[p], 16)
                sp.dma_start(hv[p][:, :, :], v_d[:, bass.ds(h * P, P)].rearrange("(t p) d -> p t d", p=P)).then_inc(head_in[p], 16)

            sp.wait_ge(ada2_used, 16)
            load_head(0, 0)
            sp.wait_ge(mod0_done, 3)
            load_head(1, 1)
            with sp.Fori(1, NH // 2) as i:
                for p in range(2):
                    sp.wait_ge(pv_done, 4 * i + (2 * p - 2))
                    load_head(i * 2 + p, p)
            with sp.Fori(0, NG) as g:
                def load_g(j, src):
                    n = N_SSM + j
                    sp.wait_ge(w_split[n % 2], g * 3 + n // 2)
                    return sp.dma_start(raw[n % 2][:, :].rearrange(W3, c=WC), src).then_inc(raw_in[n % 2], 16)

                bc = raw[0][:, :].rearrange(W3, c=WC)
                sp.wait_ge(w_split[0], g * 3 + N_SSM // 2)
                sp.dma_start(bc[:, :, 0:P], cols(w, g * P + C_B, P)).then_inc(raw_in[0], 16)
                sp.dma_start(bc[:, :, P:WC], cols(w, g * P + C_C, P)).then_inc(c_cols_in, 16)
                load_g(1, cols(w, g * DG + C_X))
                load_g(2, cols(w, g * DG + (C_X + WC)))
                load_g(3, cols(w, g * DG + C_Z))
                load_g(4, cols(w, g * DG + (C_Z + WC)))
                load_g(5, cols(w, g * WC + C_GA))
            def load_gates(j, tile, turn=None):
                v = 4 * (j - 1)
                if j >= 2 or turn is not None:
                    sp.wait_ge(gate_used, v if turn is None else turn * 16 + v)
                sp.dma_start(gates[j % 2][:, :, :], gate_d[bass.ds(tile, 2)].rearrange("a p s -> p a s")).then_inc(gates_in[j % 2], 16)

            for j in range(4):
                load(N_O + j, cols(w_o_att[0], j * WC))
                if j == 1:
                    for m in range(2):
                        sp.wait_ge(ga_stored[m], 16 * (NG + 1))
                    for k in range(4):
                        sp.dma_start(act_raw[k][:, :], acts_d[k]).then_inc(act_in[k], 16)
                    for m in range(2):
                        sp.wait_ge(y_stored[m], 16 * (2 * NG + 1))
                    load_gates(0, 0)
                    load_gates(1, 2)
                elif j >= 2:
                    load_gates(j, 2 * j)
            with sp.Fori(0, 2) as i:
                rows_o = w_o_ssd[0][bass.ds(i * D, D), :]
                for j in range(4):
                    load(N_O + 4 + j, cols(rows_o, j * WC), turn=i, per=4)
                    load_gates(4 + j, KT + 2 * j, turn=i)
            for j in range(4):
                load(N_OUT + j, cols(w_out[0], j * WC))
            sp.wait_ge(gate_used, 16 * 3)
            for t in range(NT):
                if t >= 4:
                    sp.wait_ge(x1_made, t - 3)
                sp.dma_start(x_in[t % 4][:, :], x[0, t * P:(t + 1) * P, :]).then_inc(res_in[t % 4], 16)
            def down(j):
                return w_down[0][bass.ds(j * WC, WC), :].rearrange("(k p) c -> p k c", p=P)

            def load_down(n, j, turn=None):
                load(n, down(j), raw[n % 2][:, :].rearrange(W3, c=D), turn=turn, per=4)

            load(N_MLP, cols(w_up[0], 0))
            with sp.Fori(0, NC // 2 - 1) as i:
                load(N_MLP + 1, cols(w_up[0], i * 2 * WC + WC), turn=i, per=4)
                load_down(N_MLP + 2, i * 2, turn=i)
                load(N_MLP + 3, cols(w_up[0], i * 2 * WC + 2 * WC), turn=i, per=4)
                load_down(N_MLP + 4, i * 2 + 1, turn=i)
            load(N_ALL - 3, cols(w_up[0], (NC - 1) * WC))
            load_down(N_ALL - 2, NC - 2)
            load_down(N_ALL - 1, NC - 1)
            sp.wait_ge(w_used[0], N_ALL // 2)

            def load_x1(t):
                sp.wait_ge(x_landed[t], 32)
                sp.dma_start(x_in[t % 4][:, :], x1_d[t * P:(t + 1) * P, :]).then_inc(res_in[t % 4], 16)

            for t in range(4):
                load_x1(t)
            for t in range(NT):
                sp.wait_ge(out_made, t + 1)
                if t + 4 < NT:
                    load_x1(t + 4)
                sp.dma_start(out[0, t * P:(t + 1) * P, :], x_tm[:, t, :]).then_inc(out_stored, 16)
            sp.wait_ge(out_stored, 16 * NT)

        @block.gpsimd
        def _(pool):
            nc.gpsimd.memset(ones[:, :], 1.0).then_inc(const_made, 1)
            nc.gpsimd.memset(ident[:, :], 0.0).then_inc(const_made, 1)
            nc.gpsimd.memset(future[:, :], 0.0).then_inc(const_made, 1)
            nc.gpsimd.memset(past_bf[:, :], 0.0).then_inc(const_made, 1)
            pool.wait_ge(const_made, 4)
            nc.gpsimd.affine_select(out=ident[:, :], in_=ident[:, :], compare_op=ALU.not_equal, fill=1.0,
                                    base=0, pattern=[[-1, P]], channel_multiplier=1).then_inc(const_made, 1)
            nc.gpsimd.affine_select(out=tri[:, :], in_=ones[:, :], compare_op=ALU.is_ge, fill=0.0,
                                    base=0, pattern=[[1, P]], channel_multiplier=-1).then_inc(const_made, 1)
            nc.gpsimd.affine_select(out=future[:, :], in_=future[:, :], compare_op=ALU.is_ge, fill=NEG,
                                    base=0, pattern=[[-1, P]], channel_multiplier=1).then_inc(const_made, 1)
            nc.gpsimd.affine_select(out=past_bf[:, :], in_=past_bf[:, :], compare_op=ALU.is_ge, fill=NEG,
                                    base=0, pattern=[[1, P]], channel_multiplier=-1).then_inc(const_made, 1)
            pool.wait_ge(const_made, 8)
            nc.gpsimd.tensor_copy(ident_bf[:, :], ident[:, :]).then_inc(const_made, 1)

            def split(n, width=KT * WC, turn=None, per=2, landed=16):
                s, v = n % 2, n // 2
                if turn is not None:
                    v = turn * (per // 2) + v
                pool.wait_ge(raw_in[s], v * 16 + (landed + (16 if n >= 2 and s == 1 else 0)))
                if n >= 2:
                    pool.wait_ge(w_used[s], v)
                pool.sem_inc(pool_own, 1)
                src, hi, lo = raw[s][:, 0:width], w_hi[s][:, 0:width], w_lo[s][:, 0:width]
                nc.gpsimd.tensor_copy(hi, src).then_inc(hi_made, 1)
                pool.wait_ge(hi_made, n + 1 if turn is None else turn * per + (n + 1))
                nc.gpsimd.tensor_tensor(lo, src, hi.bitcast(F32), ALU.subtract).then_inc(w_split[s], 1)

            split(0)
            split(1, width=KT * NSM, landed=32)
            with pool.Fori(0, (N_SSM - 2) // 2) as i:
                split(2, turn=i)
                split(3, turn=i)
            with pool.Fori(0, NG) as g:
                pool.wait_ge(c_cols_in, g * 16 + 16)
                for j in range(6):
                    split(N_SSM + j, turn=g, per=6)

                def heads(t, k):
                    return spread(t[:, k, bass.ds(g * HG, HG)], PD)

                pool.wait_ge(tile_out, g * 5 + 5)
                for k in range(NT):
                    if k >= 2:
                        pool.wait_ge(mix_done, g * NT + (k - 1))
                    pool.sem_inc(pool_own, 1)
                    xs_k = xs_tm[:, k, :].rearrange("p (h d) -> p h d", h=HG)
                    nc.gpsimd.tensor_tensor(xdt[k % 2][:, :, :], xs_k, heads(dt, k), ALU.mult).then_inc(xs_dt, 1)
                    pool.wait_ge(xs_dt, g * NT + (k + 1))
                    pool.sem_inc(pool_own, 1)
                    nc.gpsimd.tensor_tensor(xde[k % 2][:, :, :], xdt[k % 2][:, :, :], heads(dte, k), ALU.mult).then_inc(xs_dte, 1)
                    nc.gpsimd.tensor_tensor(xs_k, xs_k, spread(skip_row[:, bass.ds(g * HG, HG)], PD), ALU.mult).then_inc(xs_skip, 1)
            with pool.Fori(0, (N_ALL - N_O) // 2) as i:
                split(N_O, turn=i)
                split(N_O + 1, turn=i)
            pool.wait_ge(pool_own, N_ALL + NG * NT * 2)

        @block.tensor
        def _(pe):
            def w_tile(t, s, k, c0, c1, width=WC):
                return t[s][:, k * width + c0:k * width + c1]

            def w_wait(n, extra=0):
                pe.wait_ge(w_split[n % 2], n // 2 + 1 + extra)

            def mm(o, a, b, start=False, stop=False):
                return nc.tensor.matmul(o, a, b, start=start, stop=stop)

            def fm_block(n, group, extra=0, act_ready=None, act_used=None):
                s = n % 2
                w_wait(n, extra)
                for k in range(KT):
                    if act_ready is not None:
                        act_ready(k)
                    for m in range(2):
                        wh = w_tile(w_hi, s, k, m * P, m * P + P)
                        wl = w_tile(w_lo, s, k, m * P, m * P + P)
                        for q in range(2):
                            o = ps[:, 4 * group + 2 * m + q, :]
                            r = slice(q * 512, q * 512 + 512)
                            mm(o, wh, a_hi[:, k, r], start=(k == 0))
                            mm(o, wh, a_lo[:, k, r])
                        for q in range(2):
                            last = mm(ps[:, 4 * group + 2 * m + q, :], wl, a_hi[:, k, q * 512:q * 512 + 512],
                                      stop=(k == KT - 1))
                    if act_used is not None:
                        last = act_used(k, last)
                return last

            def tm_token(n, t, o, width, stationary=None, nk=KT, c0=0, wwidth=None):
                s = n % 2
                sh, sl = stationary or (a_hi, a_lo)
                ww = wwidth or width
                for k in range(nk):
                    r = slice(t * P, t * P + P)
                    wh, wl = (w_tile(w, s, k, c0, c0 + width, ww) for w in (w_hi, w_lo))
                    mm(o, sh[:, k, r], wh, start=(k == 0))
                    mm(o, sh[:, k, r], wl)
                    last = mm(o, sl[:, k, r], wh, stop=(k == nk - 1))
                return last

            def norm_turn(j):
                for i in range(2 * KT):
                    g, k = divmod(i, KT)
                    pe.wait_ge(normed, 8 * j + 4 * (g + 1))
                    if i >= 4:
                        pe.wait_ge(h_ready, 16 * j + i - 3)
                    for t in range(4):
                        last = nc.tensor.transpose(ps[:, 4 + i % 4, t * P:(t + 1) * P],
                                                   x_tm[:, 4 * g + t, k * P:(k + 1) * P], ident[:, :])
                    last.then_inc(turned, 1)

            pe.wait_ge(const_made, 9)
            pe.wait_ge(small_in, 16 * 6)
            nc.tensor.transpose(ps[:, 0, 0:112], rows_a[:, :], ident[0:112, 0:112])
            nc.tensor.transpose(ps[:, 1, 0:112], rows_b[:, :], ident[0:112, 0:112]).then_inc(vec_turned, 1)
            pe.wait_ge(c_ready, 1)
            for k in range(KT):
                pe.wait_ge(ada_in[k], 16)
                for q in range(4):
                    last = mm(ps[0:1, q, :], c_act[:, k:k + 1], ada0[:, k, q * 512:q * 512 + 512],
                              start=(k == 0), stop=(k == KT - 1))
            last.then_inc(mod0_done, 1)
            pe.wait_ge(row_out, 1)
            for m in range(2 * KT):
                last = mm(ps[:, 4, m:m + 1], mod_row[0:1, m * P:(m + 1) * P], ones[0:1, 0:1], start=True, stop=True)
            last.then_inc(mod0_done, 1)
            pe.wait_ge(c_ready, 2)
            norm_turn(0)
            meet(pe, 0)

            w_wait(0)
            for t in range(NT):
                last = tm_token(0, t, ps[:, t // 2, (t % 2) * R:(t % 2) * R + R], R)
            last.then_inc(w_used[0], 1)
            w_wait(1)
            for t in range(NT):
                last = tm_token(1, t, ps[:, 4 + t // 4, (t % 4) * NSM:(t % 4) * NSM + NSM], NSM)
            last.then_inc(w_used[1], 1)
            for b in range(2):
                pe.wait_ge(kv_read, b + 1)
                fm_block(2 + b, b).then_inc(w_used[b], 1)
            pe.wait_ge(qi_out, 2)
            for t in range(NT):
                last = nc.tensor.transpose(ps[:, t // 4, (t % 4) * P:(t % 4 + 1) * P], kidx_tm[:, t, :], ident[:, :])
            last.then_inc(kv_turned, 1)
            pe.wait_ge(qi_out, 4)
            for r in range(2):
                for t in range(NT):
                    last = nc.tensor.transpose(ps[:, 4 + 2 * r + t // 4, (t % 4) * P:(t % 4 + 1) * P],
                                               ckv_tm[:, t, r * P:(r + 1) * P], ident[:, :])
            last.then_inc(kv_turned, 1)
            pe.wait_ge(k_idx_out, 1)
            i = 0
            for b in range(NT):
                for k0 in range(0, (b + 1) * P, 512):
                    n = min(512, (b + 1) * P - k0)
                    for h in range(HI):
                        if i >= 4:
                            pe.wait_ge(relu_done, i - 3)
                        mm(ps[:, i % 4, 0:n], q_idx[:, h // 2, b * P:(b + 1) * P], k_idx_half[h % 2][:, k0:k0 + n],
                           start=True, stop=True).then_inc(logit_done, 1)
                        i += 1

            pe.wait_ge(relu_done, LOGITS)
            def fm_unit_blocks(n, u, turns):
                with pe.Fori(0, turns) as i:
                    for j in range(2):
                        first = u + 2 * j
                        pe.wait_ge(unit_out, i * 4 + (first - 2) if first >= 2 else i * 4)
                        fm_block(n + j, (first % 4) // 2, extra=i).then_inc(w_used[(n + j) % 2], 1)

            fm_block(4, 0).then_inc(w_used[0], 1)
            pe.wait_ge(kv_out_split, 2)
            fm_block(5, 1).then_inc(w_used[1], 1)
            pe.wait_ge(unit_out, 2)
            fm_block(6, 0).then_inc(w_used[0], 1)
            pe.wait_ge(unit_out, 4)
            fm_block(7, 1).then_inc(w_used[1], 1)
            u = 8
            s = N_UK % 2
            w_wait(N_UK)
            for h in range(NH):
                pe.wait_ge(unit_out, u - 3)
                for q in range(2):
                    o = ps[:, 2 * (u % 4) + q, :]
                    r = slice(q * 512, q * 512 + 512)
                    for k in range(2):
                        wh, wl = (w_tile(t, s, k, h * P, h * P + P, NH * HD) for t in (w_hi, w_lo))
                        mm(o, wh, ckv_hi[:, k, r], start=(k == 0))
                        mm(o, wh, ckv_lo[:, k, r])
                        last = mm(o, wl, ckv_hi[:, k, r], stop=(k == 1))
                last.then_inc(unit_done, 1)
                u += 1
            pe.drain().then_inc(w_used[0], 1)
            w_wait(N_UK + 1)
            for t in range(NT):
                pe.wait_ge(unit_out, u - 3)
                for q in range(2):
                    last = tm_token(N_UK + 1, t, ps[:, 2 * (u % 4) + q, :], 512, (ckv_hi, ckv_lo), 2, q * 512, NH * HD)
                last.then_inc(unit_done, 1)
                u += 1
            pe.drain().then_inc(w_used[1], 1)
            fm_unit_blocks(N_GS, u, 2)
            pe.wait_ge(unit_out, 32)
            with pe.Fori(0, 8) as i:
                for s in range(2):
                    pe.wait_ge(ada2_in[s], i * 16 + 16)
                    for k in range(KT):
                        last = mm(ps[0:1, bass.ds(i, 1), s * WC:s * WC + WC], c_act[:, k:k + 1], ada_raw[s][:, k, :],
                                  start=(k == 0), stop=(k == KT - 1))
                    last.then_inc(ada2_used, 1)
            pe.wait_ge(row_out, 2)
            for m in range(4 * KT):
                last = mm(ps[:, 0, m:m + 1], mod_row[0:1, m * P:(m + 1) * P], ones[0:1, 0:1], start=True, stop=True)
            last.then_inc(mod0_done, 1)
            meet(pe, 1)

            pe.wait_ge(dta_ready, 1)
            flat = "p c h -> p (c h)"
            mm(ps[:, 6, 0:NT * NS], tri[:, :], dta[:, :, :].rearrange(flat), start=True, stop=True)
            mm(ps[:, 7, 0:NT * NS], ones[:, :], dta[:, :, :].rearrange(flat), start=True, stop=True).then_inc(acum_done, 1)
            def attend(i, positions, turns, last=False):
                for t in positions:
                    if t < STEPS or not last:
                        p, b = t // NT % 2, t % NT
                        if b == 0:
                            pe.wait_ge(head_in[p], i * 48 + 48 * (1 + t // STEPS))
                        if t >= 2:
                            pe.wait_ge(masked, i * STEPS + (t - 1))
                        for j, (k0, n) in enumerate(key_chunks(b)):
                            ins = mm(ps[:, 2 * (t % 2) + j, 0:n], hq[p][:, b * P:(b + 1) * P], hk[p][:, k0:k0 + n],
                                     start=True, stop=True)
                        ins.then_inc(qk_done, 1)
                    if t >= 6 and (t - 3) % 4 == 3:
                        g = (t - 3) // 4
                        p, half = divmod(g, 2)
                        pe.wait_ge(pt_out, i * 24 + 12 * p + (4, 12)[half])
                        if g >= 2:
                            pe.wait_ge(pv_out, i * 4 + (g - 1))
                        nk = 4 * half + 4
                        for k in range(nk):
                            q0 = max(0, k - 4 * half) * P
                            ins = mm(ps[:, 6 + g % 2, q0:512], hv[p][:, k, :], probT[g % 2][:, k, q0:512],
                                     start=(k == 0), stop=(k == nk - 1))
                        ins.then_inc(pv_done, 1)
                    if t >= 2 and (t < STEPS + 2 or not last):
                        b = (t - 2) % NT
                        pe.wait_ge(p_ready, i * STEPS + (t - 1))
                        for k in range(b + 1):
                            if k % 4 == 0 and turns >= 2:
                                pe.wait_ge(pt_out, i * 24 + (turns - 1))
                            ins = nc.tensor.transpose(ps[:, 4 + turns % 2, (k % 4) * P:(k % 4 + 1) * P],
                                                      prob[(t - 2) % 4][:, k * P:(k + 1) * P], ident[:, :])
                            if k % 4 == 3 or k == b:
                                ins.then_inc(pt_done, 1)
                                turns += 1

            attend(0, range(3), 0)
            with pe.Fori(0, NH // 2 - 1) as i:
                attend(i, range(3, STEPS + 3), 1)
            attend(NH // 2 - 1, range(3, STEPS + 3), 1, last=True)
            meet(pe, 2)

            with pe.Fori(0, NG) as g:
                def turn_tile(r, src):
                    pe.wait_ge(silu_done, g * 6 + (1, 3, 4, 5, 6)[r])
                    if r >= 2:
                        pe.wait_ge(tile_out, g * 5 + (r - 1))
                    for t in range(NT):
                        last = nc.tensor.transpose(ps[:, 2 * (r % 2) + t // 4, (t % 4) * P:(t % 4 + 1) * P],
                                                   src[:, t * P:(t + 1) * P], ident[:, :])
                    last.then_inc(tile_turned, 1)

                def z_block(j):
                    n = N_SSM + 3 + j
                    w_wait(n, g * 3)
                    for t in range(NT):
                        v = NT * j + t
                        if v >= 4:
                            pe.wait_ge(z_out, g * 16 + (v - 3))
                        last = tm_token(n, t, ps[:, 4 + v % 4, 0:WC], WC)
                        last.then_inc(z_done, 1)
                    pe.drain().then_inc(w_used[n % 2], 1)

                fm_block(N_SSM, 0, extra=g * 3).then_inc(w_used[0], 1)
                pe.wait_ge(yt_out, g * 4 + 4)
                fm_block(N_SSM + 1, 1, extra=g * 3).then_inc(w_used[1], 1)
                pe.wait_ge(conv_in, g * 6 + 2)
                fm_block(N_SSM + 2, 0, extra=g * 3).then_inc(w_used[0], 1)
                pe.wait_ge(conv_in, g * 6 + 4)
                z_block(0)
                pe.wait_ge(conv_in, g * 6 + 6)
                turn_tile(0, b_fm)
                turn_tile(1, c_out[0])
                turn_tile(2, c_out[1])
                z_block(1)
                turn_tile(3, c_out[0])
                turn_tile(4, c_out[1])
                pe.wait_ge(tile_out, g * 5 + 5)
                pe.wait_ge(dtag_ready, g + 1)

                def segments(k):
                    if k >= 1:
                        pe.wait_ge(cb_out, g * NT + k)
                    r = slice(k * P, k * P + P)
                    mm(ps[:, 7, 0:P], b_fm[:, r], c_fm[:, r], start=True, stop=True)
                    if k >= 1:
                        pe.wait_ge(decay_done, g * NT + k)
                    for j in range(2):
                        o = ps[:, j, :]
                        mm(o.rearrange("p (h l) -> p h l", h=4), ident_bf[:, :],
                           past_bf[:, :].rearrange("p (o l) -> p o l", o=1).broadcast_to([P, 4, P]), start=True)
                        for h in range(4):
                            last = mm(o[:, h * P:(h + 1) * P],
                                      dta_g[:, k, 4 * j + h:4 * j + h + 1].broadcast_to([P, P]), tri[:, :], stop=(h == 3))
                    last.then_inc(seg_done, 1)

                segments(0)
                segments(1)
                for k in range(NT):
                    pe.wait_ge(mix_ready, g * NT + (k + 1))
                    pe.wait_ge(xs_dte, g * NT + (k + 1))
                    if k >= 2:
                        pe.wait_ge(y_ready, g * NT + (k - 1))
                    for h in range(HG):
                        mm(ps[:, 2 + 2 * (k % 2), h * PD:(h + 1) * PD], decay[k % 2][:, h, :], xdt[k % 2][:, h, :], start=True, stop=True)
                    if k >= 1:
                        pe.wait_ge(state_ready, g * 7 + k)
                        mm(ps[:, 3 + 2 * (k % 2), :], c_fm[:, k * P:(k + 1) * P], state[:, :, :].rearrange("p h d -> p (h d)"),
                           start=True, stop=True)
                    mm(ps[:, 6, :], b_tm[:, k, :], xde[k % 2][:, :, :].rearrange("p h d -> p (h d)"),
                       start=True, stop=True).then_inc(mix_done, 1)
                    if k + 2 < NT:
                        segments(k + 2)
                pe.wait_ge(y_ready, g * NT + NT - 1)
                fm_block(N_SSM + 5, 0, extra=g * 3).then_inc(w_used[1], 1)
                pe.wait_ge(y_ready, g * NT + NT)
                for f in range(4):
                    if f == 0:
                        pe.wait_ge(gn_ready, g * NT + NT)
                    if f >= 2:
                        pe.wait_ge(yt_out, g * 4 + (f + 3))
                    for t in range(NT):
                        last = nc.tensor.transpose(ps[:, 4 + 2 * (f % 2) + t // 4, (t % 4) * P:(t % 4 + 1) * P],
                                                   zy[:, t, f * P:(f + 1) * P], ident[:, :])
                    last.then_inc(yt_done, 1)
                pe.wait_ge(ga_out, g * 2 + 2)

            def out_block(n, j, o, turn=None):
                def at_turn(v, per):
                    return v if turn is None else turn * per + v
                v = 4 * (4 * o + j - 1)
                if 4 * o + j >= 2:
                    pe.wait_ge(gate_used, at_turn(v, 16))
                ready = (lambda k: pe.wait_ge(act_split, at_turn(8 * o + k + 1, 8))) if j == 0 else None
                used = (lambda k, ins: ins.then_inc(act_used, 1)) if j == 3 else None
                last = fm_block(n, j % 2, extra=0 if turn is None else turn * 2, act_ready=ready, act_used=used)
                if j == 3:
                    pe.drain().then_inc(w_used[n % 2], 1)
                else:
                    last.then_inc(w_used[n % 2], 1)

            for j in range(4):
                out_block(N_O + j, j, 0)
            with pe.Fori(0, 2) as i:
                for j in range(4):
                    out_block(N_O + 4 + j, j, 1, turn=i)
            pe.wait_ge(gate_used, 44)
            pe.wait_ge(diag_made, 1)
            for i in range(2 * KT):
                ins = mm(ps[:, i // 4, (i % 4) * P:(i % 4 + 1) * P], ones[:, :], diag[:, i, :], start=True, stop=True)
            ins.then_inc(diag_used, 1)
            meet(pe, 3)
            pe.wait_ge(act_split, 4 * KT)
            for j in range(4):
                n = N_OUT + j
                w_wait(n)
                for t in range(NT):
                    if j:
                        pe.wait_ge(merge_out, 8 * j + t - 7)
                    last = tm_token(n, t, ps[:, t, 0:WC], WC)
                    last.then_inc(merge_done, 1)
                pe.drain().then_inc(w_used[n % 2], 1)
            pe.wait_ge(merge_out, 32)
            norm_turn(1)
            pe.wait_ge(h_split, 4 * KT)

            def up(n, c, extra=0):
                if c is not None:
                    pe.wait_ge(up_out, c * 4)
                fm_block(n, 0, extra=extra).then_inc(w_used[n % 2], 1)

            def down(n, c, b, extra=0, first=False):
                w_wait(n, extra)
                pe.wait_ge(u_split, c * 4 + 4)
                for t in range(NT):
                    if t >= 2 or not first:
                        pe.wait_ge(down_out, c * 8 + (t - 1))
                    for q in range(2):
                        last = tm_token(n, t, ps[:, 4 + 2 * (t % 2) + q, :], 512, (u_hi[b], u_lo[b]), 2, q * 512, D)
                    last.then_inc(down_done, 1)
                pe.drain().then_inc(w_used[n % 2], 1)

            up(N_MLP, None)
            up(N_MLP + 1, 1)
            down(N_MLP + 2, 0, 0, first=True)
            up(N_MLP + 3, 2)
            down(N_MLP + 4, 1, 1)
            with pe.Fori(1, NC // 2 - 1) as i:
                up(N_MLP + 1, i * 2 + 1, extra=i * 2)
                down(N_MLP + 2, i * 2, 0, extra=i * 2)
                up(N_MLP + 3, i * 2 + 2, extra=i * 2)
                down(N_MLP + 4, i * 2 + 1, 1, extra=i * 2)
            up(N_ALL - 3, NC - 1)
            down(N_ALL - 2, NC - 2, 0)
            down(N_ALL - 1, NC - 1, 1)

        @block.scalar
        def _(act):
            A = Count(act, act_own)

            def norm_evac(j, shift):
                for i in range(2 * KT):
                    k = i % KT
                    act.wait_ge(turned, 16 * j + i + 1)
                    if i >= 4:
                        act.wait_ge(h_split, 16 * j + i - 3)
                    if i == 0 and j == 0:
                        act.wait_ge(gain_ready, 1)
                    g = i // KT
                    for dst in (a_hi[:, k, g * 512:g * 512 + 512], h_tmp[i % 4][:, :])[i % 2:]:
                        ins = nc.scalar.activation(dst, ps[:, 4 + i % 4, :], ACT.Identity,
                                                   bias=mod[:, shift + k:shift + k + 1],
                                                   scale=gain[:, j * KT + k:j * KT + k + 1])
                    ins.then_inc(h_ready, 1)

            def rows(t):
                return t.rearrange("(a p) -> a p", p=P)

            act.dma_start(rows_a[0:48, :], rows(ada_b[0])).then_inc(small_in, 16)
            act.dma_start(rows_a[48:56, :], rows(c[0])).then_inc(small_in, 16)
            act.dma_start(rows_a[56:88, :], norm_g[0].rearrange("j (a p) -> (j a) p", p=P)).then_inc(small_in, 16)
            act.dma_start(rows_a[88:112, :], rows(conv_b[0])).then_inc(small_in, 16)
            act.dma_start(rows_b[0:96, :], conv_w[0].rearrange("j (a p) -> (j a) p", p=P)).then_inc(small_in, 16)
            act.dma_start(rows_b[96:112, :], rows(ssm_norm_g[0])).then_inc(small_in, 16)
            for dst, src, n in ((kv_row, kv_norm_g, R), (ki_row, kidx_norm_g, DI), (dtb_row, dt_bias, NS),
                                (alog_row, a_log, NS), (skip_row, d_skip, NS)):
                act.dma_start(dst[:, :], src[0:1, :].broadcast_to([P, n])).then_inc(rows_in, 16)
            act.wait_ge(vec_turned, 1)
            A.add(nc.scalar.copy(vec_a[:, :], ps[:, 0, 0:112]))
            A.link(nc.scalar.copy(vec_b[:, :], ps[:, 1, 0:112]))
            nc.scalar.activation(c_act[:, :], vec_a[:, 48:56], ACT.Silu).then_inc(c_ready, 1)
            for t in range(NT):
                act.wait_ge(x_landed[t], 16)
                A.link(nc.scalar.activation(sq0[:, :], x_tm[:, t, :], ACT.Square, accum_out=stat[:, t:t + 1]))
            act.sem_inc(squares, 1)
            act.wait_ge(vars_ready, 1)
            nc.scalar.activation(stat[:, 0:NT], stat[:, 0:NT], ACT.Sqrt).then_inc(roots, 1)
            act.wait_ge(mod0_done, 1)
            nc.scalar.copy(mod_row[0:1, 0:2 * D].rearrange("p (a b) -> p a b", a=4), ps[0:1, 0:4, :]).then_inc(row_out, 1)
            act.wait_ge(mod0_done, 2)
            nc.scalar.copy(mod[:, 0:16], ps[:, 4, 0:16]).then_inc(c_ready, 1)
            norm_evac(0, 0)
            meet(act, 0)

            act.wait_ge(w_used[0], 1)
            for t in range(NT):
                A.link(nc.scalar.activation(sq0[:, 512:512 + R], ps[:, t // 2, (t % 2) * R:(t % 2) * R + R], ACT.Square,
                                            accum_out=stat[:, 64 + t:65 + t]))
            act.sem_inc(kv_sq, 1)
            act.wait_ge(kv_var, 1)
            nc.scalar.activation(stat[:, 64:72], stat[:, 64:72], ACT.Sqrt).then_inc(kv_root, 1)
            act.wait_ge(w_used[1], 1)
            for g in range(2):
                ins = nc.scalar.activation(sq0[:, g * 256:g * 256 + 256].rearrange("p (t c) -> p t c", t=4),
                                           ps[:, 4 + g, 0:4 * NSM].rearrange("p (t c) -> p t c", t=4)[:, :, 0:DI], ACT.Square)
            ins.then_inc(kv_sq, 1)
            act.wait_ge(kv_var, 2)
            nc.scalar.activation(stat[:, 72:80], stat[:, 72:80], ACT.Sqrt).then_inc(kv_root, 1)
            for b in range(2):
                act.wait_ge(w_used[b], 2)
                for m in range(2):
                    nc.scalar.copy(q_idx[:, 2 * b + m, :].rearrange("p (a b) -> p a b", a=2),
                                   ps[:, 4 * b + 2 * m:4 * b + 2 * m + 2, :]).then_inc(qi_out, 1)
            act.wait_ge(kv_turned, 1)
            for i in range(2):
                half = slice(DI * i, DI * i + DI)
                ins = nc.scalar.copy(k_idx_half[i][half, :].rearrange("p (a b) -> p a b", a=2), ps[half, 0:2, :])
            ins.then_inc(k_idx_out, 1)
            act.wait_ge(kv_turned, 2)
            for r in range(2):
                nc.scalar.copy(ckv_hi[:, r, :].rearrange("p (a b) -> p a b", a=2), ps[:, 4 + 2 * r:6 + 2 * r, :]).then_inc(kv_out, 1)
            i = 0
            for b in range(NT):
                for k0 in range(0, (b + 1) * P, 512):
                    n = min(512, (b + 1) * P - k0)
                    for h in range(HI):
                        act.wait_ge(logit_done, i + 1)
                        if i >= 4:
                            act.wait_ge(relu_used, i - 3)
                        nc.scalar.activation(relu_buf[:, i % 4, 0:n], ps[:, i % 4, 0:n], ACT.Relu).then_inc(relu_done, 1)
                        i += 1

            def unit(u, func, dst, turn=None, per=0):
                b = u % 4
                if u >= 4 or turn is not None:
                    act.wait_ge(spilled[b], 16 * (u // 4) + (0 if turn is None else turn * (4 * per)))
                nc.scalar.activation(spill[b][:, :].rearrange("p (a b) -> p a b", a=2),
                                     ps[:, 2 * b:2 * b + 2, :], func).then_inc(unit_out, 1)
                act.wait_ge(unit_out, u + 1 + (0 if turn is None else turn * per))
                act.dma_start(dst, spill[b][:, :]).then_inc(spilled[b], 16)

            def fm_units(n, u, func, dst, turns):
                with act.Fori(0, turns) as i:
                    for j in range(4):
                        if j % 2 == 0:
                            act.wait_ge(w_used[(n + j // 2) % 2], (n + j // 2) // 2 + 1 + i)
                        unit(u + j, func, dst(i, j), turn=i, per=4)

            act.wait_ge(rows_in, 16 * 5)
            flat = "p c h -> p (c h)"
            act.wait_ge(dt_abs, 1)
            nc.scalar.activation(ea[:, :, :], acum[:, :, :], ACT.Exp, scale=-1.0).then_inc(dt_exp, 1)
            nc.scalar.activation(alog_row[:, :], alog_row[:, :], ACT.Exp).then_inc(dt_exp, 1)
            act.wait_ge(relu_used, LOGITS)
            for j in range(8):
                if j % 2 == 0:
                    act.wait_ge(w_used[(j // 2) % 2], 3 + j // 4)
                unit(j, ACT.Copy, q_d[j])
            for u in range(8, 24):
                act.wait_ge(unit_done, u - 7)
                unit(u, ACT.Copy, k_d[u - 8] if u < 16 else v_d[(u - 16) * P:(u - 15) * P, :])
            act.wait_ge(dt_plus, 1)
            nc.scalar.activation(dec[:, :, :], dte[:, :, :], ACT.Ln).then_inc(dt_ln, 1)
            fm_units(N_GS, 24, ACT.Sigmoid, lambda i, j: gate_d[bass.ds(i * 4 + (KT + j), 1)].rearrange("a p s -> p (a s)"), 2)
            act.wait_ge(ada2_used, 16)
            for b in range(4):
                act.wait_ge(spilled[b], 16 * 8)
            nc.scalar.copy(mod_row[0:1, :].rearrange("p (a b) -> p a b", a=8), ps[0:1, :, :]).then_inc(row_out, 1)
            act.wait_ge(mod0_done, 3)
            nc.scalar.copy(mod[:, 16:48], ps[:, 0, 0:32]).then_inc(mod_ready, 1)
            meet(act, 1)

            act.wait_ge(acum_done, 1)
            nc.scalar.activation(acum[:, :, :].rearrange(flat), ps[:, 6, 0:NT * NS], ACT.Copy, scale=-1.0).then_inc(aend_out, 1)
            nc.scalar.activation(ea[:, :, :].rearrange(flat), ps[:, 6, 0:NT * NS], ACT.Exp).then_inc(aend_out, 1)
            nc.scalar.activation(dec[:, :, :].rearrange(flat), ps[:, 7, 0:NT * NS], ACT.Exp).then_inc(aend_out, 1)
            act.wait_ge(dte_ready, 1)
            nc.scalar.activation(dte[:, :, :], dte[:, :, :], ACT.Exp)
            def attend(i, positions, turns, last=False):
                for t in positions:
                    if t < STEPS or not last:
                        n = (t % NT + 1) * P
                        act.wait_ge(masked, i * STEPS + (t + 1))
                        st = 4 * (t % 4)
                        nc.scalar.activation(prob[t % 4][:, 0:n], prob[t % 4][:, 0:n], ACT.Exp, scale=SCALE,
                                             bias=att_stat[:, st + 1:st + 2],
                                             accum_out=att_stat[:, st + 2:st + 3]).then_inc(exp_done, 1)
                    if t >= 6 and (t - 3) % 4 == 3:
                        g = (t - 3) // 4
                        act.wait_ge(pv_done, i * 4 + (g + 1))
                        act.wait_ge(att_stored, i * 64 + 16 * (g + 1))
                        nc.scalar.copy(att_o[:, :], ps[:, 6 + g % 2, :]).then_inc(pv_out, 1)
                        act.wait_ge(pv_out, i * 4 + (g + 1))
                        dst = acts_d[bass.ds(i * 2 + g // 2, 1)].rearrange("a p s -> p (a s)")
                        act.dma_start(dst[:, (g % 2) * 512:(g % 2) * 512 + 512], att_o[:, :]).then_inc(att_stored, 16)
                    if t >= 2 and (t < STEPS + 2 or not last):
                        b = (t - 2) % NT
                        g = (t - 2) // 4
                        q0 = (b % 4) * P
                        for k0 in range(0, b + 1, 4):
                            m = min(4, b + 1 - k0)
                            act.wait_ge(pt_done, i * 24 + (turns + 1))
                            if g >= 2:
                                act.wait_ge(pv_done, i * 4 + (g - 1))
                            nc.scalar.copy(probT[g % 2][:, k0:k0 + m, q0:q0 + P],
                                           ps[:, 4 + turns % 2, 0:m * P].rearrange("p (k q) -> p k q", k=m)).then_inc(pt_out, 1)
                            turns += 1

            act.sem_inc(att_stored, 16)
            attend(0, range(3), 0)
            with act.Fori(0, NH // 2 - 1) as i:
                attend(i, range(3, STEPS + 3), 1)
            attend(NH // 2 - 1, range(3, STEPS + 3), 1, last=True)
            act.wait_ge(att_stored, 16 * (2 * NH + 1))
            meet(act, 2)

            act.sem_inc(yt_out, 4)
            for m in range(2):
                act.sem_inc(ga_stored[m], 16)
                act.sem_inc(y_stored[m], 16)
            with act.Fori(0, NG) as g:
                def evac(T):
                    if T >= 2:
                        act.wait_ge(conv_done, g * 6 + (T - 1))
                    else:
                        act.wait_ge(ga_stored[T], g * 16 + 16)
                        act.wait_ge(y_stored[T], g * 32 + 16)
                    nc.scalar.copy(c_in[T % 2][:, TAPS - 1:TAPS - 1 + SEQ].rearrange("p (a b) -> p a b", a=2),
                                   ps[:, 2 * (T % 4):2 * (T % 4) + 2, :]).then_inc(conv_in, 1)

                def silu(T):
                    act.wait_ge(conv_done, g * 6 + (T + 1))
                    dst = (b_fm, c_fm, *c_out, *c_out)[T]
                    col = (g + (88 + 16), g + (88 + 20))[T] if T < 2 else g * 4 + (88 + T - 2)
                    nc.scalar.activation(dst[:, :], c_out[T % 2][:, :], ACT.Silu,
                                         bias=vec_a[:, bass.ds(col, 1)]).then_inc(silu_done, 1)

                def z_evac(j):
                    for t in range(NT):
                        v = NT * j + t
                        act.wait_ge(z_done, g * 16 + (v + 1))
                        nc.scalar.activation(zy[:, t, WC * j:WC * j + WC], ps[:, 4 + v % 4, 0:WC], ACT.Silu).then_inc(z_out, 1)

                def tile_evac(r):
                    act.wait_ge(tile_turned, g * 5 + (r + 1))
                    dst = b_tm[:, :, :] if r == 0 else xs_tm[:, :, (r - 1) * P:r * P]
                    nc.scalar.copy(dst, ps[:, 2 * (r % 2):2 * (r % 2) + 2, :].rearrange("p a (b f) -> p (a b) f", f=P)).then_inc(tile_out, 1)

                act.wait_ge(w_used[0], g * 3 + (N_SSM // 2 + 1))
                evac(0)
                evac(1)
                silu(0)
                silu(1)
                act.wait_ge(w_used[1], g * 3 + (N_SSM // 2 + 1))
                evac(2)
                evac(3)
                silu(2)
                silu(3)
                act.wait_ge(w_used[0], g * 3 + (N_SSM // 2 + 2))
                evac(4)
                evac(5)
                z_evac(0)
                tile_evac(0)
                tile_evac(1)
                tile_evac(2)
                silu(4)
                silu(5)
                z_evac(1)
                tile_evac(3)
                tile_evac(4)
                def squares_of(k):
                    act.wait_ge(y_ready, g * NT + (k + 1))
                    nc.scalar.activation(c_out[k % 2][:, 0:DG], zy[:, k, :], ACT.Square,
                                         accum_out=stat[:, 96 + k:97 + k]).then_inc(gn_squares, 1)
                    act.wait_ge(gn_squares, g * NT + (k + 1))

                for k in range(NT):
                    act.wait_ge(seg_done, g * NT + (k + 1))
                    if k >= 1:
                        act.wait_ge(mix_ready, g * NT + k)
                    nc.scalar.copy(cb_sb[:, :], ps[:, 7, 0:P]).then_inc(cb_out, 1)
                    if k >= 2:
                        act.wait_ge(mix_done, g * NT + (k - 1))
                    for h in range(HG):
                        ins = nc.scalar.activation(decay[k % 2][:, h, :], ps[:, h // 4, (h % 4) * P:(h % 4 + 1) * P], ACT.Exp,
                                                   bias=acum[:, k, bass.ds(g * HG + h, 1)])
                    ins.then_inc(decay_done, 1)
                    if k >= 2:
                        squares_of(k - 2)
                squares_of(NT - 2)
                squares_of(NT - 1)
                act.wait_ge(gn_var, g + 1)
                nc.scalar.activation(stat[:, 96:104], stat[:, 96:104], ACT.Sqrt).then_inc(gn_root, 1)
                act.wait_ge(w_used[1], g * 3 + (N_SSM // 2 + 3))
                for m in range(2):
                    nc.scalar.activation(c_in[m][:, TAPS - 1:TAPS - 1 + SEQ].rearrange("p (a b) -> p a b", a=2),
                                         ps[:, 2 * m:2 * m + 2, :], ACT.Sigmoid).then_inc(ga_out, 1)
                for m in range(2):
                    act.wait_ge(ga_out, g * 2 + (m + 1))
                    act.dma_start(gate_d[bass.ds(g * 2 + m, 1)].rearrange("a p s -> p (a s)"),
                                  c_in[m][:, TAPS - 1:TAPS - 1 + SEQ]).then_inc(ga_stored[m], 16)
                for f in range(4):
                    act.wait_ge(yt_done, g * 4 + (f + 1))
                    if f >= 2:
                        act.wait_ge(y_stored[f % 2], g * 32 + 32)
                    nc.scalar.activation(c_out[f % 2][:, :].rearrange("p (a b) -> p a b", a=2),
                                         ps[:, 4 + 2 * (f % 2):6 + 2 * (f % 2), :], ACT.Copy,
                                         scale=vec_b[:, bass.ds(g * 4 + (96 + f), 1)]).then_inc(yt_out, 1)
                    act.wait_ge(yt_out, g * 4 + (f + 5))
                    act.dma_start(acts_d[bass.ds(g * 4 + (KT + f), 1)].rearrange("a p s -> p (a s)"),
                                  c_out[f % 2][:, :]).then_inc(y_stored[f % 2], 16)

            def act_load(k, tile):
                act.dma_start(act_raw[k % 4][:, :], acts_d[bass.ds(tile, 1)].rearrange("a p s -> p (a s)")).then_inc(act_in[k % 4], 16)

            for k in range(KT):
                act.wait_ge(act_in[k % 4], 16 * (k // 4 + 1))
                nc.scalar.copy(a_hi[:, k, :], act_raw[k % 4][:, :]).then_inc(hi_copied, 1)
                if 1 <= k < KT - 3:
                    act.wait_ge(act_split, k)
                    act_load(k + 3, k + 3)
            for m in range(2):
                act.wait_ge(y_stored[m], 16 * (2 * NG + 1))
            with act.Fori(0, 2) as i:
                for k in range(4):
                    act.wait_ge(act_split, i * 8 + (KT - 3 + k))
                    act_load(k, i * 8 + (KT + k))
                for k in range(KT):
                    act.wait_ge(act_used, i * 8 + (k + 1))
                    act.wait_ge(act_in[k % 4], i * 32 + (32 + 16 * (k // 4 + 1)))
                    nc.scalar.copy(a_hi[:, k, :], act_raw[k % 4][:, :]).then_inc(hi_copied, 1)
                    if 1 <= k < KT - 3:
                        act.wait_ge(act_split, i * 8 + (8 + k))
                        act_load(k + 3, i * 8 + (8 + k + 3))
            for k in range(KT):
                act.wait_ge(act_used, 2 * KT + k + 1)
                act.wait_ge(acc_final, 1 if k < KT - 2 else 2)
                nc.scalar.copy(a_hi[:, k, :], acc[:, k, :]).then_inc(hi_copied, 1)
                if k == KT - 3:
                    act.wait_ge(diag_used, 1)
                    for i in range(2):
                        nc.scalar.copy(row[i][:, :].rearrange("p (a b) -> p a b", a=2), ps[:, 2 * i:2 * i + 2, :])
            meet(act, 3)

            def merge_evac(j, t):
                act.wait_ge(merge_done, 8 * j + t + 1)
                nc.scalar.activation(sq[:, 0:WC], ps[:, t, 0:WC], ACT.Square, accum_out=stat[:, 64 + 4 * t + j:65 + 4 * t + j])
                A.link(nc.scalar.copy(x_tm[:, t, j * WC:(j + 1) * WC], ps[:, t, 0:WC]))
                act.sem_inc(merge_out, 1)

            for j in range(3):
                for t in range(NT):
                    merge_evac(j, t)
            merge_evac(3, 0)
            for t in range(NT + 4):
                if t < NT:
                    act.wait_ge(y_var, t + 1)
                    nc.scalar.activation(stat[:, 16 + t:17 + t], stat[:, 16 + t:17 + t], ACT.Sqrt).then_inc(y_root, 1)
                if t + 1 < NT:
                    merge_evac(3, t + 1)
                if 3 <= t < NT + 3:
                    u = t - 3
                    act.wait_ge(x1_var, u + 1)
                    nc.scalar.activation(stat[:, 32 + u:33 + u], stat[:, 32 + u:33 + u], ACT.Sqrt).then_inc(x1_root, 1)
                if 2 <= t < NT + 2:
                    u = t - 2
                    act.wait_ge(x1_made, u + 1)
                    act.dma_start(x1_d[u * P:(u + 1) * P, :], x_tm[:, u, :]).then_inc(x_landed[u], 16)
                    A.link(nc.scalar.activation(sq[:, :], x_tm[:, u, :], ACT.Square, accum_out=stat[:, 32 + u:33 + u]))
                    act.sem_inc(x1_square, 1)
                if t >= 4:
                    u = t - 4
                    act.wait_ge(x1_scale, u + 1)
                    act.wait_ge(x_landed[u], 32)
                    nc.scalar.activation(x_tm[:, u, :], x_tm[:, u, :], ACT.Copy, scale=stat[:, 40 + u:41 + u]).then_inc(normed, 1)
            norm_evac(1, 24)

            def hidden(n, c, extra=0, first=False):
                act.wait_ge(w_used[n % 2], n // 2 + 1 + extra)
                for j in range(4):
                    if not first:
                        act.wait_ge(u_split, c * 4 + (j - 3))
                    nc.scalar.activation(u_tmp[j][:, :], ps[:, j, :], ACT.Relu).then_inc(up_out, 1)
                    act.wait_ge(up_out, c * 4 + (j + 1))
                    nc.scalar.activation(u_tmp[j][:, :], u_tmp[j][:, :], ACT.Square).then_inc(u_squared, 1)

            hidden(N_MLP, 0, first=True)
            with act.Fori(0, NC // 2 - 1) as i:
                hidden(N_MLP + 1, i * 2 + 1, extra=i * 2)
                hidden(N_MLP + 3, i * 2 + 2, extra=i * 2)
            hidden(N_ALL - 3, NC - 1)
            for t in range(NT + 1):
                if t < NT:
                    act.wait_ge(down_out, 8 * (NC - 1) + t + 1)
                    A.link(nc.scalar.activation(sq[:, :], x_tm[:, t, :], ACT.Square, accum_out=stat[:, 48 + t:49 + t]))
                    act.sem_inc(z_square, 1)
                if t >= 1:
                    act.wait_ge(z_var, t)
                    nc.scalar.activation(stat[:, 47 + t:48 + t], stat[:, 47 + t:48 + t], ACT.Sqrt).then_inc(z_root, 1)

        @block.vector
        def _(dve):
            V = Count(dve, dve_own)
            ve = nc.vector

            def norm_split(j):
                for i in range(2 * KT):
                    g, k = divmod(i, KT)
                    dve.wait_ge(h_ready, 16 * j + i + 1)
                    r = slice(g * 512, g * 512 + 512)
                    if i % 2:
                        V.link(ve.tensor_copy(a_hi[:, k, r], h_tmp[i % 4][:, :]))
                    ve.tensor_tensor(a_lo[:, k, r], h_tmp[i % 4][:, :], a_hi[:, k, r].bitcast(F32),
                                     ALU.subtract).then_inc(h_split, 1)

            dve.wait_ge(squares, 1)
            ve.tensor_scalar(stat[:, 0:NT], stat[:, 0:NT], 1.0 / D, EPS, ALU.mult, ALU.add).then_inc(vars_ready, 1)
            dve.wait_ge(roots, 1)
            V.link(ve.reciprocal(stat[:, NT:2 * NT], stat[:, 0:NT]))
            for t in range(NT):
                ve.tensor_scalar(x_tm[:, t, :], x_tm[:, t, :], stat[:, NT + t:NT + t + 1], None, ALU.mult).then_inc(normed, 1)
            dve.wait_ge(c_ready, 2)
            V.link(ve.tensor_tensor(mod[:, 0:16], mod[:, 0:16], vec_a[:, 0:16], ALU.add))
            V.link(ve.tensor_scalar(gain[:, 0:KT], mod[:, 8:16], 1.0, None, ALU.add))
            ve.tensor_tensor(gain[:, 0:KT], gain[:, 0:KT], vec_a[:, 56:64], ALU.mult).then_inc(gain_ready, 1)
            norm_split(0)
            meet(dve, 0)

            for i in range(2):
                V.link(ve.memset(k_idx_half[1 - i][DI * i:DI * i + DI, :], 0.0))
            dve.wait_ge(rows_in, 16 * 5)
            dve.wait_ge(kv_sq, 1)
            ve.tensor_scalar(stat[:, 64:72], stat[:, 64:72], 1.0 / R, EPS, ALU.mult, ALU.add).then_inc(kv_var, 1)
            dve.wait_ge(kv_root, 1)
            V.link(ve.reciprocal(stat[:, 80:88], stat[:, 64:72]))
            for t in range(NT):
                ins = ve.scalar_tensor_tensor(ckv_tm[:, t, :], ps[:, t // 2, (t % 2) * R:(t % 2) * R + R],
                                              stat[:, 80 + t:81 + t], kv_row[:, :], ALU.mult, ALU.mult)
            ins.then_inc(kv_read, 1)
            dve.wait_ge(kv_sq, 2)
            V.link(ve.tensor_reduce(stat[:, 72:80], sq0[:, 0:NT * DI].rearrange("p (t c) -> p t c", t=NT), AX_X, ALU.add))
            ve.tensor_scalar(stat[:, 72:80], stat[:, 72:80], 1.0 / DI, EPS, ALU.mult, ALU.add).then_inc(kv_var, 1)
            dve.wait_ge(kv_root, 2)
            V.link(ve.reciprocal(stat[:, 88:96], stat[:, 72:80]))
            for t in range(NT):
                small = ps[:, 4 + t // 4, (t % 4) * NSM:(t % 4) * NSM + NSM]
                for half in range(2):
                    ve.scalar_tensor_tensor(kidx_tm[:, t, half * DI:half * DI + DI], small[:, 0:DI],
                                            stat[:, 88 + t:89 + t], ki_row[:, :], ALU.mult, ALU.mult)
                ve.tensor_scalar(w_idx[:, t, :], small[:, DI:DI + HI], HI ** -0.5, None, ALU.mult)
                ins = ve.tensor_copy(dt[:, t, :], small[:, DI + HI:NSM])
            ins.then_inc(kv_read, 1)
            i = 0
            for b in range(NT):
                for k0, n in key_chunks(b):
                    s = score[:, b, k0:k0 + n]
                    for h in range(HI):
                        dve.wait_ge(relu_done, i + 1)
                        r = relu_buf[:, i % 4, 0:n]
                        w = w_idx[:, b, h:h + 1]
                        if h:
                            dve.wait_ge(relu_used, i)
                            ins = ve.scalar_tensor_tensor(s, r, w, s, ALU.mult, ALU.add)
                        else:
                            ins = ve.tensor_scalar(s, r, w, None, ALU.mult)
                        ins.then_inc(relu_used, 1)
                        i += 1
            dve.wait_ge(relu_used, LOGITS)
            for r in range(2):
                dve.wait_ge(kv_out, 2)
                ve.tensor_tensor(ckv_lo[:, r, :].rearrange("p (a b) -> p a b", a=2), ps[:, 4 + 2 * r:6 + 2 * r, :],
                                 ckv_hi[:, r, :].bitcast(F32).rearrange("p (a b) -> p a b", a=2), ALU.subtract).then_inc(kv_out_split, 1)

            ROUNDS = TOPK // 8
            rows8 = [P, NT, NS]

            def every_chunk(row):
                return row[:, :].rearrange("p (o h) -> p o h", o=1).broadcast_to(rows8)

            V.link(ve.tensor_tensor(dt[:, :, :], dt[:, :, :], every_chunk(dtb_row), ALU.add))
            ve.scalar_tensor_tensor(acum[:, :, :], dt[:, :, :], -1.0, dt[:, :, :], ALU.mult, ALU.max).then_inc(dt_abs, 1)
            for b in range(2):
                if b:
                    V.link(ve.memset(bias_bf[:, b, 0:b * P], 0.0))
                V.link(ve.tensor_copy(bias_bf[:, b, b * P:(b + 1) * P], future[:, :]))
            done = 0
            for b0 in range(2, NT, 2):
                if b0 == 4:
                    dve.wait_ge(dt_exp, 2)
                    ve.tensor_scalar(dte[:, :, :], ea[:, :, :], 1.0, None, ALU.add).then_inc(dt_plus, 1)
                    dve.wait_ge(dt_plus, 1)
                    V.link(ve.tensor_scalar(dta[:, :, :], dte[:, :, :], 1.0, None, ALU.is_equal))
                if b0 == 6:
                    dve.wait_ge(dt_ln, 1)
                    V.link(ve.tensor_tensor(dec[:, :, :], dec[:, :, :], dta[:, :, :], ALU.add))
                    V.link(ve.scalar_tensor_tensor(dte[:, :, :], dte[:, :, :], -1.0, dta[:, :, :], ALU.add, ALU.add))
                    V.link(ve.reciprocal(dte[:, :, :], dte[:, :, :]))
                    V.link(ve.tensor_tensor(dec[:, :, :], dec[:, :, :], dte[:, :, :], ALU.mult))
                    V.link(ve.tensor_tensor(dec[:, :, :], dec[:, :, :], ea[:, :, :], ALU.mult))
                    V.link(ve.scalar_tensor_tensor(dt[:, :, :], dt[:, :, :], 0.0, dec[:, :, :], ALU.max, ALU.add))
                    V.link(ve.tensor_scalar(alog_row[:, :], alog_row[:, :], -1.0, None, ALU.mult))
                    ve.tensor_tensor(dta[:, :, :], dt[:, :, :], every_chunk(alog_row), ALU.mult).then_inc(dta_ready, 1)
                pair = [score[:, b, 0:(b + 1) * P] for b in (b0, b0 + 1)]
                for j, b in enumerate((b0, b0 + 1)):
                    d = score[:, b, b * P:(b + 1) * P]
                    ve.tensor_tensor(d, d, future[:, :], ALU.add).then_inc(topk_step, 1)
                done += 2
                with dve.Fori(0, ROUNDS) as i:
                    V.enter(i, 4)
                    for j in range(2):
                        dve.wait_ge(topk_step, i * 4 + (done - 1 + j))
                        V.step()
                        ve.max(top8[j][:, :], pair[j]).then_inc(topk_step, 1)
                    for j in range(2):
                        dve.wait_ge(topk_step, i * 4 + (done + 1 + j))
                        V.step()
                        ve.match_replace(pair[j], top8[j][:, :], pair[j], TAKEN).then_inc(topk_step, 1)
                    V.leave(ROUNDS)
                done += 4 * ROUNDS
                dve.wait_ge(topk_step, done)
                for j, b in enumerate((b0, b0 + 1)):
                    V.link(ve.tensor_scalar(bias_bf[:, b, 0:(b + 1) * P], pair[j], TAKEN, NEG, ALU.not_equal, ALU.mult))
            dve.wait_ge(mod_ready, 1)
            V.link(ve.tensor_tensor(mod[:, 16:48], mod[:, 16:48], vec_a[:, 16:48], ALU.add))
            V.link(ve.tensor_scalar(gain[:, KT:2 * KT], mod[:, 32:40], 1.0, None, ALU.add))
            V.link(ve.tensor_tensor(gain[:, KT:2 * KT], gain[:, KT:2 * KT], vec_a[:, 72:80], ALU.mult))
            V.link(ve.tensor_tensor(gate_cols[:, 0:KT], mod[:, 16:24], vec_a[:, 64:72], ALU.mult))
            V.link(ve.tensor_tensor(gate_cols[:, KT:2 * KT], mod[:, 40:48], vec_a[:, 80:88], ALU.mult))
            meet(dve, 1)

            dve.wait_ge(aend_out, 3)
            V.link(ve.tensor_tensor(dte[:, :, :].rearrange("p c h -> p (c h)"), ps[:, 7, 0:NT * NS],
                                    acum[:, :, :].rearrange("p c h -> p (c h)"), ALU.add))
            dve.sem_inc(dte_ready, 1)
            def attend(i, positions, last=False):
                for t in positions:
                    if t < STEPS or not last:
                        b = t % NT
                        n = (b + 1) * P
                        st = 4 * (t % 4)
                        dve.wait_ge(qk_done, i * STEPS + (t + 1))
                        s = ps[:, 2 * (t % 2):2 * (t % 2) + 2, :].rearrange("p a b -> p (a b)")[:, 0:n]
                        V.step()
                        V.link(ve.tensor_tensor_reduce(out=prob[t % 4][:, 0:n], in0=s, in1=bias_bf[:, b, 0:n], scale=1.0,
                                                       scalar=TAKEN, op0=ALU.add, op1=ALU.max,
                                                       accum_out=att_stat[:, st:st + 1]))
                        ve.tensor_scalar(att_stat[:, st + 1:st + 2], att_stat[:, st:st + 1], -SCALE, None, ALU.mult).then_inc(masked, 1)
                    if t >= 1:
                        n = ((t - 1) % NT + 1) * P
                        st = 4 * ((t - 1) % 4)
                        dve.wait_ge(exp_done, i * STEPS + t)
                        V.link(ve.reciprocal(att_stat[:, st + 3:st + 4], att_stat[:, st + 2:st + 3]))
                        ve.tensor_scalar(prob[(t - 1) % 4][:, 0:n], prob[(t - 1) % 4][:, 0:n], att_stat[:, st + 3:st + 4],
                                         None, ALU.mult).then_inc(p_ready, 1)

            attend(0, range(1))
            with dve.Fori(0, NH // 2 - 1) as i:
                V.enter(i, 3 * STEPS)
                attend(i, range(1, STEPS + 1))
                V.leave(NH // 2 - 1)
            attend(NH // 2 - 1, range(1, STEPS + 1), last=True)
            meet(dve, 2)

            for m in range(2):
                V.link(ve.memset(c_in[m][:, 0:TAPS - 1], 0.0))
            with dve.Fori(0, NG) as g:
                V.enter(g, 6 * (TAPS - 1) + 4 * NT - 2)
                ve.tensor_copy(dta_g[:, :, :], dta[:, :, bass.ds(g * HG, HG)]).then_inc(dtag_ready, 1)
                for T in range(6):
                    dve.wait_ge(conv_in, g * 6 + (T + 1))
                    if T >= 2:
                        dve.wait_ge(silu_done, g * 6 + (T - 1)) if T < 4 else dve.wait_ge(tile_turned, g * 5 + (T - 2))
                    o = c_out[T % 2][:, :]
                    for j in range(TAPS):
                        col = (g + (24 * j + 16), g + (24 * j + 20))[T] if T < 2 else g * 4 + (24 * j + T - 2)
                        wj = vec_b[:, bass.ds(col, 1)]
                        src = c_in[T % 2][:, j:j + SEQ]
                        if j == 0:
                            V.link(ve.tensor_scalar(o, src, wj, None, ALU.mult))
                        elif j < TAPS - 1:
                            V.link(ve.scalar_tensor_tensor(o, src, wj, o, ALU.mult, ALU.add))
                        else:
                            ve.scalar_tensor_tensor(o, src, wj, o, ALU.mult, ALU.add).then_inc(conv_done, 1)

                def heads(t, k):
                    return t[:, k, bass.ds(g * HG, HG)]

                dve.wait_ge(tile_out, g * 5 + 5)

                def xs3(k):
                    return xs_tm[:, k, :].rearrange("p (h d) -> p h d", h=HG)

                def mix_in(k):
                    dve.wait_ge(decay_done, g * NT + (k + 1))
                    ve.tensor_tensor(decay[k % 2][:, :, :], decay[k % 2][:, :, :],
                                     cb_sb[:, :].rearrange("p (o l) -> p o l", o=1).broadcast_to([P, HG, P]), ALU.mult).then_inc(mix_ready, 1)

                def bank(b):
                    return ps[:, b, :].rearrange("p (h d) -> p h d", h=HG)

                mix_in(0)
                for k in range(NT):
                    if k + 1 < NT:
                        mix_in(k + 1)
                    dve.wait_ge(mix_done, g * NT + (k + 1))
                    if k == 0:
                        ve.tensor_copy(state[:, :, :], bank(6)).then_inc(state_ready, 1)
                    elif k < NT - 1:
                        V.link(ve.tensor_tensor(state[:, :, :], state[:, :, :], spread(heads(dec, k), PD), ALU.mult))
                        ve.tensor_tensor(state[:, :, :], state[:, :, :], bank(6), ALU.add).then_inc(state_ready, 1)
                    y = y_t[k % 2][:, :, :]
                    if k == 0:
                        V.link(ve.tensor_copy(y, bank(2)))
                    else:
                        V.link(ve.tensor_tensor(y, bank(3 + 2 * (k % 2)), spread(heads(ea, k), PD), ALU.mult))
                        V.link(ve.tensor_tensor(y, y, bank(2 + 2 * (k % 2)), ALU.add))
                    dve.wait_ge(xs_skip, g * NT + (k + 1))
                    V.link(ve.tensor_tensor(y, y, xs3(k), ALU.add))
                    z = zy[:, k, :].rearrange("p (h d) -> p h d", h=HG)
                    ve.tensor_tensor(z, z, y, ALU.mult).then_inc(y_ready, 1)
                dve.wait_ge(gn_squares, g * NT + NT)
                ve.tensor_scalar(stat[:, 96:104], stat[:, 96:104], 1.0 / DG, EPS, ALU.mult, ALU.add).then_inc(gn_var, 1)
                dve.wait_ge(gn_root, g + 1)
                V.link(ve.reciprocal(stat[:, 104:112], stat[:, 96:104]))
                for k in range(NT):
                    ve.tensor_scalar(zy[:, k, :], zy[:, k, :], stat[:, 104 + k:105 + k], None, ALU.mult).then_inc(gn_ready, 1)
                V.leave(NG)

            def act_lo(first, src=None, tiles=range(KT)):
                for k in tiles:
                    dve.wait_ge(hi_copied, first + (k + 1))
                    raw_k = act_raw[k % 4][:, :] if src is None else src[:, k, :]
                    ve.tensor_tensor(a_lo[:, k, :], raw_k, a_hi[:, k, :].bitcast(F32), ALU.subtract).then_inc(act_split, 1)

            def gate_block(n, j, turn):
                dve.wait_ge(w_used[n % 2], turn * 2 + (n // 2 + 1))
                dve.wait_ge(gates_in[j % 2], turn * 32 + 16 * (j // 2 + 1))
                for b in range(4):
                    m, q = divmod(b, 2)
                    r = slice(q * 512, q * 512 + 512)
                    ve.tensor_tensor(gated[b % 2][:, :], ps[:, 4 * (j % 2) + b, :], gates[j % 2][:, m, r], ALU.mult).then_inc(gate_used, 1)
                    dve.wait_ge(gate_used, turn * 16 + (4 * j + b + 1))
                    V.link(ve.tensor_tensor(acc[:, 2 * j + m, r], acc[:, 2 * j + m, r], gated[b % 2][:, :], ALU.add))

            act_lo(0)
            V.link(ve.memset(acc[:, :, :], 0.0))
            with dve.Fori(0, 2) as i:
                V.enter(i, 16)
                for j in range(3):
                    gate_block(N_O + j, j, i)
                act_lo(i * 8 + 8)
                gate_block(N_O + 3, 3, i)
                V.leave(2)
            for j in range(3):
                gate_block(N_O + j, j, 2)
            dve.sem_inc(acc_final, 1)
            for i in range(2 * KT):
                ins = ve.tensor_scalar(diag[:, i, :], ident[:, :], gate_cols[:, i:i + 1], None, ALU.mult)
            ins.then_inc(diag_made, 1)
            act_lo(3 * KT, acc, range(KT - 2))
            gate_block(N_O + 3, 3, 2)
            dve.sem_inc(acc_final, 1)
            act_lo(3 * KT, acc, range(KT - 2, KT))
            meet(dve, 3)
            for t in range(NT + 3):
                if t < NT:
                    dve.wait_ge(merge_out, 24 + t + 1)
                    V.link(ve.tensor_reduce(stat[:, 16 + t:17 + t], stat[:, 64 + 4 * t:68 + 4 * t], AX_X, ALU.add))
                    ve.tensor_scalar(stat[:, 16 + t:17 + t], stat[:, 16 + t:17 + t], 1.0 / D, EPS, ALU.mult, ALU.add).then_inc(y_var, 1)
                if t >= 3:
                    u = t - 3
                    dve.wait_ge(x1_square, u + 1)
                    ve.tensor_scalar(stat[:, 32 + u:33 + u], stat[:, 32 + u:33 + u], 1.0 / D, EPS, ALU.mult, ALU.add).then_inc(x1_var, 1)
                if 1 <= t <= NT:
                    u = t - 1
                    dve.wait_ge(y_root, u + 1)
                    V.link(ve.reciprocal(stat[:, 24 + u:25 + u], stat[:, 16 + u:17 + u]))
                    V.link(ve.scalar_tensor_tensor(x_tm[:, u, :], x_tm[:, u, :], stat[:, 24 + u:25 + u], row[0][:, :], ALU.mult, ALU.mult))
                    dve.wait_ge(res_in[u % 4], 16 * (u // 4 + 1))
                    ve.tensor_tensor(x_tm[:, u, :], x_tm[:, u, :], x_in[u % 4][:, :], ALU.add).then_inc(x1_made, 1)
                if t >= 3:
                    u = t - 3
                    dve.wait_ge(x1_root, u + 1)
                    ve.reciprocal(stat[:, 40 + u:41 + u], stat[:, 32 + u:33 + u]).then_inc(x1_scale, 1)
            norm_split(1)

            def u_part(c, b, j):
                m, q = divmod(j, 2)
                r = slice(q * 512, q * 512 + 512)
                dve.wait_ge(u_squared, c * 4 + (j + 1))
                V.link(ve.tensor_copy(u_hi[b][:, m, r], u_tmp[j][:, :]))
                ve.tensor_tensor(u_lo[b][:, m, r], u_tmp[j][:, :], u_hi[b][:, m, r].bitcast(F32), ALU.subtract).then_inc(u_split, 1)

            def add_down(c, t, first=False):
                dve.wait_ge(down_done, c * 8 + (t + 1))
                if not first:
                    dve.wait_ge(down_out, c * 8 + (t - 7))
                o = x_tm[:, t, :].rearrange("p (a b) -> p a b", a=2)
                part = ps[:, 4 + 2 * (t % 2):6 + 2 * (t % 2), :]
                ins = ve.tensor_copy(o, part) if first else ve.tensor_tensor(o, o, part, ALU.add)
                ins.then_inc(down_out, 1)

            def chunk(c, b, last=False, first=False, down_before=None):
                if down_before is not None:
                    dve.wait_ge(*down_before)
                for t in range(NT):
                    if t < 4 and not last:
                        u_part(c + 1, 1 - b, t)
                    add_down(c, t, first)

            for j in range(4):
                u_part(0, 0, j)
            chunk(0, 0, first=True)
            chunk(1, 1, down_before=(w_used[0], (N_MLP + 2) // 2 + 1))
            with dve.Fori(1, NC // 2 - 1) as i:
                V.enter(i - 1, 8)
                chunk(i * 2, 0, down_before=(w_used[0], i * 2 + (N_MLP // 2 + 1)))
                chunk(i * 2 + 1, 1, down_before=(w_used[0], i * 2 + (N_MLP // 2 + 2)))
                V.leave(NC // 2 - 2)
            chunk(NC - 2, 0, down_before=(w_used[0], (N_ALL - 4) // 2 + 1))
            for t in range(NT + 2):
                if t < NT:
                    add_down(NC - 1, t)
                if 1 <= t <= NT:
                    u = t - 1
                    dve.wait_ge(z_square, u + 1)
                    ve.tensor_scalar(stat[:, 48 + u:49 + u], stat[:, 48 + u:49 + u], 1.0 / D, EPS, ALU.mult, ALU.add).then_inc(z_var, 1)
                if t >= 2:
                    u = t - 2
                    dve.wait_ge(z_root, u + 1)
                    V.link(ve.reciprocal(stat[:, 56 + u:57 + u], stat[:, 48 + u:49 + u]))
                    V.link(ve.scalar_tensor_tensor(x_tm[:, u, :], x_tm[:, u, :], stat[:, 56 + u:57 + u], row[1][:, :], ALU.mult, ALU.mult))
                    dve.wait_ge(res_in[u % 4], 16 * (u // 4 + 3))
                    ve.tensor_tensor(x_tm[:, u, :], x_tm[:, u, :], x_in[u % 4][:, :], ALU.add).then_inc(out_made, 1)


_INS = ['x', 'c', 'ada_w', 'ada_b', 'norm_g', 'w_in', 'kv_norm_g', 'kidx_norm_g', 'w_uk', 'w_uv', 'conv_w', 'conv_b',
        'dt_bias', 'a_log', 'd_skip', 'ssm_norm_g', 'w_o_att', 'w_o_ssd', 'w_out', 'w_up', 'w_down']
_OUTS = [((1, 1024, 1024), 'float32')]


def kernel(**inputs):
    import numpy as _np
    import concourse.bacc as _bacc
    from concourse import mybir as _mybir
    from concourse.bass_utils import run_bass_kernel_spmd as _run

    nc = _bacc.Bacc("TRN2", target_bir_lowering=False, num_devices=1)
    arrays, args = {}, []
    for name in _INS:
        a = _np.ascontiguousarray(inputs[name])
        arrays[f"in_{name}_dram"] = a
        args.append(nc.dram_tensor(f"in_{name}_dram", a.shape, _mybir.dt.from_np(a.dtype), kind="ExternalInput").ap())
    for i, (shape, dtype) in enumerate(_OUTS):
        dt = _mybir.dt.from_np(_np.dtype(dtype))
        args.append(nc.dram_tensor(f"out_{i}_dram", shape, dt, kind="ExternalOutput").ap())
    hybrid_block(nc, *args)
    r = _run(nc, [arrays], core_ids=[0])
    return r.results[0]["out_0_dram"]
```
